# Optimizing a Trainium2 kernel written in Bass

```python
import math
import numpy as np
import jax, jax.numpy as jnp
from jax import lax

D_MODEL = 1024
BATCH = 1
SEQ = 2048
DEPTH = 1
DEC_BATCH = 8
DEC_SEQ = 16
PAST_LEN = 1024

CHUNK = 64
Q_BLOCK = 128
FOX_DIM = 64
FOX_HEADS = (D_MODEL // 2) // FOX_DIM
FOX_WIDTH = FOX_HEADS * FOX_DIM
GDN_DK = 128
GDN_DV = 128
GDN_HEADS = (D_MODEL // 2) // GDN_DV
GDN_QK = GDN_HEADS * GDN_DK
GDN_WIDTH = GDN_HEADS * GDN_DV
GDN_CONV_CH = 2 * GDN_QK + GDN_WIDTH
GDN_CONV = 4
MIX_WIDTH = FOX_WIDTH + GDN_WIDTH
D_FF = ((8 * D_MODEL // 3 + 127) // 128) * 128
FFN_CONV = 3
N_IN = 3 * FOX_WIDTH + FOX_HEADS + GDN_CONV_CH + 2 * GDN_HEADS + GDN_WIDTH
EPS = 1e-6

kernel_name = 'hybrid_fox_gdn_convffn_stream_step'

def rmsnorm(x, w):
    xf = x.astype(jnp.float32)
    y = xf * lax.rsqrt(jnp.mean(xf * xf, axis=-1, keepdims=True) + EPS)
    return (y * w.astype(jnp.float32)).astype(x.dtype)

def l2norm(x):
    xf = x.astype(jnp.float32)
    return xf * lax.rsqrt(jnp.sum(xf * xf, axis=-1, keepdims=True) + EPS)

def causal_dwconv(x_hist, w):
    width = w.shape[0]
    T = x_hist.shape[1] - (width - 1)
    acc = x_hist[:, 0:T] * w[0]
    for i in range(1, width):
        acc = acc + x_hist[:, i:i + T] * w[i]
    return acc

def fox_block(qi, cq, qpos, k, v, ck):
    scale = FOX_DIM ** -0.5
    logits = jnp.einsum('bqhd,bkhd->bhqk', qi, k, preferred_element_type=jnp.float32) * scale
    logits = logits + cq[..., :, None] - ck[..., None, :]
    mask = jnp.arange(k.shape[1])[None, :] <= qpos[:, None]
    logits = jnp.where(mask, logits, -jnp.inf)
    p = jax.nn.softmax(logits, axis=-1).astype(v.dtype)
    return jnp.einsum('bhqk,bkhd->bqhd', p, v)

def fox_prompt(q, k, v, logf):
    B, S, H, D = q.shape
    nb = S // Q_BLOCK
    c = jnp.cumsum(logf, axis=1).transpose(0, 2, 1)
    qb = q.reshape(B, nb, Q_BLOCK, H, D).transpose(1, 0, 2, 3, 4)
    cqb = c.reshape(B, H, nb, Q_BLOCK).transpose(2, 0, 1, 3)
    posb = jnp.arange(S).reshape(nb, Q_BLOCK)
    o = lax.map(lambda a: fox_block(a[0], a[1], a[2], k, v, c), (qb, cqb, posb))
    return o.transpose(1, 0, 2, 3, 4).reshape(B, S, H * D)

def gdn_chunked(q, k, v, g, beta, s0, chunk):
    B, T, H, DK = q.shape
    DV = v.shape[-1]
    n = T // chunk

    def blocks(a):
        return a.reshape(B, n, chunk, H, a.shape[-1]).transpose(1, 0, 3, 2, 4)

    qc, kc, vc = blocks(q), blocks(k), blocks(v)
    gc = g.reshape(B, n, chunk, H).transpose(1, 0, 3, 2)
    bc = beta.reshape(B, n, chunk, H).transpose(1, 0, 3, 2)
    G = jnp.cumsum(gc, axis=-1)
    incl = jnp.tril(jnp.ones((chunk, chunk), dtype=bool))
    strict = jnp.tril(jnp.ones((chunk, chunk), dtype=bool), -1)
    decay = jnp.exp(jnp.where(incl, G[..., :, None] - G[..., None, :], -jnp.inf))
    kb = kc * bc[..., None]
    L = jnp.where(strict, jnp.einsum('nbhid,nbhjd->nbhij', kb, kc) * decay, 0.0)
    eye = jnp.eye(chunk, dtype=jnp.float32)
    rhs = jnp.concatenate([vc * bc[..., None], kb * jnp.exp(G)[..., None]], axis=-1)
    sol = lax.linalg.triangular_solve(eye + L, rhs, left_side=True, lower=True)
    u, w = sol[..., :DV], sol[..., DV:]
    a_qk = jnp.einsum('nbhid,nbhjd->nbhij', qc, kc) * decay

    def step(S, xs):
        qi, ki, Gi, ui, wi, ai = xs
        delta = ui - jnp.einsum('bhck,bhkv->bhcv', wi, S)
        o = (jnp.einsum('bhck,bhkv->bhcv', qi * jnp.exp(Gi)[..., None], S)
             + jnp.einsum('bhij,bhjv->bhiv', ai, delta))
        g_last = Gi[..., -1:]
        S = (S * jnp.exp(g_last)[..., None]
             + jnp.einsum('bhck,bhcv->bhkv', ki * jnp.exp(g_last - Gi)[..., None], delta))
        return S, o

    s_final, o = lax.scan(step, s0, (qc, kc, G, u, w, a_qk))
    o = o.transpose(1, 0, 3, 2, 4).reshape(B, T, H, DV)
    return o, s_final

def hybrid_layer(x, fox_past, gdn_conv_hist, gdn_state, ffn_conv_hist,
                 w_in, b_fox_f, gdn_conv_w, gdn_a_log, gdn_dt_bias, gdn_norm_w, w_o,
                 norm_mix_w, norm_ffn_w, w_up, ffn_conv_w, ffn_conv_b, w_down):
    f32 = jnp.float32
    B, T, _ = x.shape
    xn = rmsnorm(x, norm_mix_w)
    proj = jnp.einsum('btd,de->bte', xn, w_in)
    sizes = (FOX_WIDTH, FOX_WIDTH, FOX_WIDTH, FOX_HEADS, GDN_CONV_CH, GDN_HEADS, GDN_HEADS, GDN_WIDTH)
    idx = np.cumsum(sizes)[:-1].tolist()
    fq, fk, fv, ff, gqkv, ga, gb, gz = jnp.split(proj, idx, axis=-1)

    q = fq.reshape(B, T, FOX_HEADS, FOX_DIM)
    k = fk.reshape(B, T, FOX_HEADS, FOX_DIM)
    v = fv.reshape(B, T, FOX_HEADS, FOX_DIM)
    logf = jax.nn.log_sigmoid(ff.astype(f32) + b_fox_f.astype(f32))
    if fox_past is None:
        o_fox = fox_prompt(q, k, v, logf)
    else:
        k_past, v_past, logf_past = fox_past
        P = k_past.shape[1]
        k_all = jnp.concatenate([k_past.astype(k.dtype), k], axis=1)
        v_all = jnp.concatenate([v_past.astype(v.dtype), v], axis=1)
        c = jnp.cumsum(jnp.concatenate([logf_past.astype(f32), logf], axis=1), axis=1).transpose(0, 2, 1)
        o_fox = fox_block(q, c[:, :, P:], P + jnp.arange(T), k_all, v_all, c).reshape(B, T, FOX_WIDTH)

    hist = jnp.concatenate([gdn_conv_hist.astype(gqkv.dtype), gqkv], axis=1)
    new_gdn_conv = hist[:, T:]
    qkv = jax.nn.silu(causal_dwconv(hist, gdn_conv_w))
    gq, gk, gv = jnp.split(qkv, [GDN_QK, 2 * GDN_QK], axis=-1)
    qd = l2norm(gq.reshape(B, T, GDN_HEADS, GDN_DK)) * (GDN_DK ** -0.5)
    kd = l2norm(gk.reshape(B, T, GDN_HEADS, GDN_DK))
    vd = gv.reshape(B, T, GDN_HEADS, GDN_DV).astype(f32)
    g = -jnp.exp(gdn_a_log.astype(f32)) * jax.nn.softplus(ga.astype(f32) + gdn_dt_bias.astype(f32))
    beta = jax.nn.sigmoid(gb.astype(f32))
    o_gdn, new_gdn_state = gdn_chunked(qd, kd, vd, g, beta, gdn_state.astype(f32), min(CHUNK, T))
    z = jax.nn.silu(gz.astype(f32)).reshape(B, T, GDN_HEADS, GDN_DV)
    o_gdn = (rmsnorm(o_gdn, gdn_norm_w) * z).reshape(B, T, GDN_WIDTH)

    mix = jnp.concatenate([o_fox.astype(x.dtype), o_gdn.astype(x.dtype)], axis=-1)
    h = x + jnp.einsum('bte,ed->btd', mix, w_o)

    hn = rmsnorm(h, norm_ffn_w)
    up = jnp.einsum('btd,df->btf', hn, w_up)
    uhist = jnp.concatenate([ffn_conv_hist.astype(up.dtype), up], axis=1)
    new_ffn_conv = uhist[:, T:]
    uc = causal_dwconv(uhist, ffn_conv_w) + ffn_conv_b
    gate, val = jnp.split(uc, 2, axis=-1)
    h = h + jnp.einsum('btf,fd->btd', jax.nn.silu(gate) * val, w_down)
    return h, (k, v, logf, new_gdn_state, new_gdn_conv, new_ffn_conv)

def setup_inputs(seed: int = 0) -> dict:
    key = jax.random.key(seed)
    ks = jax.random.split(key, 24)
    f32 = jnp.float32

    def nrm(k, shape, s):
        return s * jax.random.normal(k, shape, f32)

    x_prompt = nrm(ks[0], (BATCH, SEQ, D_MODEL), 1.0)
    x_sample = nrm(ks[1], (DEC_BATCH, DEC_SEQ, D_MODEL), 1.0)
    cache_fox_k = nrm(ks[2], (DEPTH, DEC_BATCH, PAST_LEN, FOX_HEADS, FOX_DIM), 1.0)
    cache_fox_v = nrm(ks[3], (DEPTH, DEC_BATCH, PAST_LEN, FOX_HEADS, FOX_DIM), 1.0)
    cache_fox_logf = jax.nn.log_sigmoid(3.0 + nrm(ks[4], (DEPTH, DEC_BATCH, PAST_LEN, FOX_HEADS), 0.5))
    state_gdn = nrm(ks[5], (DEPTH, DEC_BATCH, GDN_HEADS, GDN_DK, GDN_DV), 0.3)
    state_gdn_conv = nrm(ks[6], (DEPTH, DEC_BATCH, GDN_CONV - 1, GDN_CONV_CH), 1.0)
    state_ffn_conv = nrm(ks[7], (DEPTH, DEC_BATCH, FFN_CONV - 1, 2 * D_FF), 1.0)
    w_in = nrm(ks[8], (DEPTH, D_MODEL, N_IN), D_MODEL ** -0.5)
    b_fox_f = 3.0 + nrm(ks[9], (DEPTH, FOX_HEADS), 0.5)
    gdn_conv_w = nrm(ks[10], (DEPTH, GDN_CONV, GDN_CONV_CH), GDN_CONV ** -0.5)
    gdn_a_log = jnp.log(jax.random.uniform(ks[11], (DEPTH, GDN_HEADS), f32, 1.0, 16.0))
    dt = jnp.exp(jax.random.uniform(ks[12], (DEPTH, GDN_HEADS), f32, math.log(1e-3), math.log(1e-1)))
    gdn_dt_bias = dt + jnp.log(-jnp.expm1(-dt))
    gdn_norm_w = 1.0 + nrm(ks[13], (DEPTH, GDN_DV), 0.02)
    w_o = nrm(ks[14], (DEPTH, MIX_WIDTH, D_MODEL), MIX_WIDTH ** -0.5)
    norm_mix_w = 1.0 + nrm(ks[15], (DEPTH, D_MODEL), 0.02)
    norm_ffn_w = 1.0 + nrm(ks[16], (DEPTH, D_MODEL), 0.02)
    w_up = nrm(ks[17], (DEPTH, D_MODEL, 2 * D_FF), D_MODEL ** -0.5)
    ffn_conv_w = nrm(ks[18], (DEPTH, FFN_CONV, 2 * D_FF), FFN_CONV ** -0.5)
    ffn_conv_b = nrm(ks[19], (DEPTH, 2 * D_FF), 0.01)
    w_down = nrm(ks[20], (DEPTH, D_FF, D_MODEL), D_FF ** -0.5)
    norm_final_w = 1.0 + nrm(ks[21], (D_MODEL,), 0.02)
    return {'x_prompt': x_prompt, 'x_sample': x_sample,
            'cache_fox_k': cache_fox_k, 'cache_fox_v': cache_fox_v, 'cache_fox_logf': cache_fox_logf,
            'state_gdn': state_gdn, 'state_gdn_conv': state_gdn_conv, 'state_ffn_conv': state_ffn_conv,
            'w_in': w_in, 'b_fox_f': b_fox_f, 'gdn_conv_w': gdn_conv_w, 'gdn_a_log': gdn_a_log,
            'gdn_dt_bias': gdn_dt_bias, 'gdn_norm_w': gdn_norm_w, 'w_o': w_o,
            'norm_mix_w': norm_mix_w, 'norm_ffn_w': norm_ffn_w, 'w_up': w_up,
            'ffn_conv_w': ffn_conv_w, 'ffn_conv_b': ffn_conv_b, 'w_down': w_down,
            'norm_final_w': norm_final_w}

def reference(x_prompt, x_sample, cache_fox_k, cache_fox_v, cache_fox_logf, state_gdn,
              state_gdn_conv, state_ffn_conv, w_in, b_fox_f, gdn_conv_w, gdn_a_log, gdn_dt_bias,
              gdn_norm_w, w_o, norm_mix_w, norm_ffn_w, w_up, ffn_conv_w, ffn_conv_b, w_down,
              norm_final_w):
    hp, hs = x_prompt, x_sample
    Bp = x_prompt.shape[0]
    sp_list, ss_list = [], []
    for l in range(DEPTH):
        lw = (w_in[l], b_fox_f[l], gdn_conv_w[l], gdn_a_log[l], gdn_dt_bias[l], gdn_norm_w[l], w_o[l],
              norm_mix_w[l], norm_ffn_w[l], w_up[l], ffn_conv_w[l], ffn_conv_b[l], w_down[l])
        hp, sp = hybrid_layer(
            hp, None,
            jnp.zeros((Bp, GDN_CONV - 1, GDN_CONV_CH), hp.dtype),
            jnp.zeros((Bp, GDN_HEADS, GDN_DK, GDN_DV), jnp.float32),
            jnp.zeros((Bp, FFN_CONV - 1, 2 * D_FF), hp.dtype), *lw)
        hs, ss = hybrid_layer(
            hs, (cache_fox_k[l], cache_fox_v[l], cache_fox_logf[l]),
            state_gdn_conv[l], state_gdn[l], state_ffn_conv[l], *lw)
        sp_list.append(sp)
        ss_list.append(ss)
    pk, pv, pf, ps, pc, pfc = [jnp.stack(a) for a in zip(*sp_list)]
    sk, sv, sf, sst, sc, sfc = [jnp.stack(a) for a in zip(*ss_list)]
    y_prompt = rmsnorm(hp, norm_final_w)
    y_sample = rmsnorm(hs, norm_final_w)
    return (y_prompt, y_sample, pk, pv, pf, ps, pc, pfc, sk, sv, sf, sst, sc, sfc)


_drawn_inputs = setup_inputs


def setup_inputs(seed=0):
    import zlib

    import numpy as np

    out = dict(_drawn_inputs(seed))
    spreads = {}
    factors = {'cache_fox_logf': 5.432,
     'gdn_norm_w': 6.299,
     'norm_ffn_w': 2.839,
     'ffn_conv_b': 8.0,
     'norm_final_w': 2.747}
    for name, (base, spread) in spreads.items():
        noise = np.random.default_rng([zlib.crc32(name.encode()), seed]).standard_normal(out[name].shape)
        drawn = base * np.exp(spread * noise) if base else spread * noise
        out[name] = __import__('jax').numpy.asarray(drawn.astype(out[name].dtype))
    for name, factor in factors.items():
        out[name] = (out[name] * factor).astype(out[name].dtype)
    return out
```

```python
from contextlib import ExitStack

import concourse.bass as bass
from concourse import mybir

P = 128
NEG = -1e30
EPS = 1e-6
F32 = mybir.dt.float32
ALU = mybir.AluOpType
ACT = mybir.ActivationFunctionType
AX = mybir.AxisListType
BANK = 512


class Phase:

    def __init__(self, nc, name):
        self.nc, self.name, self.sems, self.stack = nc, name, [], ExitStack()

    def sb(self, name, shape, dt=F32):
        return self.stack.enter_context(self.nc.sbuf_tensor(f"{self.name}_{name}", shape, dt))

    def sem(self, name):
        s = self.nc.alloc_semaphore(f"{self.name}_{name}")
        self.sems.append(s)
        return s

    def close(self):
        self.stack.close()
        self.nc.clear_and_free_semaphores(self.sems)
        self.nc.all_engine_barrier()


class Step:

    def __init__(self, eng, sem):
        self.eng, self.sem, self.n = eng, sem, 0

    def __call__(self, ins):
        self.n += 1
        ins.then_inc(self.sem, 1)
        self.eng.wait_ge(self.sem, self.n)


def spread(ap, shape):
    return ap.to_broadcast(list(shape))


def build_constants(nc, c):
    ph = Phase(nc, "const")
    pool_done, sums_done, step_sem = ph.sem("pool_done"), ph.sem("sums_done"), ph.sem("pool_step")
    DB, DS = c["DB"], c["DS"]
    later = ph.sb("later", [P, DB, DS])
    upto = ph.sb("upto", [P, DB, DS])
    with nc.Block() as block:

        @block.gpsimd
        def _(pool):
            step = Step(pool, step_sem)

            def keep(t, pattern, base, mult, fill=0.0, op=ALU.is_ge):
                step(nc.gpsimd.affine_select(out=t, in_=t, pattern=pattern, base=base, channel_multiplier=mult,
                                             compare_op=op, fill=fill))

            step(nc.gpsimd.memset(c["ones"][:], 1.0))
            step(nc.gpsimd.memset(c["eps"][:], EPS))
            step(nc.gpsimd.memset(c["ident"][:], 0.0))
            keep(c["ident"][:], [[-1, P]], 0, 1, 1.0, ALU.not_equal)
            step(nc.gpsimd.memset(c["tri"][:], 1.0))
            keep(c["tri"][:], [[1, P]], 0, -1)
            same = c["same_stream"][:].rearrange("p (b r) -> p b r", r=DS)
            step(nc.gpsimd.memset(c["same_stream"][:], 1.0))
            keep(same, [[-DS, DB], [0, DS]], 0, 1)
            keep(same, [[DS, DB], [0, DS]], DS - 1, -1)
            step(nc.gpsimd.tensor_copy(c["tri_s"][:], c["same_stream"][:]))
            keep(c["tri_s"][:], [[1, P]], 0, -1)
            step(nc.gpsimd.memset(c["stream_rows"][:], 1.0))
            keep(c["stream_rows"][:], [[-DS, DB]], 0, 1)
            keep(c["stream_rows"][:], [[DS, DB]], DS - 1, -1)
            step(nc.gpsimd.memset(c["causal"][:], 0.0))
            keep(c["causal"][:], [[-1, P]], 0, 1, NEG)
            step(nc.gpsimd.memset(c["after"][:], 1.0))
            keep(c["after"][:], [[-1, P]], -1, 1)
            step(nc.gpsimd.memset(c["before_q"][:], 1.0))
            keep(c["before_q"][:], [[-DS, DB], [0, DS]], 0, 1)
            keep(c["before_q"][:], [[DS, DB], [1, DS]], 0, -1)
            for n, m in enumerate(c["level"]):
                s = 1 << n
                v = m[:].rearrange("p (a h r) -> p a h r", h=2, r=s)
                step(nc.gpsimd.memset(m[:], 0.0))
                step(nc.gpsimd.memset(v[:, :, 0, :], -1.0))
                keep(v[:, :, 0, :], [[-2 * s, P // (2 * s)], [0, s]], -s, 1)
                keep(v[:, :, 0, :], [[2 * s, P // (2 * s)], [0, s]], 2 * s - 1, -1)
            v = c["level0_t"][:].rearrange("p (a h) -> p a h", h=2)
            step(nc.gpsimd.memset(c["level0_t"][:], 0.0))
            step(nc.gpsimd.memset(v[:, :, 1:2], -1.0))
            keep(v[:, :, 1:2], [[-2, P // 2], [0, 1]], 0, 1)
            keep(v[:, :, 1:2], [[2, P // 2], [0, 1]], 0, -1)
            step(nc.gpsimd.memset(later[:], 1.0))
            keep(later[:], [[-DS, DB], [-1, DS]], -1, 1)
            keep(later[:], [[DS, DB], [0, DS]], DS - 1, -1)
            step(nc.gpsimd.memset(upto[:], 1.0))
            keep(upto[:], [[-DS, DB], [-1, DS]], 0, 1)
            keep(upto[:], [[DS, DB], [0, DS]], DS - 1, -1)
            pool.sem_inc(pool_done, 1)

        @block.vector
        def _(dve):
            step = Step(dve, sums_done)
            dve.wait_ge(pool_done, 1)
            step(nc.vector.tensor_reduce(c["later_in_stream"][:], later[:].rearrange("p b k -> p k b"), AX.X, ALU.add))
            step(nc.vector.tensor_reduce(c["causal_s"][:], upto[:].rearrange("p b k -> p k b"), AX.X, ALU.add))
            for m in (c["causal_s"][:],):
                step(nc.vector.tensor_scalar(m, m, -1.0, -NEG, ALU.add, ALU.mult))
            step(nc.vector.tensor_scalar(c["decay_mask"][:], c["tri"][:], -1.0, -NEG, ALU.add, ALU.mult))
            step(nc.vector.tensor_scalar(c["decay_mask_s"][:], c["tri_s"][:], -1.0, -NEG, ALU.add, ALU.mult))
    ph.close()


def project(nc, c, io, bank):
    ph = Phase(nc, "proj")
    D, FW, FH, GC, GH, GW, CW = (c[k] for k in ("D", "FW", "FH", "GC", "GH", "GW", "CW"))
    DB, DS, SEQ = c["DB"], c["DS"], c["SEQ"]
    KD, NCH, H3 = D // P, GC // P, CW - 1
    GT = 4
    W = GT * P
    NG = SEQ // W
    off_f = 3 * FW
    off_g = off_f + FH
    off_a = off_g + GC
    off_z = off_a + 2 * GH
    NS = FH + 2 * GH
    N_IN = off_z + GW
    HB = KD // 2

    w = ph.sb("w", [P, KD, N_IN])
    x = ph.sb("x", [P, 2, D])
    squares = ph.sb("squares", [P, D])
    xn = ph.sb("xn", [P, 2, D])
    xnT = ph.sb("xnT", [P, KD, W])
    vec_rows = ph.sb("vec_rows", [KD + CW * NCH, P])
    vecs = ph.sb("vecs", [P, KD + CW * NCH])
    rows = ph.sb("rows", [P, 4, BANK])
    ss, ln_ms, rs = (ph.sb(n, [P, 2]) for n in ("ss", "ln_ms", "rs"))
    raw = ph.sb("raw", [P, 2, H3 + W])
    acc = ph.sb("acc", [P, 2, W])
    hist = ph.sb("hist", [P, NCH, H3])
    hist_s = ph.sb("hist_s", [P, NCH, DB, H3])
    tails_s = ph.sb("tails_s", [DB * H3, GC])
    tails_p = ph.sb("tails_p", [H3, GC])
    sign, shift = ph.sb("sign", [P, NS]), ph.sb("shift", [P, NS])
    expa = ph.sb("expa", [P, GH])
    gy, gpos, gabs, gexp, gln, gsp = (ph.sb(n, [P, GT, NS]) for n in ("gy", "gpos", "gabs", "gexp", "gln", "gsp"))
    glogf = ph.sb("glogf", [P, GT, FH])
    gout = ph.sb("gout", [P, GT, 2 * GH])

    w_loaded = [ph.sem(f"w_loaded{n}") for n in range(8)]
    x_loaded = [ph.sem(f"x_loaded{n}") for n in range(2)]
    small_loaded, hist_loaded, setup_done = ph.sem("small_loaded"), ph.sem("hist_loaded"), ph.sem("setup_done")
    vecs_turned, vecs_ready = ph.sem("vecs_turned"), ph.sem("vecs_ready")
    x_squared, ln_done, rs_ready = ph.sem("x_squared"), ph.sem("ln_done"), ph.sem("rs_ready")
    xn_ready, xn_turned, xnT_ready, xnT_used = (ph.sem(n) for n in ("xn_ready", "xn_turned", "xnT_ready", "xnT_used"))
    rows_mm, rows_out = ph.sem("rows_mm"), ph.sem("rows_out")
    rows_stored = [ph.sem(f"rows_stored{n}") for n in range(4)]
    gates_mm, gates_read, gate_v, gate_a, gates_stored = (ph.sem(n) for n in (
        "gates_mm", "gates_read", "gate_v", "gate_a", "gates_stored"))
    chan_mm, chan_raw, conv_step, conv_done, silu_done = (ph.sem(n) for n in (
        "chan_mm", "chan_raw", "conv_step", "conv_done", "silu_done"))
    chan_stored = [ph.sem(f"chan_stored{n}") for n in range(2)]
    tail_turned, tail_ready, tail_stored = ph.sem("tail_turned"), ph.sem("tail_ready"), ph.sem("tail_stored")

    wi = io["w_in"][0].rearrange("(k p) n -> p k n", p=P)
    w_parts = [(0, FW), (FW, 2 * FW), (2 * FW, 3 * FW), (off_z, N_IN), (off_f, off_g), (off_a, off_z),
               (off_g, off_g + GC // 2), (off_g + GC // 2, off_a)]
    row_chunks = [(0, "q"), (FW, "k"), (2 * FW, "v"), (off_z, "z")]

    def place(g, m):
        if g is None:
            return 0, 0, 0, 1
        s = m % 2
        return g * GT + (m + 1), m, s, g * (GT // 2) + (m // 2 + 1 + (1 if s == 0 else 0))

    def slot_free(g, m):
        return g * GT + (m + 1 if m == 0 else m)

    def rows_dst(name, g, m):
        if g is None:
            return {"q": io["q_tok"][SEQ:, :], "k": io["k_s"], "v": io["v_s"], "z": io["z_tok"][SEQ:, :]}[name]
        return {"q": io["q_tok"], "k": io["k_p"], "v": io["v_p"], "z": io["z_tok"]}[name][
            bass.ds(g * W + m * P, P), :]

    with nc.Block() as block:

        @block.sync
        def _(sp):
            sp.dma_start(x[:, 0], io["x_s"]).then_inc(x_loaded[0], 16)
            sp.dma_start(vec_rows[0:KD], io["norm_mix_w"].rearrange("l (k p) -> (l k) p", p=P)) \
                .then_inc(small_loaded, 16)
            sp.dma_start(vec_rows[KD:], io["gdn_conv_w"].rearrange("l i (k p) -> (l i k) p", p=P)) \
                .then_inc(small_loaded, 16)
            sp.dma_start(shift[:, 0:FH], io["b_fox_f"][0].partition_broadcast(P)).then_inc(small_loaded, 16)
            sp.dma_start(shift[:, FH:FH + GH], io["gdn_dt_bias"][0].partition_broadcast(P)).then_inc(small_loaded, 16)
            sp.dma_start(expa[:], io["gdn_a_log"][0].partition_broadcast(P)).then_inc(small_loaded, 16)
            sp.dma_start(tails_s[:], io["conv_state"]).then_inc(hist_loaded, 16)
            for n, (a, b) in enumerate(w_parts):
                sp.dma_start(w[:, :, a:b], wi[:, :, a:b]).then_inc(w_loaded[n], 16)
            with sp.Fori(0, NG) as g:
                for m in range(GT):
                    sp.wait_ge(xn_ready, slot_free(g, m))
                    sp.dma_start(x[:, m % 2], io["x_p"][bass.ds(g * W + m * P, P), :]).then_inc(x_loaded[m % 2], 16)

        @block.tensor
        def _(pe):
            def turn(g, m):
                T, at, s, _ = place(g, m)
                pe.wait_ge(xn_ready, T + 1)
                for h in range(2):
                    pe.wait_ge(xnT_ready, 2 * T + (h + 1))
                    for k in range(HB):
                        mm = pe.transpose(bank[:, h, k * P:(k + 1) * P],
                                          xn[:, s, (h * HB + k) * P:(h * HB + k + 1) * P], c["ident"][:])
                    mm.then_inc(xn_turned, 1)

            def row_products(g, m):
                T, at, _, _ = place(g, m)
                pe.wait_ge(xnT_ready, 2 * T + 4)
                for n, (col, _) in enumerate(row_chunks):
                    if g is None:
                        pe.wait_ge(w_loaded[n], 16)
                    pe.wait_ge(rows_out, 4 * T + (n + 1))
                    for k in range(KD):
                        mm = pe.matmul(bank[:, 2 + n % 2, :], xnT[:, k, at * P:(at + 1) * P], w[:, k, col:col + BANK],
                                       start=(k == 0), stop=(k == KD - 1))
                    mm.then_inc(rows_mm, 1)
                if g is None:
                    pe.wait_ge(w_loaded[4], 16)
                    pe.wait_ge(w_loaded[5], 16)
                for a, b, o in ((off_f, off_g, 0), (off_a, off_z, FH)):
                    for k in range(KD):
                        mm = pe.matmul(bank[:, 6, at * NS + o:at * NS + o + b - a], xnT[:, k, at * P:(at + 1) * P],
                                       w[:, k, a:b], start=(k == 0), stop=(k == KD - 1))
                mm.then_inc(gates_mm, 1)

            def channel_products(G, width):
                for ch in range(NCH):
                    if width == P and ch % (NCH // 2) == 0:
                        pe.wait_ge(w_loaded[6 + ch // (NCH // 2)], 16)
                    pe.wait_ge(chan_raw, NCH * G + (ch + 1))
                    for k in range(KD):
                        mm = pe.matmul(bank[:, 4 + ch % 2, 0:width], w[:, k, off_g + ch * P:off_g + (ch + 1) * P],
                                       xnT[:, k, 0:width], start=(k == 0), stop=(k == KD - 1))
                    mm.then_inc(chan_mm, 1)

            pe.wait_ge(small_loaded, 16 * 5)
            pe.transpose(bank[:, 6, 0:KD + CW * NCH], vec_rows[:], c["ident"][0:KD + CW * NCH, 0:KD + CW * NCH])
            pe.wait_ge(hist_loaded, 16)
            for ch in range(NCH):
                mm = pe.transpose(bank[:, 7, ch * DB * H3:(ch + 1) * DB * H3], tails_s[:, ch * P:(ch + 1) * P],
                                  c["ident"][0:DB * H3, 0:DB * H3])
            mm.then_inc(vecs_turned, 1)
            turn(None, 0)
            pe.wait_ge(vecs_ready, 2)
            row_products(None, 0)
            channel_products(0, P)
            with pe.Fori(0, NG) as g:
                pe.wait_ge(gates_read, g + 1)
                turn(g, 0)
                turn(g, 1)
                for m in range(GT):
                    row_products(g, m)
                    if m + 2 < GT:
                        turn(g, m + 2)
                channel_products(g + 1, W)
            pe.wait_ge(conv_done, NCH * (NG + 1) + 2)
            pe.wait_ge(rows_out, 4 * (NG * GT + 1) + 2)
            for ch in range(NCH):
                pe.transpose(bank[0:DB * H3, ch // 4, (ch % 4) * P:(ch % 4 + 1) * P],
                             hist_s[:, ch].rearrange("p b r -> p (b r)"), c["ident"][:])
                mm = pe.transpose(bank[0:H3, 3 + ch // 4, (ch % 4) * P:(ch % 4 + 1) * P], hist[:, ch], c["ident"][:])
            mm.then_inc(tail_turned, 1)

        @block.scalar
        def _(act):
            def norm_factor(g, m):
                T, _, s, loads = place(g, m)
                act.wait_ge(x_loaded[s], 16 * loads)
                if g is not None:
                    act.wait_ge(xn_ready, slot_free(g, m))
                nc.scalar.activation(squares[:], x[:, s], ACT.Square, accum_out=ss[:, s:s + 1]).then_inc(x_squared, 1)
                act.wait_ge(x_squared, T + 1)
                nc.scalar.activation(ln_ms[:, s:s + 1], ss[:, s:s + 1], ACT.Ln, scale=1.0 / D, bias=c["eps"][:]) \
                    .then_inc(ln_done, 1)
                act.wait_ge(ln_done, T + 1)
                nc.scalar.activation(rs[:, s:s + 1], ln_ms[:, s:s + 1], ACT.Exp, scale=-0.5).then_inc(rs_ready, 1)

            def row_copies(g, m):
                T, _, _, _ = place(g, m)
                for n, (_, name) in enumerate(row_chunks):
                    act.wait_ge(rows_mm, 4 * T + (n + 1))
                    act.wait_ge(rows_stored[n], 16 * T + 16)
                    nc.scalar.activation(rows[:, n], bank[:, 2 + n % 2, :], ACT.Silu if name == "z" else ACT.Copy) \
                        .then_inc(rows_out, 1)
                    act.wait_ge(rows_out, 4 * T + (n + 3))
                    act.dma_start(rows_dst(name, g, m), rows[:, n]).then_inc(rows_stored[n], 16)

            def gates(G, g, tiles):
                act.wait_ge(gate_v, 7 * G + 4)
                nc.scalar.activation(gexp[:, 0:tiles], gabs[:, 0:tiles], ACT.Exp, scale=-1.0).then_inc(gate_a, 1)
                act.wait_ge(gate_a, 3 * G + 2)
                nc.scalar.activation(gln[:, 0:tiles], gexp[:, 0:tiles], ACT.Ln, bias=c["ones"][:, 0:1]) \
                    .then_inc(gate_a, 1)
                act.wait_ge(gate_v, 7 * G + 5)
                nc.scalar.activation(gout[:, 0:tiles, GH:], gsp[:, 0:tiles, FH + GH:], ACT.Exp, scale=-1.0) \
                    .then_inc(gate_a, 1)
                act.wait_ge(gate_a, 3 * G + 4)
                act.wait_ge(gate_v, 7 * G + 7)
                if g is None:
                    logf_dst, gb_dst = io["logf_s"].unsqueeze(1), io["gb_tok"][SEQ:, :].unsqueeze(1)
                else:
                    logf_dst, gb_dst = (io[n][bass.ds(g * W, W), :].rearrange("(m p) h -> p m h", p=P)
                                        for n in ("logf_p", "gb_tok"))
                act.dma_start(logf_dst, glogf[:, 0:tiles]).then_inc(gates_stored, 16)
                act.dma_start(gb_dst, gout[:, 0:tiles]).then_inc(gates_stored, 16)

            def silu(G, g, ch):
                s, width = ch % 2, P if g is None else W
                act.wait_ge(conv_done, NCH * G + (ch + 3))
                nc.scalar.activation(acc[:, s, 0:width], acc[:, s, 0:width], ACT.Silu).then_inc(silu_done, 1)
                act.wait_ge(silu_done, NCH * G + (ch + 1))
                cols = slice(SEQ, SEQ + P) if g is None else bass.ds(g * W, W)
                act.dma_start(io["gch"][ch * P:(ch + 1) * P, cols], acc[:, s, 0:width]).then_inc(chan_stored[s], 16)

            def channels(G, g):
                for ch in range(NCH):
                    s = ch % 2
                    act.wait_ge(chan_mm, NCH * G + (ch + 1))
                    act.wait_ge(conv_done, NCH * G + (ch + 1))
                    if g is None:
                        nc.scalar.copy(raw[:, s, 0:DB * (H3 + DS)].rearrange("p (b r) -> p b r", b=DB)[:, :, H3:],
                                       bank[:, 4 + s, 0:P].rearrange("p (b r) -> p b r", b=DB)).then_inc(chan_raw, 1)
                    else:
                        nc.scalar.copy(raw[:, s, H3:], bank[:, 4 + s, :]).then_inc(chan_raw, 1)
                    if ch >= 1:
                        silu(G, g, ch - 1)
                silu(G, g, NCH - 1)

            act.sem_inc(rows_out, 2)
            act.sem_inc(chan_raw, 2)
            for n in range(4):
                act.sem_inc(rows_stored[n], 16)
            for s in range(2):
                act.sem_inc(chan_stored[s], 16)
            act.wait_ge(small_loaded, 16 * 5)
            nc.scalar.activation(expa[:], expa[:], ACT.Exp).then_inc(gate_a, 1)
            norm_factor(None, 0)
            row_copies(None, 0)
            gates(0, None, 1)
            channels(0, None)
            with act.Fori(0, NG) as g:
                norm_factor(g, 0)
                norm_factor(g, 1)
                norm_factor(g, 2)
                row_copies(g, 0)
                norm_factor(g, 3)
                for m in range(1, GT):
                    row_copies(g, m)
                gates(g + 1, g, GT)
                channels(g + 1, g)
            act.wait_ge(tail_ready, 1)
            act.dma_start(io["conv_s"], tails_s[:]).then_inc(tail_stored, 16)
            act.dma_start(io["conv_p"], tails_p[:]).then_inc(tail_stored, 16)
            for n in range(4):
                act.wait_ge(rows_stored[n], 16 * (NG * GT + 2))
            for s in range(2):
                act.wait_ge(chan_stored[s], 16 * (NG + 1) * (NCH // 2) + 16)
            act.wait_ge(gates_stored, 32 * (NG + 1))
            act.wait_ge(tail_stored, 32)

        @block.vector
        def _(dve):
            def normalise(g, m):
                T, at, s, _ = place(g, m)
                dve.wait_ge(rs_ready, T + 1)
                if g is not None:
                    dve.wait_ge(xn_turned, 2 * slot_free(g, m))
                nc.vector.tensor_scalar(xn[:, s], x[:, s], rs[:, s:s + 1], None, ALU.mult).then_inc(xn_ready, 1)
                if g is not None:
                    dve.wait_ge(chan_mm, NCH * (g + 1))
                for h in range(2):
                    dve.wait_ge(xn_turned, 2 * T + (h + 1))
                    nc.vector.tensor_tensor(
                        xnT[:, h * HB:(h + 1) * HB, at * P:(at + 1) * P],
                        bank[:, h, :].rearrange("p (k t) -> p k t", t=P),
                        spread(vecs[:, h * HB:(h + 1) * HB].unsqueeze(2), [P, HB, P]), ALU.mult) \
                        .then_inc(xnT_ready, 1)

            def gates(G, g, tiles):
                if g is not None:
                    dve.wait_ge(gates_stored, 32 * G)
                dve.wait_ge(gates_mm, 1 if g is None else g * GT + (GT + 1))
                v = 7 * G
                y, sh = gy[:, 0:tiles], [P, tiles, NS]
                nc.vector.tensor_tensor(y, bank[:, 6, 0:tiles * NS].rearrange("p (m n) -> p m n", n=NS),
                                        spread(sign[:].unsqueeze(1), sh), ALU.mult).then_inc(gate_v, 1)
                dve.wait_ge(gate_v, v + 1)
                dve.sem_inc(gates_read, 1)
                nc.vector.tensor_tensor(y, y, spread(shift[:].unsqueeze(1), sh), ALU.add).then_inc(gate_v, 1)
                dve.wait_ge(gate_v, v + 2)
                nc.vector.tensor_scalar(gpos[:, 0:tiles], y, 0.0, None, ALU.max).then_inc(gate_v, 1)
                nc.vector.scalar_tensor_tensor(gabs[:, 0:tiles], y, -1.0, y, ALU.mult, ALU.max).then_inc(gate_v, 1)
                dve.wait_ge(gate_a, 3 * G + 3)
                dve.wait_ge(gate_v, v + 4)
                nc.vector.tensor_tensor(gsp[:, 0:tiles], gpos[:, 0:tiles], gln[:, 0:tiles], ALU.add) \
                    .then_inc(gate_v, 1)
                dve.wait_ge(gate_v, v + 5)
                nc.vector.tensor_scalar(glogf[:, 0:tiles], gsp[:, 0:tiles, 0:FH], -1.0, None, ALU.mult) \
                    .then_inc(gate_v, 1)
                nc.vector.scalar_tensor_tensor(gout[:, 0:tiles, 0:GH], gsp[:, 0:tiles, FH:FH + GH], -1.0,
                                               spread(expa[:].unsqueeze(1), [P, tiles, GH]), ALU.mult, ALU.mult) \
                    .then_inc(gate_v, 1)

            def conv(G, g, ch):
                s, n, st = ch % 2, NCH * G + ch, 5 * (NCH * G + ch)
                width = P if g is None else W
                if g is None:
                    r = raw[:, s, 0:DB * (H3 + DS)].rearrange("p (b r) -> p b r", b=DB)
                    a = acc[:, s, 0:P].rearrange("p (b r) -> p b r", b=DB)
                    past, old, new = hist_s[:, ch], r[:, :, 0:H3], r[:, :, DS:]
                    taps = [r[:, :, i:i + DS] for i in range(CW)]
                else:
                    r, a = raw[:, s], acc[:, s]
                    past, old, new = hist[:, ch], r[:, 0:H3], r[:, W:]
                    taps = [r[:, i:i + W] for i in range(CW)]
                wt = [vecs[:, KD + i * NCH + ch:KD + i * NCH + ch + 1] for i in range(CW)]
                dve.wait_ge(conv_done, n + 1)
                nc.vector.tensor_copy(old, past).then_inc(conv_step, 1)
                dve.wait_ge(conv_step, st + 1)
                dve.wait_ge(chan_raw, n + 3)
                nc.vector.tensor_copy(past, new).then_inc(conv_step, 1)
                dve.wait_ge(chan_stored[s], 16 * ((NCH // 2) * G + (ch // 2 + 1)))
                nc.vector.tensor_scalar(a, taps[0], wt[0], None, ALU.mult).then_inc(conv_step, 1)
                for i in range(1, CW):
                    dve.wait_ge(conv_step, st + (2 + i))
                    nc.vector.scalar_tensor_tensor(a, taps[i], wt[i], a, ALU.mult, ALU.add) \
                        .then_inc(conv_step if i < CW - 1 else conv_done, 1)

            dve.sem_inc(xnT_ready, 2)
            dve.sem_inc(conv_done, 2)
            step = Step(dve, setup_done)
            step(nc.vector.memset(sign[:], -1.0))
            step(nc.vector.memset(sign[:, FH:FH + GH], 1.0))
            step(nc.vector.memset(shift[:, FH + GH:], 0.0))
            step(nc.vector.memset(hist[:], 0.0))
            dve.wait_ge(small_loaded, 16 * 5)
            step(nc.vector.tensor_tensor(shift[:], shift[:], sign[:], ALU.mult))
            dve.wait_ge(vecs_turned, 1)
            nc.vector.tensor_copy(vecs[:], bank[:, 6, 0:KD + CW * NCH]).then_inc(vecs_ready, 1)
            nc.vector.tensor_copy(hist_s[:].rearrange("p c b r -> p (c b r)"), bank[:, 7, 0:NCH * DB * H3]) \
                .then_inc(vecs_ready, 1)
            dve.wait_ge(vecs_ready, 2)
            dve.wait_ge(gate_a, 1)
            normalise(None, 0)
            gates(0, None, 1)
            for ch in range(NCH):
                conv(0, None, ch)
            with dve.Fori(0, NG) as g:
                for m in range(GT):
                    normalise(g, m)
                gates(g + 1, g, GT)
                for ch in range(NCH):
                    conv(g + 1, g, ch)
            dve.wait_ge(tail_turned, 1)
            step = Step(dve, setup_done)
            step.n = 5
            for n in range(NCH // 4):
                step(nc.vector.tensor_copy(tails_s[:, n * BANK:(n + 1) * BANK], bank[0:DB * H3, n, :]))
                step(nc.vector.tensor_copy(tails_p[:, n * BANK:(n + 1) * BANK], bank[0:H3, 3 + n, :]))
            dve.sem_inc(tail_ready, 1)
    ph.close()


def delta(nc, c, io, bank):
    ph = Phase(nc, "gdn")
    GH, GC, DK, DV, FW, DB, DS, SEQ = (c[k] for k in ("GH", "GC", "DK", "DV", "FW", "DB", "DS", "SEQ"))
    NCH, NC, HH = GC // P, SEQ // P, GH // 2
    LEVELS, LEVELS_S = 7, 4
    assert (1 << LEVELS) == P and (1 << LEVELS_S) == DS

    def wide(name, n=GH):
        return ph.sb(name, [P, n, P])

    qkvT = wide("qkvT", NCH)
    gb = ph.sb("gb", [P, 2 * GH])
    z, zn, gnorm = wide("z"), wide("zn"), ph.sb("gnorm", [P, DV])
    sq, ss, ln_ss, unit = wide("sq", 2 * GH), *(ph.sb(n, [P, 2 * GH]) for n in ("ss", "ln_ss", "unit"))
    gs, ex = ph.sb("gs", [P, 3 * GH]), ph.sb("ex", [P, 3 * GH])
    f_q, f_qG, f_kb, f_bG = (ph.sb(n, [P, GH]) for n in ("f_q", "f_qG", "f_kb", "f_bG"))
    dx, dec = wide("dx"), wide("dec")
    kn, kb, qn, qG, vb, kbG, kd = (wide(n) for n in ("kn", "kb", "qn", "qG", "vb", "kbG", "kd"))
    knT, kbT, qnT, qGT = (wide(n) for n in ("knT", "kbT", "qnT", "qGT"))
    LT, AT, wn, X, XT, x0 = (wide(n) for n in ("LT", "AT", "wn", "X", "XT", "x0"))
    nwT, dl, S, osq, on, mixed = (wide(n) for n in ("nwT", "dl", "S", "osq", "on", "mixed"))
    so, ln_so, ro = (ph.sb(n, [P, GH]) for n in ("so", "ln_so", "ro"))
    S_s = ph.sb("S_s", [P, DB, GH, DV])
    ex_s = ph.sb("ex_s", [P, DB, GH])
    dlT, oT, kd_b = wide("dlT"), wide("oT"), ph.sb("kd_b", [P, 2, GH, P])

    names = ("qkv_loaded gb_loaded z_loaded small_loaded state_loaded tok_turned gsum_mm decay_mm unitT_mm unitT_out "
             "kk_mm l0_mm w_mm y_mm xt_mm wt_mm nwt_ready delta_mm delta_ready o_mm s_mm state_ready o_scaled "
             "gsum_v decay_v decay_ready squares_ready sumsq_ready unit_ready ex_ready fac_v scaled_ready lt_ready "
             "x0_step x_ready w_ready xt0_ready xt_ready xt_last o_sq o_sum o_unit pool_scaled pool_x0 zn_ready mix_ready mix_stored "
             "ex_s_ready dlT_mm dlT_ready oT_mm oT_ready kdb_ready sb_mm sb_ready s_stored o_free").split()
    s = {n: ph.sem(n) for n in names}

    XR, WR, YR, TR = 2 * (LEVELS - 1), 2 * (LEVELS - 1), 2 * (LEVELS - 1), 2 * (LEVELS - 2)

    def half(t, a):
        return t[:, a * HH:(a + 1) * HH, :]

    def heads(b):
        return bank[:, b, :].rearrange("p (h n) -> p h n", n=P)

    def bank_half(b):
        return bank[:, b, 0:HH * P].rearrange("p (h n) -> p h n", n=P)

    def per_head(f):
        return spread(f.unsqueeze(2), [P, GH, P])

    with nc.Block() as block:

        @block.sync
        def _(sp):
            def load(t, qkv_free, gb_free, z_free):
                rows = bass.ds(t * P, P)
                qkv_free()
                sp.dma_start(qkvT[:], io["gch"][:, rows].rearrange("(c p) t -> p c t", p=P)) \
                    .then_inc(s["qkv_loaded"], 16)
                gb_free()
                sp.dma_start(gb[:], io["gb_tok"][rows, :]).then_inc(s["gb_loaded"], 16)
                z_free()
                sp.dma_start(z[:], io["z_tok"][rows, :].rearrange("t (h n) -> t h n", n=DV)).then_inc(s["z_loaded"], 16)

            def store(t):
                sp.wait_ge(s["mix_ready"], t + 2)
                sp.dma_start(io["mix_tok"][bass.ds(t * P, P), FW:].rearrange("t (h n) -> t h n", n=DV), mixed[:]) \
                    .then_inc(s["mix_stored"], 16)

            load(0, lambda: None, lambda: None, lambda: None)
            sp.dma_start(gnorm[:], io["gdn_norm_w"][0].partition_broadcast(P)).then_inc(s["small_loaded"], 16)
            sp.dma_start(S_s[:].rearrange("p b h n -> p (b h) n"), io["state_gdn"][0].rearrange("b h k n -> k (b h) n")) \
                .then_inc(s["state_loaded"], 16)
            with sp.Fori(0, NC) as t:
                def gb_read():
                    sp.wait_ge(s["scaled_ready"], 5 * t + 5)
                    sp.wait_ge(s["decay_mm"], t + 1)
                load(t + 1, lambda: sp.wait_ge(s["tok_turned"], 3 * t + 3), gb_read,
                     lambda: sp.wait_ge(s["zn_ready"], t + 1))
                store(t)
            store(NC)
            sp.wait_ge(s["state_ready"], GH * (NC + 1))
            sp.dma_start(io["S_p"].rearrange("h k n -> k h n"), S[:]).then_inc(s["s_stored"], 16)
            sp.wait_ge(s["sb_ready"], GH * DB)
            sp.dma_start(io["S_s"].rearrange("b h k n -> k (b h) n"), S_s[:].rearrange("p b h n -> p (b h) n")) \
                .then_inc(s["s_stored"], 16)
            sp.wait_ge(s["s_stored"], 32)
            sp.wait_ge(s["mix_stored"], 16 * (NC + 2))

        @block.tensor
        def _(pe):
            def chunk(t, streams):
                tri, total, mask = (c["tri_s"], c["same_stream"], c["decay_mask_s"]) if streams else \
                    (c["tri"], c["ones"], c["decay_mask"])
                levels = LEVELS_S if streams else LEVELS
                pe.wait_ge(s["qkv_loaded"], 16 * t + 16)
                pe.wait_ge(s["o_scaled"], t + 1)
                pe.wait_ge(s["state_ready"], GH * t + GH)
                for j in range(3):
                    for h in range(GH):
                        mm = pe.transpose(bank[:, j, h * P:(h + 1) * P], qkvT[:, j * GH + h, :], c["ident"][:])
                    mm.then_inc(s["tok_turned"], 1)
                pe.wait_ge(s["gb_loaded"], 16 * t + 16)
                pe.matmul(bank[:, 3, 0:GH], tri[:], gb[:, 0:GH], start=True, stop=True)
                mm = pe.matmul(bank[:, 3, GH:2 * GH], total[:], gb[:, 0:GH], start=True, stop=True)
                if streams:
                    for b in range(DB):
                        mm = pe.matmul(bank[:, 3, (2 + b) * GH:(3 + b) * GH],
                                       spread(c["stream_rows"][:, b:b + 1], [P, P]), gb[:, 0:GH], start=True, stop=True)
                mm.then_inc(s["gsum_mm"], 1)
                pe.matmul(bank[:, 4, :], c["ident"][:], spread(mask[:].unsqueeze(1), [P, GH, P]),
                          start=True, stop=False)
                for h in range(GH):
                    mm = pe.matmul(bank[:, 4, h * P:(h + 1) * P], spread(gb[:, h:h + 1], [P, P]), tri[:],
                                   start=False, stop=(h == GH - 1))
                mm.then_inc(s["decay_mm"], 1)
                for n, (src, b) in enumerate(((kn, 5), (kb, 6), (qn, 7), (qG, 1))):
                    pe.wait_ge(s["scaled_ready"], 5 * t + (n + 1))
                    for h in range(GH):
                        mm = pe.transpose(bank[:, b, h * P:(h + 1) * P], src[:, h, :], c["ident"][:])
                    mm.then_inc(s["unitT_mm"], 1)
                pe.wait_ge(s["unitT_out"], 4 * t + 2)
                for h in range(GH):
                    mm = pe.matmul(bank[:, 0, h * P:(h + 1) * P], knT[:, h, :], kbT[:, h, :], start=True, stop=True)
                mm.then_inc(s["kk_mm"], 1)
                pe.wait_ge(s["unitT_out"], 4 * t + 3)
                pe.wait_ge(s["scaled_ready"], 5 * t + 5)
                for h in range(GH):
                    mm = pe.matmul(bank[:, 2, h * P:(h + 1) * P], knT[:, h, :], qnT[:, h, :], start=True, stop=True)
                mm.then_inc(s["kk_mm"], 1)
                pe.wait_ge(s["lt_ready"], 2 * t + 1)
                for a in range(2):
                    for h in range(HH):
                        mm = pe.transpose(bank[:, 3 + a, h * P:(h + 1) * P], LT[:, a * HH + h, :], c["ident"][:])
                    mm.then_inc(s["l0_mm"], 1)
                pe.wait_ge(s["unitT_out"], 4 * t + 4)
                for n in range(1, levels):
                    for a in range(2):
                        pe.wait_ge(s["x_ready"], XR * t + (2 * (n - 1) + a + 1))
                        for h in range(HH):
                            mm = pe.matmul(bank[:, 5 + a, h * P:(h + 1) * P], LT[:, a * HH + h, :], X[:, a * HH + h, :],
                                           start=True, stop=True)
                        mm.then_inc(s["w_mm"], 1)
                    if n >= 2:
                        for a in range(2):
                            for h in range(HH):
                                mm = pe.transpose(bank[:, 3 + a, h * P:(h + 1) * P], X[:, a * HH + h, :], c["ident"][:])
                            mm.then_inc(s["xt_mm"], 1)
                    for a in range(2):
                        pe.wait_ge(s["w_ready"], WR * t + (2 * (n - 1) + a + 1))
                        if n == 1:
                            pe.wait_ge(s["xt0_ready"], t + 1)
                        else:
                            pe.wait_ge(s["xt_ready"], TR * t + (2 * (n - 2) + a + 1))
                        for h in range(HH):
                            at = a * HH + h
                            lhsT, rhs = (XT, wn) if n < levels - 1 else (wn, XT)
                            mm = pe.matmul(bank[:, 7 if a == 0 else 1, h * P:(h + 1) * P], lhsT[:, at, :], rhs[:, at, :],
                                           start=True, stop=True)
                        mm.then_inc(s["y_mm"], 1)
                pe.wait_ge(s["xt_last"], 2 * t + 2)
                pe.wait_ge(s["pool_scaled"], 2 * t + 2)
                for h in range(GH):
                    mm = pe.matmul(bank[:, 5, h * P:(h + 1) * P], kbG[:, h, :], XT[:, h, :], start=True, stop=True)
                mm.then_inc(s["wt_mm"], 1)
                pe.wait_ge(s["nwt_ready"], t + 1)
                pe.wait_ge(s["lt_ready"], 2 * t + 2)
                if streams:
                    finish_streams(t)
                    return
                for h in range(GH):
                    o = bank[:, 6, h * P:(h + 1) * P]
                    pe.matmul(o, XT[:, h, :], vb[:, h, :], start=True, stop=False)
                    mm = pe.matmul(o, nwT[:, h, :], S[:, h, :], start=False, stop=True)
                mm.then_inc(s["delta_mm"], 1)
                pe.wait_ge(s["delta_ready"], t + 1)
                for h in range(GH):
                    o = bank[:, 0, h * P:(h + 1) * P]
                    pe.matmul(o, qGT[:, h, :], S[:, h, :], start=True, stop=False)
                    mm = pe.matmul(o, AT[:, h, :], dl[:, h, :], start=False, stop=True)
                mm.then_inc(s["o_mm"], 1)
                for h in range(GH):
                    mm = pe.matmul(bank[:, 2, h * P:(h + 1) * P], kd[:, h, :], dl[:, h, :], start=True, stop=True)
                mm.then_inc(s["s_mm"], 1)

            def finish_streams(t):
                pe.wait_ge(s["state_loaded"], 16)
                for out, sem, first, second, cols in ((6, "dlT_mm", vb, XT, nwT), (7, "oT_mm", dl, AT, qGT)):
                    if out == 7:
                        pe.wait_ge(s["dlT_ready"], 1)
                        for h in range(GH):
                            mm = pe.transpose(bank[:, 5, h * P:(h + 1) * P], dlT[:, h, :], c["ident"][:])
                        mm.then_inc(s["delta_mm"], 1)
                        pe.wait_ge(s["delta_ready"], t + 1)
                    for h in range(GH):
                        pe.matmul(bank[:, out, h * P:(h + 1) * P], first[:, h, :], second[:, h, :],
                                  start=True, stop=False)
                        for b in range(DB):
                            at = h * P + b * DS
                            mm = pe.matmul(bank[:, out, at:at + DS], S_s[:, b, h, :], cols[:, h, b * DS:(b + 1) * DS],
                                           start=False, stop=(b == DB - 1))
                    mm.then_inc(s[sem], 1)
                pe.wait_ge(s["oT_ready"], 1)
                for h in range(GH):
                    mm = pe.transpose(bank[:, 0, h * P:(h + 1) * P], oT[:, h, :], c["ident"][:])
                mm.then_inc(s["o_mm"], 1)
                for b in range(DB):
                    pe.wait_ge(s["kdb_ready"], b + 1)
                    if b >= 2:
                        pe.wait_ge(s["sb_ready"], GH * (b - 1))
                    for h in range(GH):
                        mm = pe.matmul(bank[:, 2 + b % 2, h * P:(h + 1) * P], kd_b[:, b % 2, h, :], dl[:, h, :],
                                       start=True, stop=True)
                    mm.then_inc(s["sb_mm"], 1)

            with pe.Fori(0, NC) as t:
                chunk(t, False)
            chunk(NC, True)

        @block.scalar
        def _(act):
            def chunk(t, streams):
                levels = LEVELS_S if streams else LEVELS
                for j in range(2):
                    act.wait_ge(s["tok_turned"], 3 * t + (j + 1))
                    nc.scalar.activation(sq[:, j * GH:(j + 1) * GH, :], heads(j), ACT.Square) \
                        .then_inc(s["squares_ready"], 1)
                act.wait_ge(s["gsum_v"], 2 * t + 2)
                nc.scalar.activation(ex[:], gs[:], ACT.Exp).then_inc(s["ex_ready"], 1)
                if streams:
                    nc.scalar.activation(ex_s[:].rearrange("p b h -> p (b h)"), bank[:, 3, 2 * GH:(2 + DB) * GH],
                                         ACT.Exp).then_inc(s["ex_s_ready"], 1)
                act.wait_ge(s["sumsq_ready"], t + 1)
                nc.scalar.activation(ln_ss[:], ss[:], ACT.Ln, bias=c["eps"][:]).then_inc(s["unit_ready"], 1)
                act.wait_ge(s["unit_ready"], 2 * t + 1)
                nc.scalar.activation(unit[:], ln_ss[:], ACT.Exp, scale=-0.5).then_inc(s["unit_ready"], 1)
                act.wait_ge(s["decay_v"], t + 1)
                nc.scalar.activation(dec[:], dx[:], ACT.Exp).then_inc(s["decay_ready"], 1)
                for n, (dst, b) in enumerate(((knT, 5), (kbT, 6), (qnT, 7), (qGT, 1))):
                    act.wait_ge(s["unitT_mm"], 4 * t + (n + 1))
                    nc.scalar.copy(dst[:], heads(b)).then_inc(s["unitT_out"], 1)
                for n in range(2, levels):
                    for a in range(2):
                        act.wait_ge(s["xt_mm"], TR * t + (2 * (n - 2) + a + 1))
                        nc.scalar.copy(half(XT, a), bank_half(3 + a)).then_inc(s["xt_ready"], 1)
                act.wait_ge(s["wt_mm"], t + 1)
                nc.scalar.mul(nwT[:], heads(5), -1.0).then_inc(s["nwt_ready"], 1)
                if streams:
                    act.wait_ge(s["dlT_mm"], 1)
                    nc.scalar.copy(dlT[:], heads(6)).then_inc(s["dlT_ready"], 1)
                    act.wait_ge(s["oT_mm"], 1)
                    nc.scalar.copy(oT[:], heads(7)).then_inc(s["oT_ready"], 1)
                act.wait_ge(s["o_mm"], t + 1)
                nc.scalar.activation(osq[:], heads(0), ACT.Square).then_inc(s["o_sq"], 1)
                act.wait_ge(s["o_sum"], t + 1)
                nc.scalar.activation(ln_so[:], so[:], ACT.Ln, scale=1.0 / DV, bias=c["eps"][:]) \
                    .then_inc(s["o_unit"], 1)
                act.wait_ge(s["o_unit"], 2 * t + 1)
                nc.scalar.activation(ro[:], ln_so[:], ACT.Exp, scale=-0.5).then_inc(s["o_unit"], 1)

            with act.Fori(0, NC) as t:
                chunk(t, False)
            chunk(NC, True)

        @block.gpsimd
        def _(pool):
            def chunk(t):
                pool.wait_ge(s["z_loaded"], 16 * t + 16)
                pool.wait_ge(s["mix_ready"], t + 1)
                nc.gpsimd.tensor_tensor(zn[:], z[:], spread(gnorm[:].unsqueeze(1), [P, GH, DV]), ALU.mult) \
                    .then_inc(s["zn_ready"], 1)
                pool.wait_ge(s["scaled_ready"], 5 * t + 1)
                pool.wait_ge(s["fac_v"], 4 * t + 3)
                nc.gpsimd.tensor_tensor(kbG[:], kn[:], per_head(f_bG[:]), ALU.mult).then_inc(s["pool_scaled"], 1)
                nc.gpsimd.tensor_tensor(kd[:], kn[:], per_head(ex[:, 2 * GH:3 * GH]), ALU.mult) \
                    .then_inc(s["pool_scaled"], 1)
                pool.wait_ge(s["lt_ready"], 2 * t + 1)
                nc.gpsimd.tensor_tensor(x0[:], LT[:], spread(c["level0_t"][:].unsqueeze(1), [P, GH, P]), ALU.mult) \
                    .then_inc(s["pool_x0"], 1)
                pool.wait_ge(s["pool_x0"], t + 1)
                nc.gpsimd.tensor_tensor(XT[:], x0[:], spread(c["ident"][:].unsqueeze(1), [P, GH, P]), ALU.add) \
                    .then_inc(s["xt0_ready"], 1)
                pool.wait_ge(s["o_scaled"], t + 2)
                pool.wait_ge(s["mix_stored"], 16 * t + 16)
                pool.wait_ge(s["zn_ready"], t + 1)
                nc.gpsimd.tensor_tensor(mixed[:], on[:], zn[:], ALU.mult).then_inc(s["mix_ready"], 1)

            pool.sem_inc(s["mix_stored"], 16)
            pool.wait_ge(s["small_loaded"], 16)
            with pool.Fori(0, NC) as t:
                chunk(t)
            chunk(NC)

        @block.vector
        def _(dve):
            def chunk(t, streams):
                levels = LEVELS_S if streams else LEVELS
                tt, V = nc.vector.tensor_tensor, ALU.mult
                dve.wait_ge(s["gsum_mm"], t + 1)
                nc.vector.tensor_copy(gs[:, 0:2 * GH], bank[:, 3, 0:2 * GH]).then_inc(s["gsum_v"], 1)
                dve.wait_ge(s["gsum_v"], 2 * t + 1)
                tt(gs[:, 2 * GH:], gs[:, GH:2 * GH], gs[:, 0:GH], ALU.subtract).then_inc(s["gsum_v"], 1)
                dve.wait_ge(s["decay_mm"], t + 1)
                tt(dx[:], heads(4), per_head(gs[:, 0:GH]), ALU.subtract).then_inc(s["decay_v"], 1)
                dve.wait_ge(s["squares_ready"], 2 * t + 2)
                nc.vector.tensor_reduce(ss[:], sq[:], AX.X, ALU.add).then_inc(s["sumsq_ready"], 1)
                dve.wait_ge(s["unit_ready"], 2 * t + 2)
                dve.wait_ge(s["ex_ready"], t + 1)
                nc.vector.tensor_scalar(f_q[:], unit[:, 0:GH], float(DK) ** -0.5, None, ALU.mult).then_inc(s["fac_v"], 1)
                tt(f_kb[:], unit[:, GH:], gb[:, GH:], V).then_inc(s["fac_v"], 1)
                tt(f_bG[:], gb[:, GH:], ex[:, 0:GH], V).then_inc(s["fac_v"], 1)
                dve.wait_ge(s["fac_v"], 4 * t + 1)
                tt(f_qG[:], f_q[:], ex[:, 0:GH], V).then_inc(s["fac_v"], 1)
                tt(kn[:], heads(1), per_head(unit[:, GH:]), V).then_inc(s["scaled_ready"], 1)
                dve.wait_ge(s["fac_v"], 4 * t + 4)
                tt(kb[:], heads(1), per_head(f_kb[:]), V).then_inc(s["scaled_ready"], 1)
                tt(qn[:], heads(0), per_head(f_q[:]), V).then_inc(s["scaled_ready"], 1)
                tt(qG[:], heads(0), per_head(f_qG[:]), V).then_inc(s["scaled_ready"], 1)
                dve.wait_ge(s["tok_turned"], 3 * t + 3)
                tt(vb[:], heads(2), per_head(gb[:, GH:]), V).then_inc(s["scaled_ready"], 1)
                dve.wait_ge(s["decay_ready"], t + 1)
                dve.wait_ge(s["kk_mm"], 2 * t + 1)
                tt(LT[:], heads(0), dec[:], V).then_inc(s["lt_ready"], 1)
                dve.wait_ge(s["kk_mm"], 2 * t + 2)
                tt(AT[:], heads(2), dec[:], V).then_inc(s["lt_ready"], 1)
                for a in range(2):
                    dve.wait_ge(s["l0_mm"], 2 * t + (a + 1))
                    tt(half(wn, a), bank_half(3 + a), spread(c["level"][0][:].unsqueeze(1), [P, HH, P]), V) \
                        .then_inc(s["x0_step"], 1)
                for a in range(2):
                    dve.wait_ge(s["x0_step"], 2 * t + (a + 1))
                    tt(half(X, a), half(wn, a), spread(c["ident"][:].unsqueeze(1), [P, HH, P]), ALU.add) \
                        .then_inc(s["x_ready"], 1)
                for n in range(1, levels):
                    for a in range(2):
                        dve.wait_ge(s["w_mm"], WR * t + (2 * (n - 1) + a + 1))
                        tt(half(wn, a), bank_half(5 + a), spread(c["level"][n][:].unsqueeze(1), [P, HH, P]), V) \
                            .then_inc(s["w_ready"], 1)
                    for a in range(2):
                        dve.wait_ge(s["y_mm"], YR * t + (2 * (n - 1) + a + 1))
                        t_, sem = (X, "x_ready") if n < levels - 1 else (XT, "xt_last")
                        tt(half(t_, a), bank_half(7 if a == 0 else 1), half(t_, a), ALU.add).then_inc(s[sem], 1)
                dve.wait_ge(s["delta_mm"], t + 1)
                nc.vector.tensor_copy(dl[:], heads(5 if streams else 6)).then_inc(s["delta_ready"], 1)
                if not streams:
                    dve.wait_ge(s["s_mm"], t + 1)
                    for h in range(GH):
                        nc.vector.scalar_tensor_tensor(S[:, h, :], S[:, h, :], ex[:, GH + h:GH + h + 1],
                                                       bank[:, 2, h * P:(h + 1) * P], ALU.mult, ALU.add) \
                            .then_inc(s["state_ready"], 1)
                dve.wait_ge(s["o_sq"], t + 1)
                nc.vector.tensor_reduce(so[:], osq[:], AX.X, ALU.add).then_inc(s["o_sum"], 1)
                dve.wait_ge(s["o_unit"], 2 * t + 2)
                dve.wait_ge(s["mix_ready"], t + 1)
                tt(on[:], heads(0), per_head(ro[:]), V).then_inc(s["o_scaled"], 1)
                if streams:
                    dve.wait_ge(s["ex_s_ready"], 1)

                    def rows_of(b):
                        nc.vector.tensor_scalar(kd_b[:, b % 2], kd[:], c["stream_rows"][:, b:b + 1], None, ALU.mult) \
                            .then_inc(s["kdb_ready"], 1)

                    dve.wait_ge(s["pool_scaled"], 2 * t + 2)
                    rows_of(0)
                    rows_of(1)
                    for b in range(DB):
                        dve.wait_ge(s["sb_mm"], b + 1)
                        for h in range(GH):
                            nc.vector.scalar_tensor_tensor(S_s[:, b, h, :], S_s[:, b, h, :], ex_s[:, b, h:h + 1],
                                                           bank[:, 2 + b % 2, h * P:(h + 1) * P], ALU.mult, ALU.add) \
                                .then_inc(s["sb_ready"], 1)
                        if b + 2 < DB:
                            rows_of(b + 2)

            nc.vector.memset(S[:], 0.0).then_inc(s["state_ready"], GH)
            dve.sem_inc(s["o_scaled"], 1)
            dve.sem_inc(s["mix_ready"], 1)
            with dve.Fori(0, NC) as t:
                chunk(t, False)
            chunk(NC, True)
    ph.close()


def fox_prompt(nc, c, io, bank):
    ph = Phase(nc, "foxp")
    FH, FD, FW, SEQ = (c[k] for k in ("FH", "FD", "FW", "SEQ"))
    NB = SEQ // P
    GB = 4
    A = FD + 2
    banks_of = [n // GB + 1 for n in range(NB)]
    first = [sum(banks_of[:n]) for n in range(NB)]
    NBK = sum(banks_of)
    NG = NB // GB
    assert NB % GB == 0 and NBK % 4 == 0 and 2 * NG <= 8

    ktok, qtok, v = ph.sb("ktok", [P, NB, A]), ph.sb("qtok", [P, NB, A]), ph.sb("v", [P, NB, FD])
    kT, qT = ph.sb("kT", [A, SEQ]), ph.sb("qT", [A, SEQ])
    qscale = ph.sb("qscale", [A, 1])
    f, before, csum = (ph.sb(n, [P, NB, FH]) for n in ("f", "before", "csum"))
    logits = ph.sb("logits", [P, 3, SEQ])
    low, neg_max, row_sum, inv_sum = ph.sb("low", [P, 3, GB]), *(ph.sb(n, [P, 3]) for n in ("nmax", "rsum", "inv"))
    pT = ph.sb("pT", [P, 2, GB, P])
    o = ph.sb("o", [P, NB, FD])

    (f_loaded, f_step, c_mm, c_ready, kq_loaded, v_loaded, aug_ready, prep_mm, prep_out_a, prep_out_v, qk_mm,
     s_out, low_ready, max_ready, p_ready, pt_mm, pt_out_v, pt_out_a, pv_mm, inv_ready, o_out, o_stored) = (
        ph.sem(n) for n in (
            "f_loaded f_step c_mm c_ready kq_loaded v_loaded aug_ready prep_mm prep_out_a prep_out_v qk_mm "
            "s_out low_ready max_ready p_ready pt_mm pt_out_v pt_out_a pv_mm inv_ready o_out o_stored").split())
    in_head = "(n p) d -> p n d"
    HALF = NBK // 2

    with nc.Block() as block:

        @block.sync
        def _(sp):
            sp.dma_start(f[:], io["logf_p"].rearrange("(n p) h -> p n h", p=P)).then_inc(f_loaded, 16)
            with sp.Fori(0, FH) as h:
                cols = bass.ds(h * FD, FD)
                sp.wait_ge(prep_mm, 2 * NG * h + 1)
                sp.dma_start(ktok[:, :, 0:FD], io["k_p"][:, cols].rearrange(in_head, p=P)).then_inc(kq_loaded, 16)
                sp.dma_start(qtok[:, :, 0:FD], io["q_tok"][0:SEQ, cols].rearrange(in_head, p=P)) \
                    .then_inc(kq_loaded, 16)
                sp.wait_ge(pv_mm, NBK * h + 1)
                sp.dma_start(v[:], io["v_p"][:, cols].rearrange(in_head, p=P)).then_inc(v_loaded, 16)

        @block.tensor
        def _(pe):
            pe.sem_inc(prep_mm, 1)
            pe.sem_inc(pv_mm, 1)
            pe.wait_ge(f_loaded, 16)
            pe.wait_ge(f_step, NB)
            pe.matmul(bank[:, 0, 0:NB * FH], c["tri"][:], f[:].rearrange("p n h -> p (n h)"), start=True, stop=False)
            pe.matmul(bank[:, 0, 0:NB * FH], c["ones"][:], before[:].rearrange("p n h -> p (n h)"),
                      start=False, stop=True).then_inc(c_mm, 1)
            with pe.Fori(0, FH) as h:
                pe.wait_ge(kq_loaded, 32 * h + 32)
                pe.wait_ge(aug_ready, 2 * h + 2)
                pe.wait_ge(s_out, NBK * h + 1)
                pe.wait_ge(pt_out_a, HALF * h + 1)
                pe.wait_ge(o_out, NB * h + 1)
                for g in range(2 * NG):
                    src = ktok if g < NG else qtok
                    for b in range(GB):
                        mm = pe.transpose(bank[0:A, g, b * P:(b + 1) * P], src[:, (g % NG) * GB + b, :], c["ident"][:])
                    mm.then_inc(prep_mm, 1)
                pe.wait_ge(prep_out_a, NG * h + NG)
                pe.wait_ge(prep_out_v, NG * h + NG)
                pe.wait_ge(v_loaded, 16 * h + 16)

                def logit_banks(n):
                    for j in range(banks_of[n]):
                        r = first[n] + j
                        width = min(GB, n + 1 - j * GB) * P
                        diagonal = j == banks_of[n] - 1
                        if r >= 4:
                            pe.wait_ge(s_out, NBK * h + (r - 4 + 2))
                        mm = pe.matmul(bank[:, r % 4, 0:width], qT[:, n * P:(n + 1) * P],
                                       kT[:, j * GB * P:j * GB * P + width], start=True, stop=not diagonal)
                        if diagonal:
                            mm = pe.matmul(bank[:, r % 4, width - P:width], c["ident"][:], c["causal"][:],
                                           start=False, stop=True)
                        mm.then_inc(qk_mm, 1)

                def turn(n, j):
                    r = first[n] + j
                    if r >= 2:
                        out = pt_out_v if r % 2 == 0 else pt_out_a
                        pe.wait_ge(out, HALF * h + ((r - 2) // 2 + 2))
                    for b in range(min(GB, n + 1 - j * GB)):
                        at = (j * GB + b) * P
                        mm = pe.transpose(bank[:, 4 + r % 2, b * P:(b + 1) * P], logits[:, n % 3, at:at + P],
                                          c["ident"][:])
                    mm.then_inc(pt_mm, 1)

                def meet_v(n, j):
                    r = first[n] + j
                    pe.wait_ge(pt_out_v if r % 2 == 0 else pt_out_a, HALF * h + (r // 2 + 2))
                    for b in range(min(GB, n + 1 - j * GB)):
                        blk = j * GB + b
                        mm = pe.matmul(bank[:, 6 + n % 2, 0:FD], pT[:, r % 2, b, :], v[:, blk, :],
                                       start=(blk == 0), stop=(blk == n))
                    mm.then_inc(pv_mm, 1)

                for n in range(NB + 2):
                    if n < NB:
                        logit_banks(n)
                    if n >= 2:
                        m = n - 2
                        pe.wait_ge(p_ready, NB * h + (m + 1))
                        if m >= 2:
                            pe.wait_ge(o_out, NB * h + (m - 2 + 2))
                        for j in range(banks_of[m]):
                            turn(m, j)
                            if j >= 1:
                                meet_v(m, j - 1)
                        meet_v(m, banks_of[m] - 1)

        @block.scalar
        def _(act):
            act.sem_inc(pt_out_a, 1)
            with act.Fori(0, FH) as h:
                for g in range(NG):
                    act.wait_ge(prep_mm, 2 * NG * h + (g + 2))
                    nc.scalar.copy(kT[:, g * BANK:(g + 1) * BANK], bank[0:A, g, :]).then_inc(prep_out_a, 1)
                for n in range(NB + 2):
                    if n >= 2:
                        m = n - 2
                        for j in range(banks_of[m]):
                            r = first[m] + j
                            if r % 2:
                                width = min(GB, m + 1 - j * GB)
                                act.wait_ge(pt_mm, NBK * h + (r + 1))
                                if r >= 2:
                                    act.wait_ge(pv_mm, NBK * h + (r - 2 + 2))
                                nc.scalar.copy(pT[:, 1, 0:width, :],
                                               bank[:, 5, 0:width * P].rearrange("p (b k) -> p b k", k=P)) \
                                    .then_inc(pt_out_a, 1)
                    if n < NB:
                        L = (n + 1) * P
                        act.wait_ge(max_ready, NB * h + (n + 1))
                        nc.scalar.activation(logits[:, n % 3, 0:L], logits[:, n % 3, 0:L], ACT.Exp, scale=-1.0,
                                             bias=neg_max[:, n % 3:n % 3 + 1],
                                             accum_out=row_sum[:, n % 3:n % 3 + 1]).then_inc(p_ready, 1)
                act.wait_ge(o_out, NB * h + (NB + 1))
                act.dma_start(io["mix_tok"][0:SEQ, bass.ds(h * FD, FD)].rearrange(in_head, p=P), o[:]) \
                    .then_inc(o_stored, 16)
            act.wait_ge(o_stored, 16 * (FH + 1))

        @block.vector
        def _(dve):
            dve.sem_inc(s_out, 1)
            dve.sem_inc(pt_out_v, 1)
            dve.sem_inc(o_out, 1)
            dve.sem_inc(o_stored, 16)
            nc.vector.memset(ktok[:, :, FD:FD + 1], 1.0)
            nc.vector.memset(qtok[:, :, FD + 1:A], 1.0)
            nc.vector.memset(qscale[:], float(FD) ** -0.5)
            nc.vector.memset(before[:, 0, :], 0.0).then_inc(f_step, 1)
            dve.wait_ge(f_loaded, 16)
            for n in range(1, NB):
                dve.wait_ge(f_step, n)
                nc.vector.tensor_tensor(before[:, n, :], before[:, n - 1, :], f[:, n - 1, :], ALU.add) \
                    .then_inc(f_step, 1)
            nc.vector.memset(qscale[FD:A], 1.0).then_inc(f_step, 1)
            dve.wait_ge(c_mm, 1)
            nc.vector.tensor_copy(csum[:].rearrange("p n h -> p (n h)"), bank[:, 0, 0:NB * FH]).then_inc(c_ready, 1)
            dve.wait_ge(c_ready, 1)
            dve.wait_ge(f_step, NB + 1)
            with dve.Fori(0, FH) as h:
                hc = bass.ds(h, 1)
                dve.wait_ge(prep_mm, 2 * NG * h + 1)
                nc.vector.tensor_copy(qtok[:, :, FD:FD + 1], csum[:, :, hc]).then_inc(aug_ready, 1)
                nc.vector.tensor_scalar(ktok[:, :, FD + 1:A], csum[:, :, hc], -1.0, None, ALU.mult) \
                    .then_inc(aug_ready, 1)
                for g in range(NG):
                    dve.wait_ge(prep_mm, 2 * NG * h + (NG + g + 2))
                    nc.vector.tensor_scalar(qT[:, g * BANK:(g + 1) * BANK], bank[0:A, NG + g, :], qscale[:], None,
                                            ALU.mult).then_inc(prep_out_v, 1)
                for n in range(NB + 2):
                    if n < NB:
                        s = n % 3
                        for j in range(banks_of[n]):
                            r = first[n] + j
                            width = min(GB, n + 1 - j * GB) * P
                            dve.wait_ge(qk_mm, NBK * h + (r + 1))
                            if n >= 3 and j == 0:
                                dve.wait_ge(pt_mm, NBK * h + first[n - 2])
                            nc.vector.tensor_scalar(logits[:, s, j * BANK:j * BANK + width], bank[:, r % 4, 0:width],
                                                    -1.0, None, ALU.mult, ALU.min, accum_out=low[:, s, j:j + 1]) \
                                .then_inc(s_out, 1)
                        dve.wait_ge(s_out, NBK * h + (first[n] + banks_of[n] + 1))
                        nc.vector.tensor_reduce(neg_max[:, s:s + 1], low[:, s, 0:banks_of[n]], AX.X, ALU.min) \
                            .then_inc(max_ready, 1)
                    if n >= 2:
                        m = n - 2
                        for j in range(banks_of[m]):
                            r = first[m] + j
                            if r % 2 == 0:
                                width = min(GB, m + 1 - j * GB)
                                dve.wait_ge(pt_mm, NBK * h + (r + 1))
                                if r >= 2:
                                    dve.wait_ge(pv_mm, NBK * h + (r - 2 + 2))
                                nc.vector.tensor_copy(pT[:, 0, 0:width, :],
                                                      bank[:, 4, 0:width * P].rearrange("p (b k) -> p b k", k=P)) \
                                    .then_inc(pt_out_v, 1)
                        dve.wait_ge(p_ready, NB * h + (m + 1))
                        nc.vector.reciprocal(inv_sum[:, m % 3:m % 3 + 1], row_sum[:, m % 3:m % 3 + 1]) \
                            .then_inc(inv_ready, 1)
                        dve.wait_ge(inv_ready, NB * h + (m + 1))
                        dve.wait_ge(pv_mm, NBK * h + (first[m] + banks_of[m] + 1))
                        if m == 0:
                            dve.wait_ge(o_stored, 16 * h + 16)
                        nc.vector.tensor_scalar(o[:, m, :], bank[:, 6 + m % 2, 0:FD], inv_sum[:, m % 3:m % 3 + 1],
                                                None, ALU.mult).then_inc(o_out, 1)
    ph.close()


def fox_sample(nc, c, io, bank):
    ph = Phase(nc, "foxs")
    FH, FD, FW, DB, DS, PAST, SEQ = (c[k] for k in ("FH", "FD", "FW", "DB", "DS", "PAST", "SEQ"))
    NP = FW // P
    NK = PAST // P
    GB = 4
    NBK = (NK + GB - 1) // GB
    KW = [min(GB, NK - g * GB) for g in range(NBK)]
    ROWS = 2 * DS
    assert FW == NP * P and 2 * FD == P and NBK <= 2 and FH * DS == P

    k, v = ph.sb("k", [P, 2, NK, FW]), ph.sb("v", [P, 2, NK, FW])
    v_new = ph.sb("v_new", [DS, 2, FW])
    f = ph.sb("f", [P, 2, NK, FH])
    kT = ph.sb("kT", [P, NP, PAST])
    q_tok, k_tok, f_new = ph.sb("q_tok", [P, FW]), ph.sb("k_tok", [P, FW]), ph.sb("f_new", [P, FH])
    qT, kT_new = ph.sb("qT", [P, NP, P]), ph.sb("kT_new", [P, NP, P])
    q_heads = ph.sb("q_heads", [P, NP, P])
    f_after = ph.sb("f_after", [P, NK, FH])
    f_rows = ph.sb("f_rows", [P, FH, DS])
    f_all = ph.sb("f_all", [P, NK, FH, DS])
    f_key = ph.sb("f_key", [P, NK, FH, DS])
    logits = ph.sb("logits", [P, PAST + DS])
    low = ph.sb("low", [P, NBK + 1])
    neg_max, row_sum, inv_sum = (ph.sb(n, [P, 1]) for n in ("nmax", "rsum", "inv"))
    pT, pT_new = ph.sb("pT", [P, NK, P]), ph.sb("pT_new", [DS, P])
    head_rows = ph.sb("head_rows", [DS, P])
    oT, o = ph.sb("oT", [P, NP, P]), ph.sb("o", [P, FW])

    s = {n: ph.sem(n) for n in (
        "new_loaded new_turned new_ready kf_loaded0 kf_loaded1 v_loaded0 v_loaded1 q_ready f_step f_ready kt_mm kt_out_v "
        "kt_out_a s_mm s_out max_ready p_ready inv_ready pn_ready pt_mm pt_out pv_mm o_out o_turned o_ready o_stored"
    ).split()}

    with nc.Block() as block:

        @block.sync
        def _(sp):
            for dst, src in ((q_tok, io["q_tok"][SEQ:, :]), (k_tok, io["k_s"]), (f_new, io["logf_s"])):
                sp.dma_start(dst[:], src).then_inc(s["new_loaded"], 16)
            ck = io["cache_fox_k"].rearrange("l b (n p) h d -> (l b) p n (h d)", p=P)
            cv = io["cache_fox_v"].rearrange("l b (n p) h d -> (l b) p n (h d)", p=P)
            cf = io["cache_fox_logf"].rearrange("l b (n p) h -> (l b) p n h", p=P)
            with sp.Fori(0, DB // 2) as i:
                for a in range(2):
                    b = 2 * i + a
                    sp.wait_ge(s["s_mm"], b + 1)
                    one = bass.ds(b, 1)
                    sp.dma_start(k[:, a], ck[one].rearrange("o p n d -> (o p) n d")).then_inc(s[f"kf_loaded{a}"], 16)
                    sp.dma_start(f[:, a], cf[one].rearrange("o p n h -> (o p) n h")).then_inc(s[f"kf_loaded{a}"], 16)
                    sp.wait_ge(s["pv_mm"], b + 1)
                    sp.dma_start(v[:, a], cv[one].rearrange("o p n d -> (o p) n d")).then_inc(s[f"v_loaded{a}"], 16)
                    sp.dma_start(v_new[:, a], io["v_s"][bass.ds(b * DS, DS), :]).then_inc(s[f"v_loaded{a}"], 16)
            sp.wait_ge(s["o_ready"], 1)
            sp.dma_start(io["mix_tok"][SEQ:, 0:FW], o[:]).then_inc(s["o_stored"], 16)
            sp.wait_ge(s["o_stored"], 16)

        @block.tensor
        def _(pe):
            pe.sem_inc(s["s_mm"], 2)
            pe.sem_inc(s["pv_mm"], 2)
            pe.wait_ge(s["new_loaded"], 48)
            for n, src in enumerate((q_tok, k_tok)):
                for p in range(NP):
                    mm = pe.transpose(bank[:, n, p * P:(p + 1) * P], src[:, p * P:(p + 1) * P], c["ident"][:])
                mm.then_inc(s["new_turned"], 1)
            pe.wait_ge(s["new_ready"], 4)
            with pe.Fori(0, DB // 2) as i:
                for a in range(2):
                    b = 2 * i + a
                    pe.wait_ge(s[f"kf_loaded{a}"], 32 * i + 32)
                    for n in range(NK):
                        out = "kt_out_v" if n % 2 == 0 else "kt_out_a"
                        pe.wait_ge(s[out], (NK // 2) * b + (n // 2 + 1))
                        for p in range(NP):
                            mm = pe.transpose(bank[:, n % 4, p * P:(p + 1) * P], k[:, a, n, p * P:(p + 1) * P],
                                              c["ident"][:])
                        mm.then_inc(s["kt_mm"], 1)
                    pe.wait_ge(s["kt_out_v"], (NK // 2) * b + (NK // 2 + 2))
                    pe.wait_ge(s["kt_out_a"], (NK // 2) * b + (NK // 2 + 2))
                    pe.wait_ge(s["q_ready"], 2 * b + 2)
                    pe.wait_ge(s["f_ready"], 2 * b + 2)
                    for g in range(NBK):
                        w = KW[g] * P
                        for p in range(NP):
                            pe.matmul(bank[:, 4 + g, 0:w], q_heads[:, p, :], kT[:, p, g * BANK:g * BANK + w],
                                      start=(p == 0), stop=False)
                        for n in range(g * GB, g * GB + KW[g]):
                            at = bank[:, 4 + g, (n % GB) * P:(n % GB + 1) * P]
                            pe.matmul(at, f_key[:, n].rearrange("p h q -> p (h q)"), c["after"][:],
                                      start=False, stop=False)
                            pe.matmul(at, f_all[:, n].rearrange("p h q -> p (h q)"), c["ones"][:],
                                      start=False, stop=(n == g * GB + KW[g] - 1))
                    new = bank[:, 6, 0:DS]
                    for p in range(NP):
                        pe.matmul(new, q_heads[:, p, :], kT_new[:, p, bass.ds(b * DS, DS)], start=(p == 0), stop=False)
                    pe.matmul(new, f_rows[:].rearrange("p h q -> p (h q)"), c["later_in_stream"][:],
                              start=False, stop=False)
                    pe.matmul(new, head_rows[:], c["causal_s"][0:DS, :], start=False, stop=True) \
                        .then_inc(s["s_mm"], 1)
                    pe.wait_ge(s["pn_ready"], b + 1)
                    for n in range(NK):
                        mm = pe.transpose(bank[:, n // GB, (n % GB) * P:(n % GB + 1) * P], logits[:, n * P:(n + 1) * P],
                                          c["ident"][:])
                    mm = pe.transpose(bank[0:DS, 2, 0:P], logits[:, PAST:], c["ident"][:])
                    mm.then_inc(s["pt_mm"], 1)
                    pe.wait_ge(s[f"v_loaded{a}"], 32 * i + 32)
                    pe.wait_ge(s["pt_out"], 2 * b + 2)
                    for p in range(NP):
                        at = bank[:, 7, p * ROWS:(p + 1) * ROWS]
                        rows = slice(p * ROWS, (p + 1) * ROWS)
                        for n in range(NK):
                            pe.matmul(at, v[:, a, n, p * P:(p + 1) * P], pT[:, n, rows], start=(n == 0), stop=False)
                        mm = pe.matmul(at, v_new[:, a, p * P:(p + 1) * P], pT_new[:, rows], start=False, stop=True)
                    mm.then_inc(s["pv_mm"], 1)
            pe.wait_ge(s["o_out"], 2 * DB)
            for p in range(NP):
                mm = pe.transpose(bank[:, 0, p * P:(p + 1) * P], oT[:, p, :], c["ident"][:])
            mm.then_inc(s["o_turned"], 1)

        @block.scalar
        def _(act):
            act.sem_inc(s["kt_out_a"], 2)
            with act.Fori(0, DB // 2) as i:
                for a in range(2):
                    b = 2 * i + a
                    for n in range(1, NK, 2):
                        act.wait_ge(s["kt_mm"], NK * b + (n + 1))
                        nc.scalar.copy(kT[:, :, n * P:(n + 1) * P], bank[:, n % 4, :].rearrange("p (c t) -> p c t", t=P)) \
                            .then_inc(s["kt_out_a"], 1)
                    act.wait_ge(s["max_ready"], b + 1)
                    nc.scalar.activation(logits[:], logits[:], ACT.Exp, scale=-1.0, bias=neg_max[:],
                                         accum_out=row_sum[:]).then_inc(s["p_ready"], 1)

        @block.vector
        def _(dve):
            tt, cp = nc.vector.tensor_tensor, nc.vector.tensor_copy
            dve.sem_inc(s["kt_out_v"], 2)
            nc.vector.memset(q_heads[:], 0.0).then_inc(s["new_ready"], 1)
            dve.wait_ge(s["new_turned"], 1)
            nc.vector.tensor_scalar(qT[:], bank[:, 0, :].rearrange("p (c t) -> p c t", t=P), float(FD) ** -0.5, None,
                                    ALU.mult).then_inc(s["new_ready"], 1)
            dve.wait_ge(s["new_turned"], 2)
            cp(kT_new[:], bank[:, 1, :].rearrange("p (c t) -> p c t", t=P)).then_inc(s["new_ready"], 1)
            cp(head_rows[:].rearrange("q (h r) -> q h r", r=DS), spread(c["ident"][0:DS, 0:DS].unsqueeze(1),
                                                                      [DS, FH, DS])).then_inc(s["new_ready"], 1)
            dve.wait_ge(s["new_ready"], 4)
            dve.wait_ge(s["new_loaded"], 48)
            with dve.Fori(0, DB // 2) as i:
                for a in range(2):
                    b = 2 * i + a
                    dve.wait_ge(s["s_mm"], b + 2)
                    for e in range(2):
                        rows = q_heads[e * FD:(e + 1) * FD]
                        dst = bass.AP(tensor=rows.tensor, offset=rows.offset + e * DS,
                                      ap=[list(rows.ap[0]), [P + 2 * DS, NP], [1, DS]])
                        cp(dst, qT[e * FD:(e + 1) * FD, :, bass.ds(b * DS, DS)]).then_inc(s["q_ready"], 1)
                    dve.wait_ge(s[f"kf_loaded{a}"], 32 * i + 32)
                    nc.vector.memset(f_after[:, NK - 1, :], 0.0).then_inc(s["f_step"], 1)
                    for n in range(NK - 2, -1, -1):
                        dve.wait_ge(s["f_step"], (NK + 1) * b + (NK - 1 - n))
                        tt(f_after[:, n, :], f_after[:, n + 1, :], f[:, a, n + 1, :], ALU.add).then_inc(s["f_step"], 1)
                    tt(f_rows[:], spread(f_new[:].unsqueeze(2), [P, FH, DS]),
                       spread(c["before_q"][:, bass.ds(b, 1), :], [P, FH, DS]), ALU.mult).then_inc(s["f_step"], 1)
                    cp(f_key[:], spread(f[:, a].unsqueeze(3), [P, NK, FH, DS])).then_inc(s["f_ready"], 1)
                    dve.wait_ge(s["f_step"], (NK + 1) * b + (NK + 1))
                    tt(f_all[:], spread(f_after[:].unsqueeze(3), [P, NK, FH, DS]),
                       spread(f_rows[:].unsqueeze(1), [P, NK, FH, DS]), ALU.add).then_inc(s["f_ready"], 1)
                    for n in range(0, NK, 2):
                        dve.wait_ge(s["kt_mm"], NK * b + (n + 1))
                        cp(kT[:, :, n * P:(n + 1) * P], bank[:, n % 4, :].rearrange("p (c t) -> p c t", t=P)) \
                            .then_inc(s["kt_out_v"], 1)
                    dve.wait_ge(s["s_mm"], b + 3)
                    pieces = [(4 + g, g * BANK, KW[g] * P) for g in range(NBK)] + [(6, PAST, DS)]
                    for n, (bk, at, w) in enumerate(pieces):
                        nc.vector.tensor_scalar(logits[:, at:at + w], bank[:, bk, 0:w], -1.0, None, ALU.mult, ALU.min,
                                                accum_out=low[:, n:n + 1]).then_inc(s["s_out"], 1)
                    dve.wait_ge(s["s_out"], (NBK + 1) * b + (NBK + 1))
                    nc.vector.tensor_reduce(neg_max[:], low[:], AX.X, ALU.min).then_inc(s["max_ready"], 1)
                    dve.wait_ge(s["p_ready"], b + 1)
                    nc.vector.reciprocal(inv_sum[:], row_sum[:]).then_inc(s["inv_ready"], 1)
                    dve.wait_ge(s["inv_ready"], b + 1)
                    nc.vector.tensor_scalar(logits[:], logits[:], inv_sum[:], None, ALU.mult) \
                        .then_inc(s["pn_ready"], 1)
                    dve.wait_ge(s["pt_mm"], b + 1)
                    for g in range(NBK):
                        last = cp(pT[:, g * GB:g * GB + KW[g], :],
                                  bank[:, g, 0:KW[g] * P].rearrange("p (b k) -> p b k", k=P))
                    last.then_inc(s["pt_out"], 1)
                    cp(pT_new[:], bank[0:DS, 2, 0:P]).then_inc(s["pt_out"], 1)
                    dve.wait_ge(s["pv_mm"], b + 3)
                    for e in range(2):
                        src = bank[e * FD:(e + 1) * FD, 7, 0:NP * ROWS].rearrange("p (c t) -> p c t", t=ROWS)
                        cp(oT[e * FD:(e + 1) * FD, :, bass.ds(b * DS, DS)], src[:, :, e * DS:(e + 1) * DS]) \
                            .then_inc(s["o_out"], 1)
            dve.wait_ge(s["o_turned"], 1)
            cp(o[:], bank[:, 0, :]).then_inc(s["o_ready"], 1)
    ph.close()


def mix(nc, c, io, bank):
    ph = Phase(nc, "mix")
    D, SEQ, NT = c["D"], c["SEQ"], c["NT"]
    M = c["FW"] + c["GW"]
    KD, KM, HB = D // P, M // P, BANK // P
    ND = D // BANK
    assert KM == 2 * HB and KD == 2 * HB and ND == 2

    w = ph.sb("w", [P, KM, D])
    m_tok, x, h, hn, squares = (ph.sb(n, [P, D]) for n in ("m_tok", "x", "h", "hn", "squares"))
    mT, hT = ph.sb("mT", [P, KM, P]), ph.sb("hT", [P, KD, P])
    norm_rows, norm_w = ph.sb("norm_rows", [KD, P]), ph.sb("norm_w", [P, KD])
    ss, ln_ms, rs = (ph.sb(n, [P, 1]) for n in ("ss", "ln_ms", "rs"))
    (w_loaded, small_loaded, small_turned, small_ready, m_loaded, x_loaded, in_mm, in_out_a, in_out_v, prod_mm, h_ready,
     squared, ln_done, rs_ready, hn_ready, out_mm, hT_ready, h_stored, hT_stored) = (ph.sem(n) for n in (
         "w_loaded small_loaded small_turned small_ready m_loaded x_loaded in_mm in_out_a in_out_v prod_mm h_ready "
         "squared ln_done rs_ready hn_ready out_mm hT_ready h_stored hT_stored").split())

    def rows(t):
        return bass.ds(t * P, P)

    with nc.Block() as block:

        @block.sync
        def _(sp):
            def load_m(t):
                sp.dma_start(m_tok[:], io["mix_tok"][rows(t), :]).then_inc(m_loaded, 16)

            def load_x(t):
                sp.dma_start(x[:], io["x_s"] if t is None else io["x_p"][rows(t), :]).then_inc(x_loaded, 16)

            load_m(0)
            sp.dma_start(norm_rows[:], io["norm_ffn_w"].rearrange("l (k p) -> (l k) p", p=P)).then_inc(small_loaded, 16)
            sp.dma_start(w[:], io["w_o"][0].rearrange("(k p) n -> p k n", p=P)).then_inc(w_loaded, 16)
            load_x(0)

            def behind(t):
                sp.wait_ge(in_mm, 2 * t)
                load_m(t)
                sp.wait_ge(h_ready, 2 * t + 2)

            with sp.Fori(1, NT - 1) as t:
                behind(t)
                load_x(t)
            behind(NT - 1)
            load_x(None)

        @block.tensor
        def _(pe):
            def products(t):
                pe.wait_ge(m_loaded, 16 * t + 16)
                for n, out in enumerate((in_out_a, in_out_v)):
                    pe.wait_ge(out, t + 1)
                    for k in range(HB):
                        mm = pe.transpose(bank[:, n, k * P:(k + 1) * P], m_tok[:, (n * HB + k) * P:(n * HB + k + 1) * P],
                                          c["ident"][:])
                    mm.then_inc(in_mm, 1)
                pe.wait_ge(in_out_a, t + 2)
                pe.wait_ge(in_out_v, t + 2)
                pe.wait_ge(h_ready, 2 * t + 2)
                for n in range(ND):
                    for k in range(KM):
                        mm = pe.matmul(bank[:, 2 + n, :], mT[:, k, :], w[:, k, n * BANK:(n + 1) * BANK],
                                       start=(k == 0), stop=(k == KM - 1))
                    mm.then_inc(prod_mm, 1)

            def turn_out(t):
                pe.wait_ge(hn_ready, t + 1)
                for n in range(2):
                    pe.wait_ge(hT_ready, 2 * t + (n + 1))
                    for k in range(HB):
                        mm = pe.transpose(bank[:, 4 + n, k * P:(k + 1) * P],
                                          hn[:, (n * HB + k) * P:(n * HB + k + 1) * P], c["ident"][:])
                    mm.then_inc(out_mm, 1)

            pe.wait_ge(small_loaded, 16)
            pe.transpose(bank[:, 6, 0:KD], norm_rows[:], c["ident"][0:KD, 0:KD]).then_inc(small_turned, 1)
            pe.wait_ge(w_loaded, 16)
            products(0)
            with pe.Fori(1, NT) as t:
                products(t)
                turn_out(t - 1)
            turn_out(NT - 1)

        @block.scalar
        def _(act):
            def norm_factor(t):
                act.wait_ge(h_ready, 2 * t + 4)
                act.dma_start(io["h_tok"][rows(t), :], h[:]).then_inc(h_stored, 16)
                nc.scalar.activation(squares[:], h[:], ACT.Square, accum_out=ss[:]).then_inc(squared, 1)
                act.wait_ge(squared, t + 1)
                nc.scalar.activation(ln_ms[:], ss[:], ACT.Ln, scale=1.0 / D, bias=c["eps"][:]).then_inc(ln_done, 1)
                act.wait_ge(ln_done, t + 1)
                nc.scalar.activation(rs[:], ln_ms[:], ACT.Exp, scale=-0.5).then_inc(rs_ready, 1)

            def copy_in(t):
                act.wait_ge(in_mm, 2 * t + 1)
                nc.scalar.copy(mT[:, 0:HB, :], bank[:, 0, :].rearrange("p (k t) -> p k t", t=P)).then_inc(in_out_a, 1)

            def store_out(t):
                act.wait_ge(hT_ready, 2 * t + 4)
                act.dma_start(io["hnT"][:, rows(t)].rearrange("(k p) t -> p k t", p=P), hT[:]).then_inc(hT_stored, 16)

            act.sem_inc(in_out_a, 1)
            copy_in(0)
            norm_factor(0)
            with act.Fori(1, NT) as t:
                copy_in(t)
                norm_factor(t)
                store_out(t - 1)
            store_out(NT - 1)
            act.wait_ge(h_stored, 16 * (NT + 1))
            act.wait_ge(hT_stored, 16 * (NT + 1))

        @block.vector
        def _(dve):
            def copy_in(t):
                dve.wait_ge(in_mm, 2 * t + 2)
                nc.vector.tensor_copy(mT[:, HB:, :], bank[:, 1, :].rearrange("p (k t) -> p k t", t=P)) \
                    .then_inc(in_out_v, 1)

            def add_x(t):
                dve.wait_ge(x_loaded, 16 * t + 16)
                dve.wait_ge(h_stored, 16 * t + 16)
                for n in range(ND):
                    dve.wait_ge(prod_mm, 2 * t + (n + 1))
                    nc.vector.tensor_tensor(h[:, n * BANK:(n + 1) * BANK], bank[:, 2 + n, :],
                                            x[:, n * BANK:(n + 1) * BANK], ALU.add).then_inc(h_ready, 1)

            def normalise(t):
                dve.wait_ge(rs_ready, t + 1)
                nc.vector.tensor_scalar(hn[:], h[:], rs[:], None, ALU.mult).then_inc(hn_ready, 1)

            def weigh_out(t):
                dve.wait_ge(hT_stored, 16 * t + 16)
                for n in range(2):
                    dve.wait_ge(out_mm, 2 * t + (n + 1))
                    nc.vector.tensor_tensor(hT[:, n * HB:(n + 1) * HB, :],
                                            bank[:, 4 + n, :].rearrange("p (k t) -> p k t", t=P),
                                            spread(norm_w[:, n * HB:(n + 1) * HB].unsqueeze(2), [P, HB, P]), ALU.mult) \
                        .then_inc(hT_ready, 1)

            dve.sem_inc(in_out_v, 1)
            dve.sem_inc(h_ready, 2)
            dve.sem_inc(hT_ready, 2)
            dve.sem_inc(h_stored, 16)
            dve.sem_inc(hT_stored, 16)
            dve.wait_ge(small_turned, 1)
            nc.vector.tensor_copy(norm_w[:], bank[:, 6, 0:KD]).then_inc(small_ready, 1)
            dve.wait_ge(small_ready, 1)
            copy_in(0)
            add_x(0)
            normalise(0)
            with dve.Fori(1, NT) as t:
                copy_in(t)
                add_x(t)
                weigh_out(t - 1)
                normalise(t)
            weigh_out(NT - 1)
    ph.close()


def ffn(nc, c, io, bank):
    ph = Phase(nc, "ffn")
    D, F2, FC, DB, DS, SEQ = (c[k] for k in ("D", "F2", "FC", "DB", "DS", "SEQ"))
    KD, NF2, H2, HB = D // P, F2 // P, FC - 1, BANK // P
    NF = NF2 // 2
    WP = SEQ // 2
    WG = WP + P
    prompt_chunks = [(n * BANK, BANK, False) for n in range(WP // BANK)]
    chunks = [prompt_chunks, prompt_chunks + [(WP, P, True)]]
    tiles = [WP // P, WG // P]
    assert NF % 2 == 0 and WP % BANK == 0 and KD % 2 == 0 and F2 <= NF * WG // 2

    hnT = ph.sb("hnT", [P, KD, WG])
    gT = ph.sb("gT", [P, NF, WG])
    w_up = ph.sb("w_up", [P, 2, 2, KD, P])
    w_down = ph.sb("w_down", [P, 2, NF, P])
    raw = ph.sb("raw", [P, 2, 2, H2 + BANK])
    acc = ph.sb("acc", [P, 2, 2, BANK])
    hist, hist_s = ph.sb("hist", [P, NF2, H2]), ph.sb("hist_s", [P, NF2, DB * H2])
    vecs = ph.sb("vecs", [P, 4, NF2])
    norm_w = ph.sb("norm_w", [P, D])
    ss, ln_ms, rs = (ph.sb(n, [P, 2]) for n in ("ss", "ln_ms", "rs"))
    flat_g = gT[:].rearrange("p f t -> p (f t)")
    rows_s, rows_p = flat_g[0:DB * H2, 0:F2], flat_g[0:H2, F2:2 * F2]
    vec_rows = raw[:].rearrange("p a b n -> p (a b n)")[0:2 * NF2, 0:2 * P].rearrange("r (a p) -> r a p", p=P)
    tile4 = w_up[:].rearrange("p a b k n -> p (a b k n)").rearrange("p (x n) -> p x n", n=D)
    h_in, y = tile4[:, 0:2], tile4[:, 2:4]
    squares = acc[:].rearrange("p a b n -> p (a b n)")[:, 0:D]

    s = {n: ph.sem(n) for n in (
        "small_loaded rows_loaded setup_turned setup_ready norm_loaded hnT_loaded up0_loaded up1_loaded up_mm "
        "raw_ready conv_step conv_done silu_ready g_ready down0_loaded down1_loaded down_mm y_out "
        "h0_loaded h1_loaded y_turned y_read r_ready squared ln_done rs_ready yn_ready y_stored0 y_stored1 "
        "tail_turned tail_read tail_stored").split()}
    units = [2 * len(chunks[0]), 2 * len(chunks[1])]
    unit0 = [0, NF * units[0]]
    down0 = [0, KD * len(chunks[0])]
    tile0 = [0, tiles[0]]
    CREDIT = 2 * units[1]
    UPC, DOWNC = 2 * units[0], 2 * len(chunks[0])

    wu = io["w_up"][0].rearrange("(k p) (e f n) -> p e f k n", p=P, e=2, n=P)
    wd = io["w_down"][0].rearrange("(f p) (d n) -> p d f n", p=P, n=P)

    def each_f(eng, g, body):
        with eng.Fori(0, NF // 2) as i:
            for a in range(2):
                body(2 * i + a, g * NF + 2 * i + a, a, g * (NF // 2) + i)

    def each_chunk(g, a, f):
        for n, ch in enumerate(chunks[g]):
            yield n, ch, unit0[g] + units[g] * f + 2 * n, (a * len(chunks[g]) + n) % 2

    def chunk_no(g, f, n):
        return unit0[g] // 2 + len(chunks[g]) * f + n

    def chan(e, f):
        return e * NF + f

    with nc.Block() as block:

        @block.sync
        def _(sp):
            sp.dma_start(vec_rows[:, 0, :], io["ffn_conv_w"][:, 0:2].rearrange("l i (k p) -> (l i k) p", p=P)) \
                .then_inc(s["small_loaded"], 16)
            sp.dma_start(vec_rows[0:NF2, 1, :], io["ffn_conv_w"][:, 2:3].rearrange("l i (k p) -> (l i k) p", p=P)) \
                .then_inc(s["small_loaded"], 16)
            sp.dma_start(vec_rows[NF2:, 1, :], io["ffn_conv_b"].rearrange("l (k p) -> (l k) p", p=P)) \
                .then_inc(s["small_loaded"], 16)
            sp.dma_start(rows_s, io["ffn_state"]).then_inc(s["rows_loaded"], 16)
            for g in range(2):
                if g == 1:
                    sp.wait_ge(s["y_turned"], 2 * tile0[1])
                width = WG if g else WP
                sp.dma_start(hnT[:, :, 0:width],
                             io["hnT"][:, g * WP:g * WP + width].rearrange("(k p) t -> p k t", p=P)) \
                    .then_inc(s["hnT_loaded"], 16)
                if g == 0:
                    sp.dma_start(norm_w[:], io["norm_final_w"].partition_broadcast(P)).then_inc(s["norm_loaded"], 16)
                else:
                    sp.wait_ge(s["yn_ready"], tile0[1])
                    for a in range(2):
                        sp.wait_ge(s[f"y_stored{a}"], 16 * (tile0[1] // 2))

                def load_up(f, F, a, half):
                    sp.wait_ge(s["up_mm"], unit0[g] - units[g] + UPC + units[g] * f)
                    for e in range(2):
                        sp.dma_start(w_up[:, a, e], wu[:, e, bass.ds(f, 1)].rearrange("p o k n -> p (o k) n")) \
                            .then_inc(s[f"up{a}_loaded"], 16)

                each_f(sp, g, load_up)
                if g == 1:
                    sp.wait_ge(s["down_mm"], down0[1] + DOWNC)
                with sp.Fori(0, KD // 2) as i:
                    for a in range(2):
                        sp.wait_ge(s["down_mm"], down0[g] - len(chunks[g]) + DOWNC + len(chunks[g]) * (2 * i + a))
                        sp.dma_start(w_down[:, a], wd[:, bass.ds(2 * i + a, 1)].rearrange("p o f n -> p (o f) n")) \
                            .then_inc(s[f"down{a}_loaded"], 16)
                for t in range(tiles[g]):
                    a, T = t % 2, tile0[g] + t
                    if t < 2:
                        sp.wait_ge(s["up_mm"], unit0[g] + NF * units[g] + UPC)
                    else:
                        sp.wait_ge(s["r_ready"], 2 * (T - 1))
                    if t < 2 and g == 1:
                        sp.wait_ge(s["r_ready"], 2 * T)
                    sp.dma_start(h_in[:, a], io["h_tok"][g * WP + t * P:g * WP + (t + 1) * P, :]) \
                        .then_inc(s[f"h{a}_loaded"], 16)

        @block.tensor
        def _(pe):
            pe.sem_inc(s["up_mm"], UPC)
            pe.sem_inc(s["down_mm"], DOWNC)
            pe.wait_ge(s["small_loaded"], 48)
            pe.wait_ge(s["rows_loaded"], 16)
            for n in range(2):
                pe.transpose(bank[:, 0, n * 2 * NF2:(n + 1) * 2 * NF2], vec_rows[:, n, :],
                             c["ident"][0:2 * NF2, 0:2 * NF2])
            R = DB * H2
            for n in range(NF2):
                mm = pe.transpose(bank[:, 1 + n * R // BANK, n * R % BANK:n * R % BANK + R],
                                  rows_s[:, n * P:(n + 1) * P], c["ident"][0:R, 0:R])
            mm.then_inc(s["setup_turned"], 1)
            pe.wait_ge(s["setup_ready"], 3)
            for g in range(2):
                pe.wait_ge(s["hnT_loaded"], 16 * (g + 1))
                if g == 1:
                    pe.wait_ge(s["y_read"], 2 * tile0[1] + 2)

                def up(f, F, a, half):
                    pe.wait_ge(s[f"up{a}_loaded"], 32 * half + 32)
                    for n, (col, width, _), unit, _ in each_chunk(g, a, f):
                        for e in range(2):
                            pe.wait_ge(s["raw_ready"], 2 * unit + (2 * e + CREDIT - 2 * units[g] + 2))
                            for k in range(KD):
                                mm = pe.matmul(bank[:, 2 * n + e, 0:width], w_up[:, a, e, k, :],
                                               hnT[:, k, col:col + width], start=(k == 0), stop=(k == KD - 1))
                            mm.then_inc(s["up_mm"], 1)

                each_f(pe, g, up)
                pe.wait_ge(s["g_ready"], (unit0[g] + NF * units[g]) // 2 + 2)
                with pe.Fori(0, KD // 2) as i:
                    for a in range(2):
                        pe.wait_ge(s[f"down{a}_loaded"], 16 * (g * (KD // 2)) + 16 * i + 16)
                        for n, (col, width, _) in enumerate(chunks[g]):
                            N = (2 * i + a) * len(chunks[g]) + (down0[g] + n)
                            odd = (a * len(chunks[g]) + n + down0[g]) % 2
                            pe.wait_ge(s["y_out"], N + 1)
                            for f in range(NF):
                                mm = pe.matmul(bank[:, 6 + odd, 0:width], w_down[:, a, f, :], gT[:, f, col:col + width],
                                               start=(f == 0), stop=(f == NF - 1))
                            mm.then_inc(s["down_mm"], 1)
                pe.wait_ge(s["y_out"], down0[g] + KD * len(chunks[g]) + 2)
                for t in range(tiles[g]):
                    T = tile0[g] + t
                    for n in range(2):
                        pe.wait_ge(s["y_read"], 2 * T + n + 1)
                        for k in range(HB):
                            mm = pe.transpose(bank[:, n, k * P:(k + 1) * P],
                                              hnT[:, n * HB + k, t * P:(t + 1) * P], c["ident"][:])
                        mm.then_inc(s["y_turned"], 1)
            for q in range(NF2 // 4):
                if q >= 3:
                    pe.wait_ge(s["tail_read"], 2 * (q - 2))
                b = 2 + 2 * (q % 3)
                for n in range(4):
                    pe.transpose(bank[0:R, b, n * P:(n + 1) * P], hist_s[:, 4 * q + n, :], c["ident"][:])
                    mm = pe.transpose(bank[0:H2, b + 1, n * P:(n + 1) * P], hist[:, 4 * q + n, :], c["ident"][:])
                mm.then_inc(s["tail_turned"], 1)

        @block.scalar
        def _(act):
            act.sem_inc(s["raw_ready"], CREDIT)
            act.wait_ge(s["setup_ready"], 3)
            for g in range(2):

                def convs(f, F, a, half):
                    for n, (col, width, streams), unit, slot in each_chunk(g, a, f):
                        act.wait_ge(s["g_ready"], chunk_no(g, f, n) + 1)
                        for e in range(2):
                            act.wait_ge(s["up_mm"], unit + (e + 1 + UPC))
                            act.wait_ge(s["conv_done"], unit + (e + 1))
                            src = bank[:, 2 * n + e, 0:width]
                            if streams:
                                nc.scalar.copy(
                                    raw[:, slot, e, 0:DB * (H2 + DS)].rearrange("p (b r) -> p b r", b=DB)[:, :, H2:],
                                    src.rearrange("p (b r) -> p b r", b=DB)).then_inc(s["raw_ready"], 1)
                            else:
                                nc.scalar.copy(raw[:, slot, e, H2:], src).then_inc(s["raw_ready"], 1)
                            at = bass.ds(chan(e, f), 1)
                            nc.scalar.activation(acc[:, slot, e, 0:width], src, ACT.Identity,
                                                 scale=vecs[:, 2, at], bias=vecs[:, 3, at]).then_inc(s["raw_ready"], 1)
                        act.wait_ge(s["conv_done"], unit + 5)
                        nc.scalar.activation(acc[:, slot, 0, 0:width], acc[:, slot, 0, 0:width], ACT.Silu) \
                            .then_inc(s["silu_ready"], 1)

                each_f(act, g, convs)
                for t in range(tiles[g]):
                    T, a = tile0[g] + t, t % 2
                    act.wait_ge(s["r_ready"], 2 * T + 2)
                    nc.scalar.activation(squares, y[:, a], ACT.Square, accum_out=ss[:, a:a + 1]) \
                        .then_inc(s["squared"], 1)
                    act.wait_ge(s["squared"], T + 1)
                    nc.scalar.activation(ln_ms[:, a:a + 1], ss[:, a:a + 1], ACT.Ln, scale=1.0 / D, bias=c["eps"][:]) \
                        .then_inc(s["ln_done"], 1)
                    act.wait_ge(s["ln_done"], T + 1)
                    nc.scalar.activation(rs[:, a:a + 1], ln_ms[:, a:a + 1], ACT.Exp, scale=-0.5) \
                        .then_inc(s["rs_ready"], 1)
                    act.wait_ge(s["yn_ready"], T + 1)
                    row = g * WP + t * P
                    dst = io["y_s"] if row == SEQ else io["y_p"][row:row + P, :]
                    act.dma_start(dst, y[:, a]).then_inc(s[f"y_stored{a}"], 16)
            act.wait_ge(s["tail_read"], 2 * (NF2 // 4))
            act.dma_start(io["ffn_s"], rows_s).then_inc(s["tail_stored"], 16)
            act.dma_start(io["ffn_p"], rows_p).then_inc(s["tail_stored"], 16)
            act.wait_ge(s["tail_stored"], 32)
            for a in range(2):
                act.wait_ge(s[f"y_stored{a}"], 16 * sum((n + 1 - a) // 2 for n in tiles))

        @block.vector
        def _(dve):
            cp, stt = nc.vector.tensor_copy, nc.vector.scalar_tensor_tensor

            def move(dst, src):
                return nc.vector.tensor_scalar(dst, src, 1.0, None, ALU.mult)

            dve.sem_inc(s["conv_done"], 4)
            dve.sem_inc(s["g_ready"], 2)
            dve.sem_inc(s["y_out"], 2)
            dve.sem_inc(s["y_read"], 2)
            nc.vector.memset(hist[:], 0.0).then_inc(s["setup_ready"], 1)
            dve.wait_ge(s["setup_turned"], 1)
            cp(vecs[:].rearrange("p a n -> p (a n)"), bank[:, 0, 0:4 * NF2]).then_inc(s["setup_ready"], 1)
            R = DB * H2
            flat = hist_s[:].rearrange("p n r -> p (n r)")
            for n in range((NF2 * R + BANK - 1) // BANK):
                width = min(BANK, NF2 * R - n * BANK)
                last = cp(flat[:, n * BANK:n * BANK + width], bank[:, 1 + n, 0:width])
            last.then_inc(s["setup_ready"], 1)
            dve.wait_ge(s["setup_ready"], 3)
            for g in range(2):

                def convs(f, F, a, half):
                    for n, (col, width, streams), unit, slot in each_chunk(g, a, f):
                        for e in range(2):
                            at, st = bass.ds(chan(e, f), 1), 3 * (unit + e)
                            if streams:
                                r = raw[:, slot, e, 0:DB * (H2 + DS)].rearrange("p (b r) -> p b r", b=DB)
                                u = acc[:, slot, e, 0:width].rearrange("p (b r) -> p b r", b=DB)
                                past = hist_s[:, at, :].rearrange("p o (b r) -> p (o b) r", b=DB)
                                old, new = r[:, :, 0:H2], r[:, :, DS:]
                                taps = [r[:, :, i:i + DS] for i in range(H2)]
                            else:
                                r, u = raw[:, slot, e], acc[:, slot, e]
                                past = hist[:, at, :].rearrange("p o r -> p (o r)")
                                old, new = r[:, 0:H2], r[:, BANK:]
                                taps = [r[:, i:i + BANK] for i in range(H2)]
                            dve.wait_ge(s["conv_done"], unit + (e + 1))
                            move(old, past).then_inc(s["conv_step"], 1)
                            dve.wait_ge(s["conv_step"], st + 1)
                            dve.wait_ge(s["raw_ready"], 2 * unit + (2 * e + CREDIT + 2))
                            move(past, new).then_inc(s["conv_step"], 1)
                            stt(u, taps[1], vecs[:, 1, at], u, ALU.mult, ALU.add).then_inc(s["conv_step"], 1)
                            dve.wait_ge(s["conv_step"], st + 3)
                            stt(u, taps[0], vecs[:, 0, at], u, ALU.mult, ALU.add).then_inc(s["conv_done"], 1)
                        K = chunk_no(g, f, n)
                        dve.wait_ge(s["silu_ready"], K + 1)
                        dve.wait_ge(s["conv_done"], unit + 6)
                        nc.vector.tensor_tensor(gT[:, bass.ds(f, 1), col:col + width].rearrange("p o t -> p (o t)"),
                                                acc[:, slot, 0, 0:width], acc[:, slot, 1, 0:width], ALU.mult) \
                            .then_inc(s["g_ready"], 1)

                if g == 1:
                    dve.wait_ge(s["down_mm"], down0[1] + DOWNC)
                each_f(dve, g, convs)
                with dve.Fori(0, KD // 2) as i:
                    for a in range(2):
                        for n, (col, width, _) in enumerate(chunks[g]):
                            N = (2 * i + a) * len(chunks[g]) + (down0[g] + n)
                            odd = (a * len(chunks[g]) + n + down0[g]) % 2
                            dve.wait_ge(s["down_mm"], N + 1 + DOWNC)
                            move(hnT[:, bass.ds(2 * i + a, 1), col:col + width].rearrange("p o t -> p (o t)"),
                                 bank[:, 6 + odd, 0:width]).then_inc(s["y_out"], 1)
                dve.wait_ge(s["norm_loaded"], 16)
                for t in range(tiles[g]):
                    T, a = tile0[g] + t, t % 2
                    loads = t // 2 + 1 + (g * ((tiles[0] + 1 - a) // 2))
                    dve.wait_ge(s[f"h{a}_loaded"], 16 * loads)
                    if loads > 1:
                        dve.wait_ge(s[f"y_stored{a}"], 16 * (loads - 1))
                    for n in range(2):
                        dve.wait_ge(s["y_turned"], 2 * T + n + 1)
                        cols = slice(n * BANK, (n + 1) * BANK)
                        nc.vector.tensor_tensor(y[:, a, cols], bank[:, n, :], h_in[:, a, cols], ALU.add) \
                            .then_inc(s["r_ready"], 1)
                        dve.wait_ge(s["r_ready"], 2 * T + n + 1)
                        dve.sem_inc(s["y_read"], 1)
                    dve.wait_ge(s["rs_ready"], T + 1)
                    stt(y[:, a], y[:, a], rs[:, a:a + 1], norm_w[:], ALU.mult, ALU.mult).then_inc(s["yn_ready"], 1)
            for q in range(NF2 // 4):
                dve.wait_ge(s["tail_turned"], q + 1)
                b = 2 + 2 * (q % 3)
                cp(rows_s[:, q * BANK:(q + 1) * BANK], bank[0:R, b, :]).then_inc(s["tail_read"], 1)
                cp(rows_p[:, q * BANK:(q + 1) * BANK], bank[0:H2, b + 1, :]).then_inc(s["tail_read"], 1)
    ph.close()


def build(nc, arg, out):
    _, SEQ, D = arg["x_prompt"].shape
    DB, DS, _ = arg["x_sample"].shape
    _, _, PAST, FH, FD = arg["cache_fox_k"].shape
    _, _, GH, DK, DV = arg["state_gdn"].shape
    CW, GC = arg["gdn_conv_w"].shape[1:]
    FC, F2 = arg["ffn_conv_w"].shape[1:]
    c = dict(SEQ=SEQ, D=D, DB=DB, DS=DS, PAST=PAST, FH=FH, FD=FD, FW=FH * FD, GH=GH, DK=DK, DV=DV, GW=GH * DV,
             CW=CW, GC=GC, FC=FC, F2=F2, NT=SEQ // P + 1)
    assert arg["x_prompt"].shape[0] == 1 and DB * DS == P and FH * DS == P and DK == P and DV == P

    TOK = SEQ + P
    scratch = {n: nc.dram_tensor(f"scratch_{n}", s, F32, kind="Internal").ap() for n, s in (
        ("q_tok", (TOK, FH * FD)), ("z_tok", (TOK, GH * DV)), ("gb_tok", (TOK, 2 * GH)), ("gch", (GC, TOK)),
        ("mix_tok", (TOK, FH * FD + GH * DV)), ("h_tok", (TOK, D)), ("hnT", (D, TOK)))}
    io = dict(arg, **scratch)
    io["x_p"] = arg["x_prompt"].rearrange("a t d -> (a t) d")
    io["x_s"] = arg["x_sample"].rearrange("a t d -> (a t) d")
    io["conv_state"] = arg["state_gdn_conv"].rearrange("l b r n -> (l b r) n")
    io["ffn_state"] = arg["state_ffn_conv"].rearrange("l b r n -> (l b r) n")
    io["y_p"] = out[0].rearrange("a t d -> (a t) d")
    io["y_s"] = out[1].rearrange("a t d -> (a t) d")
    for n, i in (("k_p", 2), ("v_p", 3), ("k_s", 8), ("v_s", 9)):
        io[n] = out[i].rearrange("l a t h d -> (l a t) (h d)")
    for n, i in (("logf_p", 4), ("logf_s", 10), ("conv_p", 6), ("ffn_p", 7), ("conv_s", 12), ("ffn_s", 13)):
        io[n] = out[i].rearrange("l a t h -> (l a t) h")
    io["S_p"], io["S_s"] = out[5][0, 0], out[11][0]

    with ExitStack() as ctx:
        def sb(name, shape):
            return ctx.enter_context(nc.sbuf_tensor(name, shape, F32))

        bank = ctx.enter_context(nc.psum_tensor("bank", [P, 8, BANK], F32))
        for n in ("ones", "ident", "tri", "tri_s", "same_stream", "causal", "after", "decay_mask", "decay_mask_s",
                  "level0_t"):
            c[n] = sb(n, [P, P])
        c["level"] = [sb(f"level{n}", [P, P]) for n in range(7)]
        c["stream_rows"] = sb("stream_rows", [P, DB])
        c["before_q"] = sb("before_q", [P, DB, DS])
        c["later_in_stream"], c["causal_s"] = sb("later_in_stream", [P, DS]), sb("causal_s", [P, DS])
        c["eps"] = sb("eps", [P, 1])
        build_constants(nc, c)
        for phase in PHASES:
            phase(nc, c, io, bank)


PHASES = [project, delta, fox_prompt, fox_sample, mix, ffn]

_INS = ['x_prompt', 'x_sample', 'cache_fox_k', 'cache_fox_v', 'cache_fox_logf', 'state_gdn', 'state_gdn_conv',
        'state_ffn_conv', 'w_in', 'b_fox_f', 'gdn_conv_w', 'gdn_a_log', 'gdn_dt_bias', 'gdn_norm_w', 'w_o',
        'norm_mix_w', 'norm_ffn_w', 'w_up', 'ffn_conv_w', 'ffn_conv_b', 'w_down', 'norm_final_w']


def kernel(**inputs):
    import numpy as _np
    import concourse.bacc as _bacc
    from concourse.bass_utils import run_bass_kernel_spmd as _run

    nc = _bacc.Bacc("TRN2", target_bir_lowering=False, num_devices=1)
    arrays, arg = {}, {}
    for name in _INS:
        a = _np.ascontiguousarray(inputs[name])
        arrays[f"in_{name}_dram"] = a
        arg[name] = nc.dram_tensor(f"in_{name}_dram", a.shape, mybir.dt.from_np(a.dtype), kind="ExternalInput").ap()
    s = {n: a.shape for n, a in arg.items()}
    fox_p = (1,) + s["x_prompt"][:2] + s["cache_fox_k"][3:]
    fox_s = (1,) + s["x_sample"][:2] + s["cache_fox_k"][3:]
    outs = [s["x_prompt"], s["x_sample"],
            fox_p, fox_p, fox_p[:4], (1, 1) + s["state_gdn"][2:], (1, 1) + s["state_gdn_conv"][2:],
            (1, 1) + s["state_ffn_conv"][2:],
            fox_s, fox_s, fox_s[:4], s["state_gdn"], s["state_gdn_conv"], s["state_ffn_conv"]]
    out = [nc.dram_tensor(f"out_{i}_dram", shape, F32, kind="ExternalOutput").ap() for i, shape in enumerate(outs)]
    build(nc, arg, out)
    r = _run(nc, [arrays], core_ids=[0])
    return tuple(r.results[0][f"out_{i}_dram"] for i in range(len(outs)))
```

```python
from contextlib import ExitStack

import concourse.bass as bass
from concourse import mybir

P = 128
NEG = -1e30
EPS = 1e-6
F32 = mybir.dt.float32
F32R = mybir.dt.float32r
ALU = mybir.AluOpType
ACT = mybir.ActivationFunctionType
AX = mybir.AxisListType
BANK = 512


class Phase:

    def __init__(self, nc, name):
        self.nc, self.name, self.sems, self.stack = nc, name, [], ExitStack()

    def sb(self, name, shape, dt=F32):
        return self.stack.enter_context(self.nc.sbuf_tensor(f"{self.name}_{name}", shape, dt))

    def sem(self, name):
        s = self.nc.alloc_semaphore(f"{self.name}_{name}")
        self.sems.append(s)
        return s

    def close(self):
        self.stack.close()
        self.nc.clear_and_free_semaphores(self.sems)
        self.nc.all_engine_barrier()


class Step:

    def __init__(self, eng, sem):
        self.eng, self.sem, self.n = eng, sem, 0

    def __call__(self, ins):
        self.n += 1
        ins.then_inc(self.sem, 1)
        self.eng.wait_ge(self.sem, self.n)


def spread(ap, shape):
    return ap.to_broadcast(list(shape))


def build_constants(nc, c, first_loads):
    ph = Phase(nc, "const")
    pool_done, sums_done, step_sem = ph.sem("pool_done"), ph.sem("sums_done"), ph.sem("pool_step")
    DB, DS = c["DB"], c["DS"]
    later = ph.sb("later", [P, DB, DS])
    upto = ph.sb("upto", [P, DB, DS])
    with nc.Block() as block:

        @block.sync
        def _(sp):
            first_loads(sp)

        @block.gpsimd
        def _(pool):
            step = Step(pool, step_sem)

            def keep(t, pattern, base, mult, fill=0.0, op=ALU.is_ge):
                step(nc.gpsimd.affine_select(out=t, in_=t, pattern=pattern, base=base, channel_multiplier=mult,
                                             compare_op=op, fill=fill))

            step(nc.gpsimd.memset(c["ones"][:], 1.0))
            step(nc.gpsimd.memset(c["eps"][:], EPS))
            step(nc.gpsimd.memset(c["ident"][:], 0.0))
            keep(c["ident"][:], [[-1, P]], 0, 1, 1.0, ALU.not_equal)
            step(nc.gpsimd.memset(c["tri"][:], 1.0))
            keep(c["tri"][:], [[1, P]], 0, -1)
            same = c["same_stream"][:].rearrange("p (b r) -> p b r", r=DS)
            step(nc.gpsimd.memset(c["same_stream"][:], 1.0))
            keep(same, [[-DS, DB], [0, DS]], 0, 1)
            keep(same, [[DS, DB], [0, DS]], DS - 1, -1)
            step(nc.gpsimd.tensor_copy(c["tri_s"][:], c["same_stream"][:]))
            keep(c["tri_s"][:], [[1, P]], 0, -1)
            step(nc.gpsimd.memset(c["stream_rows"][:], 1.0))
            keep(c["stream_rows"][:], [[-DS, DB]], 0, 1)
            keep(c["stream_rows"][:], [[DS, DB]], DS - 1, -1)
            step(nc.gpsimd.memset(c["causal"][:], 0.0))
            keep(c["causal"][:], [[-1, P]], 0, 1, NEG)
            step(nc.gpsimd.memset(c["after"][:], 1.0))
            keep(c["after"][:], [[-1, P]], -1, 1)
            step(nc.gpsimd.memset(c["before_q"][:], 1.0))
            keep(c["before_q"][:], [[-DS, DB], [0, DS]], 0, 1)
            keep(c["before_q"][:], [[DS, DB], [1, DS]], 0, -1)
            for n, m in enumerate(c["level"]):
                s = 1 << n
                v = m[:].rearrange("p (a h r) -> p a h r", h=2, r=s)
                step(nc.gpsimd.memset(m[:], 0.0))
                step(nc.gpsimd.memset(v[:, :, 0, :], -1.0))
                keep(v[:, :, 0, :], [[-2 * s, P // (2 * s)], [0, s]], -s, 1)
                keep(v[:, :, 0, :], [[2 * s, P // (2 * s)], [0, s]], 2 * s - 1, -1)
            v = c["level0_t"][:].rearrange("p (a h) -> p a h", h=2)
            step(nc.gpsimd.memset(c["level0_t"][:], 0.0))
            step(nc.gpsimd.memset(v[:, :, 1:2], -1.0))
            keep(v[:, :, 1:2], [[-2, P // 2], [0, 1]], 0, 1)
            keep(v[:, :, 1:2], [[2, P // 2], [0, 1]], 0, -1)
            step(nc.gpsimd.memset(later[:], 1.0))
            keep(later[:], [[-DS, DB], [-1, DS]], -1, 1)
            keep(later[:], [[DS, DB], [0, DS]], DS - 1, -1)
            step(nc.gpsimd.memset(upto[:], 1.0))
            keep(upto[:], [[-DS, DB], [-1, DS]], 0, 1)
            keep(upto[:], [[DS, DB], [0, DS]], DS - 1, -1)
            pool.sem_inc(pool_done, 1)

        @block.vector
        def _(dve):
            step = Step(dve, sums_done)
            dve.wait_ge(pool_done, 1)
            step(nc.vector.tensor_reduce(c["later_in_stream"][:], later[:].rearrange("p b k -> p k b"), AX.X, ALU.add))
            step(nc.vector.tensor_reduce(c["causal_s"][:], upto[:].rearrange("p b k -> p k b"), AX.X, ALU.add))
            for m in (c["causal_s"][:],):
                step(nc.vector.tensor_scalar(m, m, -1.0, -NEG, ALU.add, ALU.mult))
            step(nc.vector.tensor_scalar(c["decay_mask"][:], c["tri"][:], -1.0, -NEG, ALU.add, ALU.mult))
            step(nc.vector.tensor_scalar(c["decay_mask_s"][:], c["tri_s"][:], -1.0, -NEG, ALU.add, ALU.mult))
    ph.close()


def project(nc, c, io, bank):
    ph = Phase(nc, "proj")
    D, FW, FH, GC, GH, GW, CW = (c[k] for k in ("D", "FW", "FH", "GC", "GH", "GW", "CW"))
    DB, DS, SEQ = c["DB"], c["DS"], c["SEQ"]
    KD, NCH, H3 = D // P, GC // P, CW - 1
    GT = 4
    W = GT * P
    NG = SEQ // W
    off_f = 3 * FW
    off_g = off_f + FH
    off_a = off_g + GC
    off_z = off_a + 2 * GH
    NS = FH + 2 * GH
    N_IN = off_z + GW
    HB = KD // 2

    w = ph.sb("w", [P, KD, N_IN])
    x = ph.sb("x", [P, 2, D])
    squares = ph.sb("squares", [P, D])
    xn = ph.sb("xn", [P, 2, D])
    xnT = ph.sb("xnT", [P, KD, W])
    vec_rows = ph.sb("vec_rows", [KD + CW * NCH, P])
    vecs = ph.sb("vecs", [P, KD + CW * NCH])
    rows = ph.sb("rows", [P, 4, BANK])
    ss, ln_ms, rs = (ph.sb(n, [P, 2]) for n in ("ss", "ln_ms", "rs"))
    raw = ph.sb("raw", [P, 2, H3 + W])
    acc = ph.sb("acc", [P, 2, W])
    hist = ph.sb("hist", [P, NCH, H3])
    hist_s = ph.sb("hist_s", [P, NCH, DB, H3])
    tails_s = ph.sb("tails_s", [DB * H3, GC])
    tails_p = ph.sb("tails_p", [H3, GC])
    sign, shift = ph.sb("sign", [P, NS]), ph.sb("shift", [P, NS])
    expa = ph.sb("expa", [P, GH])
    gy, gpos, gabs, gexp, gln, gsp = (ph.sb(n, [P, GT, NS]) for n in ("gy", "gpos", "gabs", "gexp", "gln", "gsp"))
    glogf = ph.sb("glogf", [P, GT, FH])
    gout = ph.sb("gout", [P, GT, 2 * GH])

    w_loaded = [ph.sem(f"w_loaded{n}") for n in range(8)]
    x_loaded = [ph.sem(f"x_loaded{n}") for n in range(2)]
    small_loaded, hist_loaded, setup_done = ph.sem("small_loaded"), ph.sem("hist_loaded"), ph.sem("setup_done")
    vecs_turned, vecs_ready = ph.sem("vecs_turned"), ph.sem("vecs_ready")
    x_squared, ln_done, rs_ready = ph.sem("x_squared"), ph.sem("ln_done"), ph.sem("rs_ready")
    xn_ready, xn_turned, xnT_ready = (ph.sem(n) for n in ("xn_ready", "xn_turned", "xnT_ready"))
    rows_mm, rows_out = ph.sem("rows_mm"), ph.sem("rows_out")
    rows_stored = [ph.sem(f"rows_stored{n}") for n in range(4)]
    gates_mm, gates_read, gate_v, gate_a, gates_stored = (ph.sem(n) for n in (
        "gates_mm", "gates_read", "gate_v", "gate_a", "gates_stored"))
    chan_mm, chan_raw, conv_step, conv_done, silu_done = (ph.sem(n) for n in (
        "chan_mm", "chan_raw", "conv_step", "conv_done", "silu_done"))
    chan_stored = [ph.sem(f"chan_stored{n}") for n in range(2)]
    tail_turned, tail_ready, tail_stored = ph.sem("tail_turned"), ph.sem("tail_ready"), ph.sem("tail_stored")

    wi = io["w_in"][0].rearrange("(k p) n -> p k n", p=P)
    w_parts = [(0, FW), (FW, 2 * FW), (2 * FW, 3 * FW), (off_z, N_IN), (off_f, off_g), (off_a, off_z),
               (off_g, off_g + GC // 2), (off_g + GC // 2, off_a)]
    row_chunks = [(0, "q"), (FW, "k"), (2 * FW, "v"), (off_z, "z")]

    def place(g, m):
        if g is None:
            return 0, 0, 0, 1
        s = m % 2
        return g * GT + (m + 1), m, s, g * (GT // 2) + (m // 2 + 1 + (1 if s == 0 else 0))

    def slot_free(g, m):
        return g * GT + (m + 1 if m == 0 else m)

    def rows_dst(name, g, m):
        if g is None:
            return {"q": io["q_tok"][SEQ:, :], "k": io["k_s"], "v": io["v_s"], "z": io["z_tok"][SEQ:, :]}[name]
        return {"q": io["q_tok"], "k": io["k_p"], "v": io["v_p"], "z": io["z_tok"]}[name][
            bass.ds(g * W + m * P, P), :]

    def first_loads(sp):
        sp.dma_start(x[:, 0], io["x_s"]).then_inc(x_loaded[0], 16)
        sp.dma_start(vec_rows[0:KD], io["norm_mix_w"].rearrange("l (k p) -> (l k) p", p=P)) \
            .then_inc(small_loaded, 16)
        sp.dma_start(vec_rows[KD:], io["gdn_conv_w"].rearrange("l i (k p) -> (l i k) p", p=P)) \
            .then_inc(small_loaded, 16)
        sp.dma_start(shift[:, 0:FH], io["b_fox_f"][0].partition_broadcast(P)).then_inc(small_loaded, 16)
        sp.dma_start(shift[:, FH:FH + GH], io["gdn_dt_bias"][0].partition_broadcast(P)).then_inc(small_loaded, 16)
        sp.dma_start(expa[:], io["gdn_a_log"][0].partition_broadcast(P)).then_inc(small_loaded, 16)
        sp.dma_start(tails_s[:], io["conv_state"]).then_inc(hist_loaded, 16)
        for n, (a, b) in enumerate(w_parts):
            sp.dma_start(w[:, :, a:b], wi[:, :, a:b]).then_inc(w_loaded[n], 16)

    build_constants(nc, c, first_loads)
    with nc.Block() as block:

        @block.sync
        def _(sp):
            with sp.Fori(0, NG) as g:
                for m in range(GT):
                    sp.wait_ge(xn_ready, slot_free(g, m))
                    sp.dma_start(x[:, m % 2], io["x_p"][bass.ds(g * W + m * P, P), :]).then_inc(x_loaded[m % 2], 16)

        @block.tensor
        def _(pe):
            def turn(g, m):
                T, at, s, _ = place(g, m)
                pe.wait_ge(xn_ready, T + 1)
                for h in range(2):
                    pe.wait_ge(xnT_ready, 2 * T + (h + 1))
                    for k in range(HB):
                        mm = pe.transpose(bank[:, h, k * P:(k + 1) * P],
                                          xn[:, s, (h * HB + k) * P:(h * HB + k + 1) * P], c["ident"][:])
                    mm.then_inc(xn_turned, 1)

            def row_products(g, m):
                T, at, _, _ = place(g, m)
                pe.wait_ge(xnT_ready, 2 * T + 4)
                for n, (col, _) in enumerate(row_chunks):
                    if g is None:
                        pe.wait_ge(w_loaded[n], 16)
                    pe.wait_ge(rows_out, 4 * T + (n + 1))
                    for k in range(KD):
                        mm = pe.matmul(bank[:, 2 + n % 2, :], xnT[:, k, at * P:(at + 1) * P], w[:, k, col:col + BANK],
                                       start=(k == 0), stop=(k == KD - 1))
                    mm.then_inc(rows_mm, 1)
                if g is None:
                    pe.wait_ge(w_loaded[4], 16)
                    pe.wait_ge(w_loaded[5], 16)
                for a, b, o in ((off_f, off_g, 0), (off_a, off_z, FH)):
                    for k in range(KD):
                        mm = pe.matmul(bank[:, 6, at * NS + o:at * NS + o + b - a], xnT[:, k, at * P:(at + 1) * P],
                                       w[:, k, a:b], start=(k == 0), stop=(k == KD - 1))
                mm.then_inc(gates_mm, 1)

            def channel_products(G, width):
                for ch in range(NCH):
                    if width == P and ch % (NCH // 2) == 0:
                        pe.wait_ge(w_loaded[6 + ch // (NCH // 2)], 16)
                    pe.wait_ge(chan_raw, NCH * G + (ch + 1))
                    for k in range(KD):
                        mm = pe.matmul(bank[:, 4 + ch % 2, 0:width], w[:, k, off_g + ch * P:off_g + (ch + 1) * P],
                                       xnT[:, k, 0:width], start=(k == 0), stop=(k == KD - 1))
                    mm.then_inc(chan_mm, 1)

            pe.wait_ge(small_loaded, 16 * 5)
            pe.transpose(bank[:, 6, 0:KD + CW * NCH], vec_rows[:], c["ident"][0:KD + CW * NCH, 0:KD + CW * NCH])
            pe.wait_ge(hist_loaded, 16)
            for ch in range(NCH):
                mm = pe.transpose(bank[:, 7, ch * DB * H3:(ch + 1) * DB * H3], tails_s[:, ch * P:(ch + 1) * P],
                                  c["ident"][0:DB * H3, 0:DB * H3])
            mm.then_inc(vecs_turned, 1)
            turn(None, 0)
            pe.wait_ge(vecs_ready, 2)
            row_products(None, 0)
            channel_products(0, P)
            with pe.Fori(0, NG) as g:
                pe.wait_ge(gates_read, g + 1)
                turn(g, 0)
                turn(g, 1)
                for m in range(GT):
                    row_products(g, m)
                    if m + 2 < GT:
                        turn(g, m + 2)
                channel_products(g + 1, W)
            pe.wait_ge(conv_done, NCH * (NG + 1) + 2)
            pe.wait_ge(rows_out, 4 * (NG * GT + 1) + 2)
            for ch in range(NCH):
                pe.transpose(bank[0:DB * H3, ch // 4, (ch % 4) * P:(ch % 4 + 1) * P],
                             hist_s[:, ch].rearrange("p b r -> p (b r)"), c["ident"][:])
                mm = pe.transpose(bank[0:H3, 3 + ch // 4, (ch % 4) * P:(ch % 4 + 1) * P], hist[:, ch], c["ident"][:])
            mm.then_inc(tail_turned, 1)

        @block.scalar
        def _(act):
            def norm_factor(g, m):
                T, _, s, loads = place(g, m)
                act.wait_ge(x_loaded[s], 16 * loads)
                if g is not None:
                    act.wait_ge(xn_ready, slot_free(g, m))
                nc.scalar.activation(squares[:], x[:, s], ACT.Square, accum_out=ss[:, s:s + 1]).then_inc(x_squared, 1)
                act.wait_ge(x_squared, T + 1)
                nc.scalar.activation(ln_ms[:, s:s + 1], ss[:, s:s + 1], ACT.Ln, scale=1.0 / D, bias=c["eps"][:]) \
                    .then_inc(ln_done, 1)
                act.wait_ge(ln_done, T + 1)
                nc.scalar.activation(rs[:, s:s + 1], ln_ms[:, s:s + 1], ACT.Exp, scale=-0.5).then_inc(rs_ready, 1)

            def row_copies(g, m):
                T, _, _, _ = place(g, m)
                for n, (_, name) in enumerate(row_chunks):
                    act.wait_ge(rows_mm, 4 * T + (n + 1))
                    act.wait_ge(rows_stored[n], 16 * T + 16)
                    nc.scalar.activation(rows[:, n], bank[:, 2 + n % 2, :], ACT.Silu if name == "z" else ACT.Copy) \
                        .then_inc(rows_out, 1)
                    act.wait_ge(rows_out, 4 * T + (n + 3))
                    act.dma_start(rows_dst(name, g, m), rows[:, n]).then_inc(rows_stored[n], 16)

            def gates(G, g, tiles):
                act.wait_ge(gate_v, 7 * G + 4)
                nc.scalar.activation(gexp[:, 0:tiles], gabs[:, 0:tiles], ACT.Exp, scale=-1.0).then_inc(gate_a, 1)
                act.wait_ge(gate_a, 3 * G + 2)
                nc.scalar.activation(gln[:, 0:tiles], gexp[:, 0:tiles], ACT.Ln, bias=c["ones"][:, 0:1]) \
                    .then_inc(gate_a, 1)
                act.wait_ge(gate_v, 7 * G + 5)
                nc.scalar.activation(gout[:, 0:tiles, GH:], gsp[:, 0:tiles, FH + GH:], ACT.Exp, scale=-1.0) \
                    .then_inc(gate_a, 1)
                act.wait_ge(gate_a, 3 * G + 4)
                act.wait_ge(gate_v, 7 * G + 7)
                if g is None:
                    logf_dst, gb_dst = io["logf_s"].unsqueeze(1), io["gb_tok"][SEQ:, :].unsqueeze(1)
                else:
                    logf_dst, gb_dst = (io[n][bass.ds(g * W, W), :].rearrange("(m p) h -> p m h", p=P)
                                        for n in ("logf_p", "gb_tok"))
                act.dma_start(logf_dst, glogf[:, 0:tiles]).then_inc(gates_stored, 16)
                act.dma_start(gb_dst, gout[:, 0:tiles]).then_inc(gates_stored, 16)

            def silu(G, g, ch):
                s, width = ch % 2, P if g is None else W
                act.wait_ge(conv_done, NCH * G + (ch + 3))
                nc.scalar.activation(acc[:, s, 0:width], acc[:, s, 0:width], ACT.Silu).then_inc(silu_done, 1)
                act.wait_ge(silu_done, NCH * G + (ch + 1))
                cols = slice(SEQ, SEQ + P) if g is None else bass.ds(g * W, W)
                act.dma_start(io["gch"][ch * P:(ch + 1) * P, cols], acc[:, s, 0:width]).then_inc(chan_stored[s], 16)

            def channels(G, g):
                for ch in range(NCH):
                    s = ch % 2
                    act.wait_ge(chan_mm, NCH * G + (ch + 1))
                    act.wait_ge(conv_done, NCH * G + (ch + 1))
                    if g is None:
                        nc.scalar.copy(raw[:, s, 0:DB * (H3 + DS)].rearrange("p (b r) -> p b r", b=DB)[:, :, H3:],
                                       bank[:, 4 + s, 0:P].rearrange("p (b r) -> p b r", b=DB)).then_inc(chan_raw, 1)
                    else:
                        nc.scalar.copy(raw[:, s, H3:], bank[:, 4 + s, :]).then_inc(chan_raw, 1)
                    if ch >= 1:
                        silu(G, g, ch - 1)
                silu(G, g, NCH - 1)

            act.sem_inc(rows_out, 2)
            act.sem_inc(chan_raw, 2)
            for n in range(4):
                act.sem_inc(rows_stored[n], 16)
            for s in range(2):
                act.sem_inc(chan_stored[s], 16)
            act.wait_ge(small_loaded, 16 * 5)
            nc.scalar.activation(expa[:], expa[:], ACT.Exp).then_inc(gate_a, 1)
            norm_factor(None, 0)
            row_copies(None, 0)
            gates(0, None, 1)
            norm_factor(0, 0)
            norm_factor(0, 1)
            channels(0, None)

            def group(g, last):
                norm_factor(g, 2)
                row_copies(g, 0)
                norm_factor(g, 3)
                for m in range(1, GT):
                    row_copies(g, m)
                gates(g + 1, g, GT)
                if not last:
                    norm_factor(g + 1, 0)
                    norm_factor(g + 1, 1)
                channels(g + 1, g)

            with act.Fori(0, NG - 1) as g:
                group(g, False)
            group(NG - 1, True)
            act.wait_ge(tail_ready, 1)
            act.dma_start(io["conv_s"], tails_s[:]).then_inc(tail_stored, 16)
            act.dma_start(io["conv_p"], tails_p[:]).then_inc(tail_stored, 16)
            for n in range(4):
                act.wait_ge(rows_stored[n], 16 * (NG * GT + 2))
            for s in range(2):
                act.wait_ge(chan_stored[s], 16 * (NG + 1) * (NCH // 2) + 16)
            act.wait_ge(gates_stored, 32 * (NG + 1))
            act.wait_ge(tail_stored, 32)

        @block.vector
        def _(dve):
            def normalise(g, m):
                T, _, s, _ = place(g, m)
                dve.wait_ge(rs_ready, T + 1)
                if g is not None:
                    dve.wait_ge(xn_turned, 2 * slot_free(g, m))
                nc.vector.tensor_scalar(xn[:, s], x[:, s], rs[:, s:s + 1], None, ALU.mult).then_inc(xn_ready, 1)

            def keep_turned(g, m):
                T, at, _, _ = place(g, m)
                if g is not None:
                    dve.wait_ge(chan_mm, NCH * (g + 1))
                for h in range(2):
                    dve.wait_ge(xn_turned, 2 * T + (h + 1))
                    nc.vector.tensor_tensor(
                        xnT[:, h * HB:(h + 1) * HB, at * P:(at + 1) * P],
                        bank[:, h, :].rearrange("p (k t) -> p k t", t=P),
                        spread(vecs[:, h * HB:(h + 1) * HB].unsqueeze(2), [P, HB, P]), ALU.mult) \
                        .then_inc(xnT_ready, 1)

            def gates(G, g, tiles):
                if g is not None:
                    dve.wait_ge(gates_stored, 32 * G)
                dve.wait_ge(gates_mm, 1 if g is None else g * GT + (GT + 1))
                v = 7 * G
                y, sh = gy[:, 0:tiles], [P, tiles, NS]
                nc.vector.tensor_tensor(y, bank[:, 6, 0:tiles * NS].rearrange("p (m n) -> p m n", n=NS),
                                        spread(sign[:].unsqueeze(1), sh), ALU.mult).then_inc(gate_v, 1)
                dve.wait_ge(gate_v, v + 1)
                dve.sem_inc(gates_read, 1)
                nc.vector.tensor_tensor(y, y, spread(shift[:].unsqueeze(1), sh), ALU.add).then_inc(gate_v, 1)
                dve.wait_ge(gate_v, v + 2)
                nc.vector.tensor_scalar(gpos[:, 0:tiles], y, 0.0, None, ALU.max).then_inc(gate_v, 1)
                nc.vector.scalar_tensor_tensor(gabs[:, 0:tiles], y, -1.0, y, ALU.mult, ALU.max).then_inc(gate_v, 1)
                dve.wait_ge(gate_a, 3 * G + 3)
                dve.wait_ge(gate_v, v + 4)
                nc.vector.tensor_tensor(gsp[:, 0:tiles], gpos[:, 0:tiles], gln[:, 0:tiles], ALU.add) \
                    .then_inc(gate_v, 1)
                dve.wait_ge(gate_v, v + 5)
                nc.vector.tensor_scalar(glogf[:, 0:tiles], gsp[:, 0:tiles, 0:FH], -1.0, None, ALU.mult) \
                    .then_inc(gate_v, 1)
                nc.vector.scalar_tensor_tensor(gout[:, 0:tiles, 0:GH], gsp[:, 0:tiles, FH:FH + GH], -1.0,
                                               spread(expa[:].unsqueeze(1), [P, tiles, GH]), ALU.mult, ALU.mult) \
                    .then_inc(gate_v, 1)

            def conv(G, g, ch):
                s, n, st = ch % 2, NCH * G + ch, 5 * (NCH * G + ch)
                width = P if g is None else W
                if g is None:
                    r = raw[:, s, 0:DB * (H3 + DS)].rearrange("p (b r) -> p b r", b=DB)
                    a = acc[:, s, 0:P].rearrange("p (b r) -> p b r", b=DB)
                    past, old, new = hist_s[:, ch], r[:, :, 0:H3], r[:, :, DS:]
                    taps = [r[:, :, i:i + DS] for i in range(CW)]
                else:
                    r, a = raw[:, s], acc[:, s]
                    past, old, new = hist[:, ch], r[:, 0:H3], r[:, W:]
                    taps = [r[:, i:i + W] for i in range(CW)]
                wt = [vecs[:, KD + i * NCH + ch:KD + i * NCH + ch + 1] for i in range(CW)]
                dve.wait_ge(conv_done, n + 1)
                nc.vector.tensor_copy(old, past).then_inc(conv_step, 1)
                dve.wait_ge(conv_step, st + 1)
                dve.wait_ge(chan_raw, n + 3)
                nc.vector.tensor_copy(past, new).then_inc(conv_step, 1)
                dve.wait_ge(chan_stored[s], 16 * ((NCH // 2) * G + (ch // 2 + 1)))
                nc.vector.tensor_scalar(a, taps[0], wt[0], None, ALU.mult).then_inc(conv_step, 1)
                for i in range(1, CW):
                    dve.wait_ge(conv_step, st + (2 + i))
                    nc.vector.scalar_tensor_tensor(a, taps[i], wt[i], a, ALU.mult, ALU.add) \
                        .then_inc(conv_step if i < CW - 1 else conv_done, 1)

            dve.sem_inc(xnT_ready, 2)
            dve.sem_inc(conv_done, 2)
            step = Step(dve, setup_done)
            step(nc.vector.memset(sign[:], -1.0))
            step(nc.vector.memset(sign[:, FH:FH + GH], 1.0))
            step(nc.vector.memset(shift[:, FH + GH:], 0.0))
            step(nc.vector.memset(hist[:], 0.0))
            dve.wait_ge(small_loaded, 16 * 5)
            step(nc.vector.tensor_tensor(shift[:], shift[:], sign[:], ALU.mult))
            dve.wait_ge(vecs_turned, 1)
            nc.vector.tensor_copy(vecs[:], bank[:, 6, 0:KD + CW * NCH]).then_inc(vecs_ready, 1)
            nc.vector.tensor_copy(hist_s[:].rearrange("p c b r -> p (c b r)"), bank[:, 7, 0:NCH * DB * H3]) \
                .then_inc(vecs_ready, 1)
            dve.wait_ge(vecs_ready, 2)
            dve.wait_ge(gate_a, 1)
            normalise(None, 0)
            keep_turned(None, 0)
            gates(0, None, 1)
            normalise(0, 0)
            normalise(0, 1)
            for ch in range(NCH):
                conv(0, None, ch)

            def group(g, last):
                keep_turned(g, 0)
                normalise(g, 2)
                keep_turned(g, 1)
                normalise(g, 3)
                keep_turned(g, 2)
                keep_turned(g, 3)
                gates(g + 1, g, GT)
                if not last:
                    normalise(g + 1, 0)
                    normalise(g + 1, 1)
                for ch in range(NCH):
                    conv(g + 1, g, ch)

            with dve.Fori(0, NG - 1) as g:
                group(g, False)
            group(NG - 1, True)
            dve.wait_ge(tail_turned, 1)
            step = Step(dve, setup_done)
            step.n = 5
            for n in range(NCH // 4):
                step(nc.vector.tensor_copy(tails_s[:, n * BANK:(n + 1) * BANK], bank[0:DB * H3, n, :]))
                step(nc.vector.tensor_copy(tails_p[:, n * BANK:(n + 1) * BANK], bank[0:H3, 3 + n, :]))
            dve.sem_inc(tail_ready, 1)
    ph.close()


def delta(nc, c, io, bank):
    ph = Phase(nc, "gdn")
    GH, GC, DK, DV, FW, DB, DS, SEQ = (c[k] for k in ("GH", "GC", "DK", "DV", "FW", "DB", "DS", "SEQ"))
    NCH, NC, HH = GC // P, SEQ // P, GH // 2
    LEVELS, LEVELS_S = 7, 4
    assert (1 << LEVELS) == P and (1 << LEVELS_S) == DS

    def wide(name, n=GH):
        return ph.sb(name, [P, n, P])

    qkvT = wide("qkvT", NCH)
    gb = ph.sb("gb", [P, 2 * GH])
    z, zn, gnorm = wide("z"), wide("zn"), ph.sb("gnorm", [P, DV])
    sq, ss, ln_ss, unit = wide("sq", 2 * GH), *(ph.sb(n, [P, 2 * GH]) for n in ("ss", "ln_ss", "unit"))
    gs, ex = ph.sb("gs", [P, 3 * GH]), ph.sb("ex", [P, 3 * GH])
    f_q, f_qG, f_kb, f_bG = (ph.sb(n, [P, GH]) for n in ("f_q", "f_qG", "f_kb", "f_bG"))
    dx, dec = wide("dx"), wide("dec")
    kn, kb, qn, qG, vb, kbG, kd = (wide(n) for n in ("kn", "kb", "qn", "qG", "vb", "kbG", "kd"))
    knT, kbT, qnT, qGT = (wide(n) for n in ("knT", "kbT", "qnT", "qGT"))
    LT, AT, wn, X, XT, x0 = (wide(n) for n in ("LT", "AT", "wn", "X", "XT", "x0"))
    nwT, dl, S, oc, osq, on, mixed = (wide(n) for n in ("nwT", "dl", "S", "oc", "osq", "on", "mixed"))
    so, ln_so, ro = (ph.sb(n, [P, GH]) for n in ("so", "ln_so", "ro"))
    S_s = ph.sb("S_s", [P, DB, GH, DV])
    ex_s = ph.sb("ex_s", [P, DB, GH])
    dlT, oT, kd_b = wide("dlT"), wide("oT"), ph.sb("kd_b", [P, 2, GH, P])

    names = ("qkv_loaded gb_loaded z_loaded small_loaded state_loaded tok_turned gsum_mm decay_mm unitT_mm unitT_out "
             "kk_mm l0_mm w_mm y_mm xt_mm wt_mm nwt_ready delta_mm delta_ready o_mm s_mm state_ready o_scaled "
             "gsum_v decay_v decay_ready squares_ready sumsq_ready unit_ready ex_ready fac_v scaled_ready lt_ready "
             "x0_step x_ready w_ready xt0_ready xt_ready xt_last o_sq o_sum o_unit pool_scaled pool_x0 zn_ready mix_ready mix_stored "
             "ex_s_ready dlT_mm dlT_ready oT_mm oT_ready kdb_ready sb_mm sb_ready s_stored o_out").split()
    s = {n: ph.sem(n) for n in names}

    XR, WR, YR, TR = 2 * (LEVELS - 1), 2 * (LEVELS - 1), 2 * (LEVELS - 1), 2 * (LEVELS - 2)

    def half(t, a):
        return t[:, a * HH:(a + 1) * HH, :]

    def heads(b):
        return bank[:, b, :].rearrange("p (h n) -> p h n", n=P)

    def bank_half(b):
        return bank[:, b, 0:HH * P].rearrange("p (h n) -> p h n", n=P)

    def per_head(f):
        return spread(f.unsqueeze(2), [P, GH, P])

    with nc.Block() as block:

        @block.sync
        def _(sp):
            def load(t, qkv_free, gb_free, z_free):
                rows = bass.ds(t * P, P)
                qkv_free()
                sp.dma_start(qkvT[:], io["gch"][:, rows].rearrange("(c p) t -> p c t", p=P)) \
                    .then_inc(s["qkv_loaded"], 16)
                gb_free()
                sp.dma_start(gb[:], io["gb_tok"][rows, :]).then_inc(s["gb_loaded"], 16)
                z_free()
                sp.dma_start(z[:], io["z_tok"][rows, :].rearrange("t (h n) -> t h n", n=DV)).then_inc(s["z_loaded"], 16)

            def store(t):
                sp.wait_ge(s["mix_ready"], t + 2)
                sp.dma_start(io["mix_tok"][bass.ds(t * P, P), FW:].rearrange("t (h n) -> t h n", n=DV), mixed[:]) \
                    .then_inc(s["mix_stored"], 16)

            load(0, lambda: None, lambda: None, lambda: None)
            sp.dma_start(gnorm[:], io["gdn_norm_w"][0].partition_broadcast(P)).then_inc(s["small_loaded"], 16)
            sp.dma_start(S_s[:].rearrange("p b h n -> p (b h) n"), io["state_gdn"][0].rearrange("b h k n -> k (b h) n")) \
                .then_inc(s["state_loaded"], 16)
            with sp.Fori(0, NC) as t:
                def gb_read():
                    sp.wait_ge(s["scaled_ready"], 5 * t + 5)
                    sp.wait_ge(s["decay_mm"], t + 1)
                load(t + 1, lambda: sp.wait_ge(s["tok_turned"], 3 * t + 3), gb_read,
                     lambda: sp.wait_ge(s["zn_ready"], t + 1))
                store(t)
            store(NC)
            sp.wait_ge(s["state_ready"], GH * (NC + 1))
            sp.dma_start(io["S_p"].rearrange("h k n -> k h n"), S[:]).then_inc(s["s_stored"], 16)
            sp.wait_ge(s["sb_ready"], GH * DB)
            sp.dma_start(io["S_s"].rearrange("b h k n -> k (b h) n"), S_s[:].rearrange("p b h n -> p (b h) n")) \
                .then_inc(s["s_stored"], 16)
            sp.wait_ge(s["s_stored"], 32)
            sp.wait_ge(s["mix_stored"], 16 * (NC + 2))

        @block.tensor
        def _(pe):
            def chunk(t, streams):
                tri, total, mask = (c["tri_s"], c["same_stream"], c["decay_mask_s"]) if streams else \
                    (c["tri"], c["ones"], c["decay_mask"])
                levels = LEVELS_S if streams else LEVELS
                pe.wait_ge(s["qkv_loaded"], 16 * t + 16)

                def turn(j):
                    for h in range(GH):
                        mm = pe.transpose(bank[:, j, h * P:(h + 1) * P], qkvT[:, j * GH + h, :], c["ident"][:])
                    mm.then_inc(s["tok_turned"], 1)

                turn(1)
                pe.wait_ge(s["gb_loaded"], 16 * t + 16)
                pe.matmul(bank[:, 3, 0:GH], tri[:], gb[:, 0:GH], start=True, stop=True)
                mm = pe.matmul(bank[:, 3, GH:2 * GH], total[:], gb[:, 0:GH], start=True, stop=True)
                if streams:
                    for b in range(DB):
                        mm = pe.matmul(bank[:, 3, (2 + b) * GH:(3 + b) * GH],
                                       spread(c["stream_rows"][:, b:b + 1], [P, P]), gb[:, 0:GH], start=True, stop=True)
                mm.then_inc(s["gsum_mm"], 1)
                pe.matmul(bank[:, 4, :], c["ident"][:], spread(mask[:].unsqueeze(1), [P, GH, P]),
                          start=True, stop=False)
                for h in range(GH):
                    mm = pe.matmul(bank[:, 4, h * P:(h + 1) * P], spread(gb[:, h:h + 1], [P, P]), tri[:],
                                   start=False, stop=(h == GH - 1))
                mm.then_inc(s["decay_mm"], 1)
                pe.wait_ge(s["o_out"], t + 1)
                turn(0)
                pe.wait_ge(s["state_ready"], GH * t + GH)
                turn(2)
                for n, (src, b) in enumerate(((kn, 5), (kb, 6), (qn, 7), (qG, 1))):
                    pe.wait_ge(s["scaled_ready"], 5 * t + (n + 1))
                    for h in range(GH):
                        mm = pe.transpose(bank[:, b, h * P:(h + 1) * P], src[:, h, :], c["ident"][:])
                    mm.then_inc(s["unitT_mm"], 1)
                pe.wait_ge(s["unitT_out"], 4 * t + 2)
                for h in range(GH):
                    mm = pe.matmul(bank[:, 0, h * P:(h + 1) * P], knT[:, h, :], kbT[:, h, :], start=True, stop=True)
                mm.then_inc(s["kk_mm"], 1)
                pe.wait_ge(s["unitT_out"], 4 * t + 3)
                pe.wait_ge(s["scaled_ready"], 5 * t + 5)
                for h in range(GH):
                    mm = pe.matmul(bank[:, 2, h * P:(h + 1) * P], knT[:, h, :], qnT[:, h, :], start=True, stop=True)
                mm.then_inc(s["kk_mm"], 1)
                pe.wait_ge(s["lt_ready"], 2 * t + 1)
                for a in range(2):
                    for h in range(HH):
                        mm = pe.transpose(bank[:, 3 + a, h * P:(h + 1) * P], LT[:, a * HH + h, :], c["ident"][:])
                    mm.then_inc(s["l0_mm"], 1)
                pe.wait_ge(s["unitT_out"], 4 * t + 4)
                for n in range(1, levels):
                    for a in range(2):
                        pe.wait_ge(s["x_ready"], XR * t + (2 * (n - 1) + a + 1))
                        for h in range(HH):
                            mm = pe.matmul(bank[:, 5 + a, h * P:(h + 1) * P], LT[:, a * HH + h, :], X[:, a * HH + h, :],
                                           start=True, stop=True)
                        mm.then_inc(s["w_mm"], 1)
                    if n >= 2:
                        for a in range(2):
                            for h in range(HH):
                                mm = pe.transpose(bank[:, 3 + a, h * P:(h + 1) * P], X[:, a * HH + h, :], c["ident"][:])
                            mm.then_inc(s["xt_mm"], 1)
                    for a in range(2):
                        pe.wait_ge(s["w_ready"], WR * t + (2 * (n - 1) + a + 1))
                        if n == 1:
                            pe.wait_ge(s["xt0_ready"], t + 1)
                        else:
                            pe.wait_ge(s["xt_ready"], TR * t + (2 * (n - 2) + a + 1))
                        for h in range(HH):
                            at = a * HH + h
                            lhsT, rhs = (XT, wn) if n < levels - 1 else (wn, XT)
                            mm = pe.matmul(bank[:, 7 if a == 0 else 1, h * P:(h + 1) * P], lhsT[:, at, :], rhs[:, at, :],
                                           start=True, stop=True)
                        mm.then_inc(s["y_mm"], 1)
                pe.wait_ge(s["xt_last"], 2 * t + 2)
                pe.wait_ge(s["pool_scaled"], 2 * t + 2)
                for h in range(GH):
                    mm = pe.matmul(bank[:, 5, h * P:(h + 1) * P], kbG[:, h, :], XT[:, h, :], start=True, stop=True)
                mm.then_inc(s["wt_mm"], 1)
                pe.wait_ge(s["nwt_ready"], t + 1)
                pe.wait_ge(s["lt_ready"], 2 * t + 2)
                if streams:
                    finish_streams(t)
                    return
                for h in range(GH):
                    o = bank[:, 6, h * P:(h + 1) * P]
                    pe.matmul(o, XT[:, h, :], vb[:, h, :], start=True, stop=False)
                    mm = pe.matmul(o, nwT[:, h, :], S[:, h, :], start=False, stop=True)
                mm.then_inc(s["delta_mm"], 1)
                pe.wait_ge(s["delta_ready"], t + 1)
                for h in range(GH):
                    o = bank[:, 0, h * P:(h + 1) * P]
                    pe.matmul(o, qGT[:, h, :], S[:, h, :], start=True, stop=False)
                    mm = pe.matmul(o, AT[:, h, :], dl[:, h, :], start=False, stop=True)
                mm.then_inc(s["o_mm"], 1)
                for h in range(GH):
                    mm = pe.matmul(bank[:, 2, h * P:(h + 1) * P], kd[:, h, :], dl[:, h, :], start=True, stop=True)
                mm.then_inc(s["s_mm"], 1)

            def finish_streams(t):
                pe.wait_ge(s["state_loaded"], 16)
                for out, sem, first, second, cols in ((6, "dlT_mm", vb, XT, nwT), (7, "oT_mm", dl, AT, qGT)):
                    if out == 7:
                        pe.wait_ge(s["dlT_ready"], 1)
                        for h in range(GH):
                            mm = pe.transpose(bank[:, 5, h * P:(h + 1) * P], dlT[:, h, :], c["ident"][:])
                        mm.then_inc(s["delta_mm"], 1)
                        pe.wait_ge(s["delta_ready"], t + 1)
                    for h in range(GH):
                        pe.matmul(bank[:, out, h * P:(h + 1) * P], first[:, h, :], second[:, h, :],
                                  start=True, stop=False)
                        for b in range(DB):
                            at = h * P + b * DS
                            mm = pe.matmul(bank[:, out, at:at + DS], S_s[:, b, h, :], cols[:, h, b * DS:(b + 1) * DS],
                                           start=False, stop=(b == DB - 1))
                    mm.then_inc(s[sem], 1)
                pe.wait_ge(s["oT_ready"], 1)
                for h in range(GH):
                    mm = pe.transpose(bank[:, 0, h * P:(h + 1) * P], oT[:, h, :], c["ident"][:])
                mm.then_inc(s["o_mm"], 1)
                for b in range(DB):
                    pe.wait_ge(s["kdb_ready"], b + 1)
                    if b >= 2:
                        pe.wait_ge(s["sb_ready"], GH * (b - 1))
                    for h in range(GH):
                        mm = pe.matmul(bank[:, 2 + b % 2, h * P:(h + 1) * P], kd_b[:, b % 2, h, :], dl[:, h, :],
                                       start=True, stop=True)
                    mm.then_inc(s["sb_mm"], 1)

            with pe.Fori(0, NC) as t:
                chunk(t, False)
            chunk(NC, True)

        @block.scalar
        def _(act):
            def chunk(t, streams):
                levels = LEVELS_S if streams else LEVELS
                for n, j in enumerate((1, 0)):
                    act.wait_ge(s["tok_turned"], 3 * t + (n + 1))
                    nc.scalar.activation(sq[:, j * GH:(j + 1) * GH, :], heads(j), ACT.Square) \
                        .then_inc(s["squares_ready"], 1)
                output_log(t)
                act.wait_ge(s["sumsq_ready"], t + 1)
                nc.scalar.activation(ln_ss[:], ss[:], ACT.Ln, bias=c["eps"][:]).then_inc(s["unit_ready"], 1)
                act.wait_ge(s["unit_ready"], 2 * t + 1)
                nc.scalar.activation(unit[:], ln_ss[:], ACT.Exp, scale=-0.5).then_inc(s["unit_ready"], 1)
                act.wait_ge(s["gsum_v"], 2 * t + 2)
                nc.scalar.activation(ex[:], gs[:], ACT.Exp).then_inc(s["ex_ready"], 1)
                if streams:
                    nc.scalar.activation(ex_s[:].rearrange("p b h -> p (b h)"), bank[:, 3, 2 * GH:(2 + DB) * GH],
                                         ACT.Exp).then_inc(s["ex_s_ready"], 1)
                act.wait_ge(s["decay_v"], t + 1)
                nc.scalar.activation(dec[:], dx[:], ACT.Exp).then_inc(s["decay_ready"], 1)
                output_factor(t)
                for n, (dst, b) in enumerate(((knT, 5), (kbT, 6), (qnT, 7), (qGT, 1))):
                    act.wait_ge(s["unitT_mm"], 4 * t + (n + 1))
                    nc.scalar.copy(dst[:], heads(b)).then_inc(s["unitT_out"], 1)
                for n in range(2, levels):
                    for a in range(2):
                        act.wait_ge(s["xt_mm"], TR * t + (2 * (n - 2) + a + 1))
                        nc.scalar.copy(half(XT, a), bank_half(3 + a)).then_inc(s["xt_ready"], 1)
                act.wait_ge(s["wt_mm"], t + 1)
                nc.scalar.mul(nwT[:], heads(5), -1.0).then_inc(s["nwt_ready"], 1)
                if streams:
                    act.wait_ge(s["dlT_mm"], 1)
                    nc.scalar.copy(dlT[:], heads(6)).then_inc(s["dlT_ready"], 1)
                    act.wait_ge(s["oT_mm"], 1)
                    nc.scalar.copy(oT[:], heads(7)).then_inc(s["oT_ready"], 1)
                act.wait_ge(s["o_mm"], t + 1)
                act.wait_ge(s["o_scaled"], t + 1)
                nc.scalar.copy(oc[:], heads(0)).then_inc(s["o_out"], 1)
                act.wait_ge(s["o_out"], t + 2)
                nc.scalar.activation(osq[:], oc[:], ACT.Square).then_inc(s["o_sq"], 1)

            def output_log(t):
                act.wait_ge(s["o_sum"], t + 1)
                nc.scalar.activation(ln_so[:], so[:], ACT.Ln, scale=1.0 / DV, bias=c["eps"][:]) \
                    .then_inc(s["o_unit"], 1)

            def output_factor(t):
                act.wait_ge(s["o_unit"], 2 * t + 1)
                act.wait_ge(s["o_scaled"], t)
                nc.scalar.activation(ro[:], ln_so[:], ACT.Exp, scale=-0.5).then_inc(s["o_unit"], 1)

            act.sem_inc(s["o_out"], 1)
            with act.Fori(0, NC) as t:
                chunk(t, False)
            chunk(NC, True)
            output_log(NC + 1)
            output_factor(NC + 1)

        @block.gpsimd
        def _(pool):
            def weigh_z(t):
                pool.wait_ge(s["z_loaded"], 16 * t + 16)
                pool.wait_ge(s["mix_ready"], t + 1)
                nc.gpsimd.tensor_tensor(zn[:], z[:], spread(gnorm[:].unsqueeze(1), [P, GH, DV]), ALU.mult) \
                    .then_inc(s["zn_ready"], 1)

            def output(t):
                pool.wait_ge(s["o_unit"], 2 * t + 4)
                pool.wait_ge(s["mix_ready"], t + 1)
                nc.gpsimd.tensor_tensor(on[:], oc[:], per_head(ro[:]), ALU.mult).then_inc(s["o_scaled"], 1)
                pool.wait_ge(s["o_scaled"], t + 2)
                pool.wait_ge(s["mix_stored"], 16 * t + 16)
                pool.wait_ge(s["zn_ready"], t + 1)
                nc.gpsimd.tensor_tensor(mixed[:], on[:], zn[:], ALU.mult).then_inc(s["mix_ready"], 1)

            def chunk(t):
                pool.wait_ge(s["scaled_ready"], 5 * t + 1)
                pool.wait_ge(s["fac_v"], 4 * t + 3)
                nc.gpsimd.tensor_tensor(kbG[:], kn[:], per_head(f_bG[:]), ALU.mult).then_inc(s["pool_scaled"], 1)
                nc.gpsimd.tensor_tensor(kd[:], kn[:], per_head(ex[:, 2 * GH:3 * GH]), ALU.mult) \
                    .then_inc(s["pool_scaled"], 1)
                pool.wait_ge(s["lt_ready"], 2 * t + 1)
                nc.gpsimd.tensor_tensor(x0[:], LT[:], spread(c["level0_t"][:].unsqueeze(1), [P, GH, P]), ALU.mult) \
                    .then_inc(s["pool_x0"], 1)
                pool.wait_ge(s["pool_x0"], t + 1)
                nc.gpsimd.tensor_tensor(XT[:], x0[:], spread(c["ident"][:].unsqueeze(1), [P, GH, P]), ALU.add) \
                    .then_inc(s["xt0_ready"], 1)

            pool.sem_inc(s["mix_stored"], 16)
            pool.sem_inc(s["o_scaled"], 1)
            pool.sem_inc(s["mix_ready"], 1)
            pool.wait_ge(s["small_loaded"], 16)
            chunk(0)
            weigh_z(0)
            with pool.Fori(1, NC) as t:
                chunk(t)
                output(t - 1)
                weigh_z(t)
            chunk(NC)
            output(NC - 1)
            weigh_z(NC)
            output(NC)

        @block.vector
        def _(dve):
            def chunk(t, streams):
                levels = LEVELS_S if streams else LEVELS
                tt, V = nc.vector.tensor_tensor, ALU.mult
                dve.wait_ge(s["gsum_mm"], t + 1)
                nc.vector.tensor_copy(gs[:, 0:2 * GH], bank[:, 3, 0:2 * GH]).then_inc(s["gsum_v"], 1)
                dve.wait_ge(s["gsum_v"], 2 * t + 1)
                tt(gs[:, 2 * GH:], gs[:, GH:2 * GH], gs[:, 0:GH], ALU.subtract).then_inc(s["gsum_v"], 1)
                dve.wait_ge(s["decay_mm"], t + 1)
                tt(dx[:], heads(4), per_head(gs[:, 0:GH]), ALU.subtract).then_inc(s["decay_v"], 1)
                dve.wait_ge(s["squares_ready"], 2 * t + 2)
                nc.vector.tensor_reduce(ss[:], sq[:], AX.X, ALU.add).then_inc(s["sumsq_ready"], 1)
                dve.wait_ge(s["unit_ready"], 2 * t + 2)
                dve.wait_ge(s["ex_ready"], t + 1)
                nc.vector.tensor_scalar(f_q[:], unit[:, 0:GH], float(DK) ** -0.5, None, ALU.mult).then_inc(s["fac_v"], 1)
                tt(f_kb[:], unit[:, GH:], gb[:, GH:], V).then_inc(s["fac_v"], 1)
                tt(f_bG[:], gb[:, GH:], ex[:, 0:GH], V).then_inc(s["fac_v"], 1)
                dve.wait_ge(s["fac_v"], 4 * t + 1)
                tt(f_qG[:], f_q[:], ex[:, 0:GH], V).then_inc(s["fac_v"], 1)
                tt(kn[:], heads(1), per_head(unit[:, GH:]), V).then_inc(s["scaled_ready"], 1)
                dve.wait_ge(s["fac_v"], 4 * t + 4)
                tt(kb[:], heads(1), per_head(f_kb[:]), V).then_inc(s["scaled_ready"], 1)
                tt(qn[:], heads(0), per_head(f_q[:]), V).then_inc(s["scaled_ready"], 1)
                tt(qG[:], heads(0), per_head(f_qG[:]), V).then_inc(s["scaled_ready"], 1)
                dve.wait_ge(s["tok_turned"], 3 * t + 3)
                tt(vb[:], heads(2), per_head(gb[:, GH:]), V).then_inc(s["scaled_ready"], 1)
                dve.wait_ge(s["decay_ready"], t + 1)
                dve.wait_ge(s["kk_mm"], 2 * t + 1)
                tt(LT[:], heads(0), dec[:], V).then_inc(s["lt_ready"], 1)
                dve.wait_ge(s["kk_mm"], 2 * t + 2)
                tt(AT[:], heads(2), dec[:], V).then_inc(s["lt_ready"], 1)
                for a in range(2):
                    dve.wait_ge(s["l0_mm"], 2 * t + (a + 1))
                    tt(half(wn, a), bank_half(3 + a), spread(c["level"][0][:].unsqueeze(1), [P, HH, P]), V) \
                        .then_inc(s["x0_step"], 1)
                for a in range(2):
                    dve.wait_ge(s["x0_step"], 2 * t + (a + 1))
                    tt(half(X, a), half(wn, a), spread(c["ident"][:].unsqueeze(1), [P, HH, P]), ALU.add) \
                        .then_inc(s["x_ready"], 1)
                for n in range(1, levels):
                    for a in range(2):
                        dve.wait_ge(s["w_mm"], WR * t + (2 * (n - 1) + a + 1))
                        tt(half(wn, a), bank_half(5 + a), spread(c["level"][n][:].unsqueeze(1), [P, HH, P]), V) \
                            .then_inc(s["w_ready"], 1)
                    for a in range(2):
                        dve.wait_ge(s["y_mm"], YR * t + (2 * (n - 1) + a + 1))
                        t_, sem = (X, "x_ready") if n < levels - 1 else (XT, "xt_last")
                        tt(half(t_, a), bank_half(7 if a == 0 else 1), half(t_, a), ALU.add).then_inc(s[sem], 1)
                dve.wait_ge(s["delta_mm"], t + 1)
                nc.vector.tensor_copy(dl[:], heads(5 if streams else 6)).then_inc(s["delta_ready"], 1)
                if not streams:
                    dve.wait_ge(s["s_mm"], t + 1)
                    for h in range(GH):
                        nc.vector.scalar_tensor_tensor(S[:, h, :], S[:, h, :], ex[:, GH + h:GH + h + 1],
                                                       bank[:, 2, h * P:(h + 1) * P], ALU.mult, ALU.add) \
                            .then_inc(s["state_ready"], 1)
                dve.wait_ge(s["o_sq"], t + 1)
                nc.vector.tensor_reduce(so[:], osq[:], AX.X, ALU.add).then_inc(s["o_sum"], 1)
                if streams:
                    dve.wait_ge(s["ex_s_ready"], 1)

                    def rows_of(b):
                        nc.vector.tensor_scalar(kd_b[:, b % 2], kd[:], c["stream_rows"][:, b:b + 1], None, ALU.mult) \
                            .then_inc(s["kdb_ready"], 1)

                    dve.wait_ge(s["pool_scaled"], 2 * t + 2)
                    rows_of(0)
                    rows_of(1)
                    for b in range(DB):
                        dve.wait_ge(s["sb_mm"], b + 1)
                        for h in range(GH):
                            nc.vector.scalar_tensor_tensor(S_s[:, b, h, :], S_s[:, b, h, :], ex_s[:, b, h:h + 1],
                                                           bank[:, 2 + b % 2, h * P:(h + 1) * P], ALU.mult, ALU.add) \
                                .then_inc(s["sb_ready"], 1)
                        if b + 2 < DB:
                            rows_of(b + 2)

            nc.vector.memset(S[:], 0.0).then_inc(s["state_ready"], GH)
            nc.vector.memset(so[:], 1.0).then_inc(s["o_sum"], 1)
            with dve.Fori(0, NC) as t:
                chunk(t, False)
            chunk(NC, True)
    ph.close()


def fox_prompt(nc, c, io, bank):
    ph = Phase(nc, "foxp")
    FH, FD, FW, SEQ = (c[k] for k in ("FH", "FD", "FW", "SEQ"))
    NB = SEQ // P
    GB = 4
    A = FD + 2
    banks_of = [n // GB + 1 for n in range(NB)]
    first = [sum(banks_of[:n]) for n in range(NB)]
    NBK = sum(banks_of)
    NG = NB // GB
    assert NB % GB == 0 and NBK % 4 == 0 and 2 * NG <= 8

    ktok, qtok, v = ph.sb("ktok", [P, NB, A]), ph.sb("qtok", [P, NB, A]), ph.sb("v", [P, NB, FD])
    kT, qT = ph.sb("kT", [A, SEQ]), ph.sb("qT", [A, SEQ])
    qscale = ph.sb("qscale", [A, 1])
    f, before, csum = (ph.sb(n, [P, NB, FH]) for n in ("f", "before", "csum"))
    logits = ph.sb("logits", [P, 3, SEQ])
    low, neg_max, row_sum, inv_sum = ph.sb("low", [P, 3, GB]), *(ph.sb(n, [P, 3]) for n in ("nmax", "rsum", "inv"))
    pT = ph.sb("pT", [P, 2, GB, P])
    o = ph.sb("o", [P, NB, FD])

    (f_loaded, f_step, c_mm, c_ready, kq_loaded, v_loaded, aug_ready, prep_mm, prep_out_a, prep_out_v, qk_mm,
     s_out, low_ready, max_ready, p_ready, pt_mm, pt_out_v, pt_out_a, pv_mm, inv_ready, o_out, o_stored) = (
        ph.sem(n) for n in (
            "f_loaded f_step c_mm c_ready kq_loaded v_loaded aug_ready prep_mm prep_out_a prep_out_v qk_mm "
            "s_out low_ready max_ready p_ready pt_mm pt_out_v pt_out_a pv_mm inv_ready o_out o_stored").split())
    in_head = "(n p) d -> p n d"
    HALF = NBK // 2

    def count(n):
        return banks_of[n] if 0 <= n < NB else 0

    def steps(n):
        return max(count(n), count(n - 2))

    with nc.Block() as block:

        @block.sync
        def _(sp):
            sp.dma_start(f[:], io["logf_p"].rearrange("(n p) h -> p n h", p=P)).then_inc(f_loaded, 16)
            with sp.Fori(0, FH) as h:
                cols = bass.ds(h * FD, FD)
                sp.wait_ge(prep_mm, 2 * NG * h + 1)
                sp.dma_start(ktok[:, :, 0:FD], io["k_p"][:, cols].rearrange(in_head, p=P)).then_inc(kq_loaded, 16)
                sp.dma_start(qtok[:, :, 0:FD], io["q_tok"][0:SEQ, cols].rearrange(in_head, p=P)) \
                    .then_inc(kq_loaded, 16)
                sp.wait_ge(pv_mm, NBK * h + 1)
                sp.dma_start(v[:], io["v_p"][:, cols].rearrange(in_head, p=P)).then_inc(v_loaded, 16)

        @block.tensor
        def _(pe):
            pe.sem_inc(prep_mm, 1)
            pe.sem_inc(pv_mm, 1)
            pe.wait_ge(f_loaded, 16)
            pe.wait_ge(f_step, NB)
            pe.matmul(bank[:, 0, 0:NB * FH], c["tri"][:], f[:].rearrange("p n h -> p (n h)"), start=True, stop=False)
            pe.matmul(bank[:, 0, 0:NB * FH], c["ones"][:], before[:].rearrange("p n h -> p (n h)"),
                      start=False, stop=True).then_inc(c_mm, 1)
            with pe.Fori(0, FH) as h:
                pe.wait_ge(kq_loaded, 32 * h + 32)
                pe.wait_ge(aug_ready, 2 * h + 2)
                pe.wait_ge(s_out, NBK * h + 1)
                pe.wait_ge(pt_out_a, HALF * h + 1)
                pe.wait_ge(o_out, NB * h + 1)
                for g in range(2 * NG):
                    src = ktok if g < NG else qtok
                    for b in range(GB):
                        mm = pe.transpose(bank[0:A, g, b * P:(b + 1) * P], src[:, (g % NG) * GB + b, :], c["ident"][:])
                    mm.then_inc(prep_mm, 1)
                pe.wait_ge(prep_out_a, NG * h + NG)
                pe.wait_ge(prep_out_v, NG * h + NG)
                pe.wait_ge(v_loaded, 16 * h + 16)

                def logit_bank(n, j):
                    r = first[n] + j
                    width = min(GB, n + 1 - j * GB) * P
                    diagonal = j == banks_of[n] - 1
                    if r >= 4:
                        pe.wait_ge(s_out, NBK * h + (r - 4 + 2))
                    mm = pe.matmul(bank[:, r % 4, 0:width], qT[:, n * P:(n + 1) * P],
                                   kT[:, j * GB * P:j * GB * P + width], start=True, stop=not diagonal)
                    if diagonal:
                        mm = pe.matmul(bank[:, r % 4, width - P:width], c["ident"][:], c["causal"][:],
                                       start=False, stop=True)
                    mm.then_inc(qk_mm, 1)

                def turn(n, j):
                    r = first[n] + j
                    if r >= 2:
                        out = pt_out_v if r % 2 == 0 else pt_out_a
                        pe.wait_ge(out, HALF * h + ((r - 2) // 2 + 2))
                    for b in range(min(GB, n + 1 - j * GB)):
                        at = (j * GB + b) * P
                        mm = pe.transpose(bank[:, 4 + r % 2, b * P:(b + 1) * P], logits[:, n % 3, at:at + P],
                                          c["ident"][:])
                    mm.then_inc(pt_mm, 1)

                def meet_v(n, j):
                    r = first[n] + j
                    pe.wait_ge(pt_out_v if r % 2 == 0 else pt_out_a, HALF * h + (r // 2 + 2))
                    for b in range(min(GB, n + 1 - j * GB)):
                        blk = j * GB + b
                        mm = pe.matmul(bank[:, 6 + n % 2, 0:FD], pT[:, r % 2, b, :], v[:, blk, :],
                                       start=(blk == 0), stop=(blk == n))
                    mm.then_inc(pv_mm, 1)

                left = None
                for n in range(NB + 2):
                    m = n - 2
                    for j in range(steps(n)):
                        if j < count(n):
                            logit_bank(n, j)
                        if j == 0 and left is not None:
                            meet_v(*left)
                        if j == 0 and m >= 0:
                            pe.wait_ge(p_ready, NB * h + (m + 1))
                            if m >= 2:
                                pe.wait_ge(o_out, NB * h + (m - 2 + 2))
                        if j < count(m):
                            turn(m, j)
                            if j >= 1:
                                meet_v(m, j - 1)
                    if m >= 0:
                        left = m, count(m) - 1
                meet_v(*left)

        @block.scalar
        def _(act):
            act.sem_inc(pt_out_a, 1)
            with act.Fori(0, FH) as h:
                for g in range(NG):
                    act.wait_ge(prep_mm, 2 * NG * h + (g + 2))
                    nc.scalar.copy(kT[:, g * BANK:(g + 1) * BANK], bank[0:A, g, :]).then_inc(prep_out_a, 1)
                for n in range(NB + 2):
                    if n >= 2:
                        m = n - 2
                        for j in range(banks_of[m]):
                            r = first[m] + j
                            if r % 2:
                                width = min(GB, m + 1 - j * GB)
                                act.wait_ge(pt_mm, NBK * h + (r + 1))
                                if r >= 2:
                                    act.wait_ge(pv_mm, NBK * h + (r - 2 + 2))
                                nc.scalar.copy(pT[:, 1, 0:width, :],
                                               bank[:, 5, 0:width * P].rearrange("p (b k) -> p b k", k=P)) \
                                    .then_inc(pt_out_a, 1)
                    if n < NB:
                        L = (n + 1) * P
                        act.wait_ge(max_ready, NB * h + (n + 1))
                        nc.scalar.activation(logits[:, n % 3, 0:L], logits[:, n % 3, 0:L], ACT.Exp, scale=-1.0,
                                             bias=neg_max[:, n % 3:n % 3 + 1],
                                             accum_out=row_sum[:, n % 3:n % 3 + 1]).then_inc(p_ready, 1)
                act.wait_ge(o_out, NB * h + (NB + 1))
                act.dma_start(io["mix_tok"][0:SEQ, bass.ds(h * FD, FD)].rearrange(in_head, p=P), o[:]) \
                    .then_inc(o_stored, 16)
            act.wait_ge(o_stored, 16 * (FH + 1))

        @block.vector
        def _(dve):
            dve.sem_inc(s_out, 1)
            dve.sem_inc(pt_out_v, 1)
            dve.sem_inc(o_out, 1)
            dve.sem_inc(o_stored, 16)
            nc.vector.memset(ktok[:, :, FD:FD + 1], 1.0)
            nc.vector.memset(qtok[:, :, FD + 1:A], 1.0)
            nc.vector.memset(qscale[:], float(FD) ** -0.5)
            nc.vector.memset(before[:, 0, :], 0.0).then_inc(f_step, 1)
            dve.wait_ge(f_loaded, 16)
            for n in range(1, NB):
                dve.wait_ge(f_step, n)
                nc.vector.tensor_tensor(before[:, n, :], before[:, n - 1, :], f[:, n - 1, :], ALU.add) \
                    .then_inc(f_step, 1)
            nc.vector.memset(qscale[FD:A], 1.0).then_inc(f_step, 1)
            dve.wait_ge(c_mm, 1)
            nc.vector.tensor_copy(csum[:].rearrange("p n h -> p (n h)"), bank[:, 0, 0:NB * FH]).then_inc(c_ready, 1)
            dve.wait_ge(c_ready, 1)
            dve.wait_ge(f_step, NB + 1)
            with dve.Fori(0, FH) as h:
                hc = bass.ds(h, 1)
                dve.wait_ge(prep_mm, 2 * NG * h + 1)
                nc.vector.tensor_copy(qtok[:, :, FD:FD + 1], csum[:, :, hc]).then_inc(aug_ready, 1)
                nc.vector.tensor_scalar(ktok[:, :, FD + 1:A], csum[:, :, hc], -1.0, None, ALU.mult) \
                    .then_inc(aug_ready, 1)
                for g in range(NG):
                    dve.wait_ge(prep_mm, 2 * NG * h + (NG + g + 2))
                    nc.vector.tensor_scalar(qT[:, g * BANK:(g + 1) * BANK], bank[0:A, NG + g, :], qscale[:], None,
                                            ALU.mult).then_inc(prep_out_v, 1)
                def finish(m):
                    dve.wait_ge(p_ready, NB * h + (m + 1))
                    nc.vector.reciprocal(inv_sum[:, m % 3:m % 3 + 1], row_sum[:, m % 3:m % 3 + 1]) \
                        .then_inc(inv_ready, 1)
                    dve.wait_ge(inv_ready, NB * h + (m + 1))
                    dve.wait_ge(pv_mm, NBK * h + (first[m] + banks_of[m] + 1))
                    if m == 0:
                        dve.wait_ge(o_stored, 16 * h + 16)
                    nc.vector.tensor_scalar(o[:, m, :], bank[:, 6 + m % 2, 0:FD], inv_sum[:, m % 3:m % 3 + 1],
                                            None, ALU.mult).then_inc(o_out, 1)

                for n in range(NB + 2):
                    s, m = n % 3, n - 2
                    for j in range(steps(n)):
                        if j < count(n):
                            r = first[n] + j
                            width = min(GB, n + 1 - j * GB) * P
                            dve.wait_ge(qk_mm, NBK * h + (r + 1))
                            if n >= 3 and j == 0:
                                dve.wait_ge(pt_mm, NBK * h + first[n - 2])
                            nc.vector.tensor_scalar(logits[:, s, j * BANK:j * BANK + width], bank[:, r % 4, 0:width],
                                                    -1.0, None, ALU.mult, ALU.min, accum_out=low[:, s, j:j + 1]) \
                                .then_inc(s_out, 1)
                        if j == 0 and m >= 1:
                            finish(m - 1)
                        if j < count(m) and (first[m] + j) % 2 == 0:
                            r = first[m] + j
                            width = min(GB, m + 1 - j * GB)
                            dve.wait_ge(pt_mm, NBK * h + (r + 1))
                            if r >= 2:
                                dve.wait_ge(pv_mm, NBK * h + (r - 2 + 2))
                            nc.vector.tensor_copy(pT[:, 0, 0:width, :],
                                                  bank[:, 4, 0:width * P].rearrange("p (b k) -> p b k", k=P)) \
                                .then_inc(pt_out_v, 1)
                    if n < NB:
                        dve.wait_ge(s_out, NBK * h + (first[n] + banks_of[n] + 1))
                        nc.vector.tensor_reduce(neg_max[:, s:s + 1], low[:, s, 0:banks_of[n]], AX.X, ALU.min) \
                            .then_inc(max_ready, 1)
                finish(NB - 1)
    ph.close()


def fox_sample(nc, c, io, bank):
    ph = Phase(nc, "foxs")
    FH, FD, FW, DB, DS, PAST, SEQ = (c[k] for k in ("FH", "FD", "FW", "DB", "DS", "PAST", "SEQ"))
    NP = FW // P
    NK = PAST // P
    GB = 4
    NBK = (NK + GB - 1) // GB
    KW = [min(GB, NK - g * GB) for g in range(NBK)]
    ROWS = 2 * DS
    assert FW == NP * P and 2 * FD == P and NBK <= 2 and FH * DS == P

    k, v = ph.sb("k", [P, 2, NK, FW]), ph.sb("v", [P, 2, NK, FW])
    v_new = ph.sb("v_new", [DS, 2, FW])
    f = ph.sb("f", [P, 2, NK, FH])
    kT = ph.sb("kT", [P, NP, PAST])
    q_tok, k_tok, f_new = ph.sb("q_tok", [P, FW]), ph.sb("k_tok", [P, FW]), ph.sb("f_new", [P, FH])
    qT, kT_new = ph.sb("qT", [P, NP, P]), ph.sb("kT_new", [P, NP, P])
    q_heads = ph.sb("q_heads", [P, 2, NP, P])
    f_after = ph.sb("f_after", [P, NK, FH])
    f_rows = ph.sb("f_rows", [P, 2, FH, DS])
    f_all = ph.sb("f_all", [P, 2, NK, FH, DS])
    f_key = ph.sb("f_key", [P, 2, NK, FH, DS])
    logits = ph.sb("logits", [P, PAST + DS])
    low = ph.sb("low", [P, NBK + 1])
    neg_max, row_sum, inv_sum = (ph.sb(n, [P, 1]) for n in ("nmax", "rsum", "inv"))
    pT, pT_new = ph.sb("pT", [P, NK, P]), ph.sb("pT_new", [DS, P])
    head_rows = ph.sb("head_rows", [DS, P])
    oT, o = ph.sb("oT", [P, NP, P]), ph.sb("o", [P, FW])

    s = {n: ph.sem(n) for n in (
        "new_loaded new_turned new_ready kf_loaded0 kf_loaded1 v_loaded0 v_loaded1 q_ready f_step f_ready kt_mm kt_out_v "
        "kt_out_a s_mm s_out max_ready p_ready inv_ready pn_ready pt_mm pt_out pv_mm o_out o_turned o_ready o_stored"
    ).split()}

    def each_stream(eng, body):
        with eng.Fori(0, DB // 2 - 1) as i:
            for a in range(2):
                body(i, a, False)
        body(DB // 2 - 1, 0, False)
        body(DB // 2 - 1, 1, True)

    def following(i, a):
        return (i, 1) if a == 0 else (i + 1, 0)

    with nc.Block() as block:

        @block.sync
        def _(sp):
            for dst, src in ((q_tok, io["q_tok"][SEQ:, :]), (k_tok, io["k_s"]), (f_new, io["logf_s"])):
                sp.dma_start(dst[:], src).then_inc(s["new_loaded"], 16)
            ck = io["cache_fox_k"].rearrange("l b (n p) h d -> (l b) p n (h d)", p=P)
            cv = io["cache_fox_v"].rearrange("l b (n p) h d -> (l b) p n (h d)", p=P)
            cf = io["cache_fox_logf"].rearrange("l b (n p) h -> (l b) p n h", p=P)
            with sp.Fori(0, DB // 2) as i:
                for a in range(2):
                    b = 2 * i + a
                    sp.wait_ge(s["s_mm"], b + 1)
                    one = bass.ds(b, 1)
                    sp.dma_start(k[:, a], ck[one].rearrange("o p n d -> (o p) n d")).then_inc(s[f"kf_loaded{a}"], 16)
                    sp.dma_start(f[:, a], cf[one].rearrange("o p n h -> (o p) n h")).then_inc(s[f"kf_loaded{a}"], 16)
                    sp.wait_ge(s["pv_mm"], b + 1)
                    sp.dma_start(v[:, a], cv[one].rearrange("o p n d -> (o p) n d")).then_inc(s[f"v_loaded{a}"], 16)
                    sp.dma_start(v_new[:, a], io["v_s"][bass.ds(b * DS, DS), :]).then_inc(s[f"v_loaded{a}"], 16)
            sp.wait_ge(s["o_ready"], 1)
            sp.dma_start(io["mix_tok"][SEQ:, 0:FW], o[:]).then_inc(s["o_stored"], 16)
            sp.wait_ge(s["o_stored"], 16)

        @block.tensor
        def _(pe):
            pe.sem_inc(s["s_mm"], 2)
            pe.sem_inc(s["pv_mm"], 2)
            pe.wait_ge(s["new_loaded"], 48)
            for n, src in enumerate((q_tok, k_tok)):
                for p in range(NP):
                    mm = pe.transpose(bank[:, n, p * P:(p + 1) * P], src[:, p * P:(p + 1) * P], c["ident"][:])
                mm.then_inc(s["new_turned"], 1)
            pe.wait_ge(s["new_ready"], 4)
            def turn_k(i, a):
                b = 2 * i + a
                pe.wait_ge(s[f"kf_loaded{a}"], 32 * i + 32)
                pe.wait_ge(s["pt_out"], 2 * b + 1)
                for n in range(NK):
                    out = "kt_out_v" if n % 2 == 0 else "kt_out_a"
                    pe.wait_ge(s[out], (NK // 2) * b + (n // 2 + 1))
                    for p in range(NP):
                        mm = pe.transpose(bank[:, n % 4, p * P:(p + 1) * P], k[:, a, n, p * P:(p + 1) * P],
                                          c["ident"][:])
                    mm.then_inc(s["kt_mm"], 1)

            def body(i, a, last):
                b = 2 * i + a
                pe.wait_ge(s["kt_out_v"], (NK // 2) * b + (NK // 2 + 2))
                pe.wait_ge(s["kt_out_a"], (NK // 2) * b + (NK // 2 + 2))
                pe.wait_ge(s["q_ready"], 2 * b + 2)
                pe.wait_ge(s["f_ready"], 2 * b + 2)
                for g in range(NBK):
                    w = KW[g] * P
                    for p in range(NP):
                        pe.matmul(bank[:, 4 + g, 0:w], q_heads[:, a, p, :], kT[:, p, g * BANK:g * BANK + w],
                                  start=(p == 0), stop=False)
                    for n in range(g * GB, g * GB + KW[g]):
                        at = bank[:, 4 + g, (n % GB) * P:(n % GB + 1) * P]
                        pe.matmul(at, f_key[:, a, n].rearrange("p h q -> p (h q)"), c["after"][:],
                                  start=False, stop=False)
                        pe.matmul(at, f_all[:, a, n].rearrange("p h q -> p (h q)"), c["ones"][:],
                                  start=False, stop=(n == g * GB + KW[g] - 1))
                new = bank[:, 6, 0:DS]
                for p in range(NP):
                    pe.matmul(new, q_heads[:, a, p, :], kT_new[:, p, bass.ds(b * DS, DS)], start=(p == 0), stop=False)
                pe.matmul(new, f_rows[:, a].rearrange("p h q -> p (h q)"), c["later_in_stream"][:],
                          start=False, stop=False)
                pe.matmul(new, head_rows[:], c["causal_s"][0:DS, :], start=False, stop=True) \
                    .then_inc(s["s_mm"], 1)
                if not last:
                    turn_k(*following(i, a))
                pe.wait_ge(s["pn_ready"], b + 1)
                if not last:
                    pe.wait_ge(s["kt_out_v"], (NK // 2) * b + (NK + 2))
                    pe.wait_ge(s["kt_out_a"], (NK // 2) * b + (NK + 2))
                for n in range(NK):
                    mm = pe.transpose(bank[:, n // GB, (n % GB) * P:(n % GB + 1) * P], logits[:, n * P:(n + 1) * P],
                                      c["ident"][:])
                mm = pe.transpose(bank[0:DS, 2, 0:P], logits[:, PAST:], c["ident"][:])
                mm.then_inc(s["pt_mm"], 1)
                pe.wait_ge(s[f"v_loaded{a}"], 32 * i + 32)
                pe.wait_ge(s["pt_out"], 2 * b + 5)
                for p in range(NP):
                    at = bank[:, 7, p * ROWS:(p + 1) * ROWS]
                    rows = slice(p * ROWS, (p + 1) * ROWS)
                    for n in range(NK):
                        pe.matmul(at, v[:, a, n, p * P:(p + 1) * P], pT[:, n, rows], start=(n == 0), stop=False)
                    mm = pe.matmul(at, v_new[:, a, p * P:(p + 1) * P], pT_new[:, rows], start=False, stop=True)
                mm.then_inc(s["pv_mm"], 1)

            turn_k(0, 0)
            each_stream(pe, body)
            pe.wait_ge(s["o_out"], 2 * DB)
            for p in range(NP):
                mm = pe.transpose(bank[:, 0, p * P:(p + 1) * P], oT[:, p, :], c["ident"][:])
            mm.then_inc(s["o_turned"], 1)

        @block.scalar
        def _(act):
            act.sem_inc(s["kt_out_a"], 2)
            def copy_k(i, a):
                b = 2 * i + a
                act.wait_ge(s["s_mm"], b + 2)
                for n in range(1, NK, 2):
                    act.wait_ge(s["kt_mm"], NK * b + (n + 1))
                    nc.scalar.copy(kT[:, :, n * P:(n + 1) * P], bank[:, n % 4, :].rearrange("p (c t) -> p c t", t=P)) \
                        .then_inc(s["kt_out_a"], 1)

            def body(i, a, last):
                b = 2 * i + a
                act.wait_ge(s["max_ready"], b + 1)
                nc.scalar.activation(logits[:], logits[:], ACT.Exp, scale=-1.0, bias=neg_max[:],
                                     accum_out=row_sum[:]).then_inc(s["p_ready"], 1)
                if not last:
                    copy_k(*following(i, a))

            copy_k(0, 0)
            each_stream(act, body)

        @block.vector
        def _(dve):
            tt, cp = nc.vector.tensor_tensor, nc.vector.tensor_copy
            dve.sem_inc(s["kt_out_v"], 2)
            dve.sem_inc(s["pt_out"], 3)
            nc.vector.memset(q_heads[:], 0.0).then_inc(s["new_ready"], 1)
            dve.wait_ge(s["new_turned"], 1)
            nc.vector.tensor_scalar(qT[:], bank[:, 0, :].rearrange("p (c t) -> p c t", t=P), float(FD) ** -0.5, None,
                                    ALU.mult).then_inc(s["new_ready"], 1)
            dve.wait_ge(s["new_turned"], 2)
            cp(kT_new[:], bank[:, 1, :].rearrange("p (c t) -> p c t", t=P)).then_inc(s["new_ready"], 1)
            cp(head_rows[:].rearrange("q (h r) -> q h r", r=DS), spread(c["ident"][0:DS, 0:DS].unsqueeze(1),
                                                                      [DS, FH, DS])).then_inc(s["new_ready"], 1)
            dve.wait_ge(s["new_ready"], 4)
            dve.wait_ge(s["new_loaded"], 48)
            def parts(i, a):
                b = 2 * i + a
                dve.wait_ge(s["s_mm"], b + 1)
                for e in range(2):
                    rows = q_heads[e * FD:(e + 1) * FD, a]
                    dst = bass.AP(tensor=rows.tensor, offset=rows.offset + e * DS,
                                  ap=[list(rows.ap[0]), [P + 2 * DS, NP], [1, DS]])
                    cp(dst, qT[e * FD:(e + 1) * FD, :, bass.ds(b * DS, DS)]).then_inc(s["q_ready"], 1)
                dve.wait_ge(s[f"kf_loaded{a}"], 32 * i + 32)
                dve.wait_ge(s["f_ready"], 2 * b)
                nc.vector.memset(f_after[:, NK - 1, :], 0.0).then_inc(s["f_step"], 1)
                for n in range(NK - 2, -1, -1):
                    dve.wait_ge(s["f_step"], (NK + 1) * b + (NK - 1 - n))
                    tt(f_after[:, n, :], f_after[:, n + 1, :], f[:, a, n + 1, :], ALU.add).then_inc(s["f_step"], 1)
                tt(f_rows[:, a], spread(f_new[:].unsqueeze(2), [P, FH, DS]),
                   spread(c["before_q"][:, bass.ds(b, 1), :], [P, FH, DS]), ALU.mult).then_inc(s["f_step"], 1)
                cp(f_key[:, a], spread(f[:, a].unsqueeze(3), [P, NK, FH, DS])).then_inc(s["f_ready"], 1)
                dve.wait_ge(s["f_step"], (NK + 1) * b + (NK + 1))
                tt(f_all[:, a], spread(f_after[:].unsqueeze(3), [P, NK, FH, DS]),
                   spread(f_rows[:, a].unsqueeze(1), [P, NK, FH, DS]), ALU.add).then_inc(s["f_ready"], 1)

            def copy_k(i, a):
                b = 2 * i + a
                dve.wait_ge(s["s_mm"], b + 2)
                for n in range(0, NK, 2):
                    dve.wait_ge(s["kt_mm"], NK * b + (n + 1))
                    cp(kT[:, :, n * P:(n + 1) * P], bank[:, n % 4, :].rearrange("p (c t) -> p c t", t=P)) \
                        .then_inc(s["kt_out_v"], 1)

            def body(i, a, last):
                b = 2 * i + a
                if not last:
                    parts(*following(i, a))
                dve.wait_ge(s["s_mm"], b + 3)
                pieces = [(4 + g, g * BANK, KW[g] * P) for g in range(NBK)] + [(6, PAST, DS)]
                for n, (bk, at, w) in enumerate(pieces):
                    nc.vector.tensor_scalar(logits[:, at:at + w], bank[:, bk, 0:w], -1.0, None, ALU.mult, ALU.min,
                                            accum_out=low[:, n:n + 1]).then_inc(s["s_out"], 1)
                dve.wait_ge(s["s_out"], (NBK + 1) * b + (NBK + 1))
                nc.vector.tensor_reduce(neg_max[:], low[:], AX.X, ALU.min).then_inc(s["max_ready"], 1)
                if not last:
                    copy_k(*following(i, a))
                dve.wait_ge(s["p_ready"], b + 1)
                nc.vector.reciprocal(inv_sum[:], row_sum[:]).then_inc(s["inv_ready"], 1)
                dve.wait_ge(s["inv_ready"], b + 1)
                nc.vector.tensor_scalar(logits[:], logits[:], inv_sum[:], None, ALU.mult) \
                    .then_inc(s["pn_ready"], 1)
                dve.wait_ge(s["pt_mm"], b + 1)
                for g in range(NBK):
                    last_copy = cp(pT[:, g * GB:g * GB + KW[g], :],
                                   bank[:, g, 0:KW[g] * P].rearrange("p (b k) -> p b k", k=P))
                last_copy.then_inc(s["pt_out"], 1)
                cp(pT_new[:], bank[0:DS, 2, 0:P]).then_inc(s["pt_out"], 1)
                dve.wait_ge(s["pv_mm"], b + 3)
                for e in range(2):
                    src = bank[e * FD:(e + 1) * FD, 7, 0:NP * ROWS].rearrange("p (c t) -> p c t", t=ROWS)
                    cp(oT[e * FD:(e + 1) * FD, :, bass.ds(b * DS, DS)], src[:, :, e * DS:(e + 1) * DS]) \
                        .then_inc(s["o_out"], 1)

            parts(0, 0)
            copy_k(0, 0)
            each_stream(dve, body)
            dve.wait_ge(s["o_turned"], 1)
            cp(o[:], bank[:, 0, :]).then_inc(s["o_ready"], 1)
    ph.close()


def mix(nc, c, io, bank):
    ph = Phase(nc, "mix")
    D, SEQ, NT = c["D"], c["SEQ"], c["NT"]
    M = c["FW"] + c["GW"]
    KD, KM, HB = D // P, M // P, BANK // P
    ND = D // BANK
    assert KM == 2 * HB and KD == 2 * HB and ND == 2

    w = ph.sb("w", [P, KM, D])
    x, h, hn = (ph.sb(n, [P, D]) for n in ("x", "h", "hn"))
    m_tok = ph.sb("m_tok", [P, D])
    hn_hi, hn_lo = c["hn_hi"], c["hn_lo"]
    squares = bank[:, 6:8, :].rearrange("p a n -> p (a n)")
    mT, hT = ph.sb("mT", [P, KM, P]), ph.sb("hT", [P, KD, P])
    norm_rows, norm_w = ph.sb("norm_rows", [KD, P]), ph.sb("norm_w", [P, KD])
    ss, ln_ms, rs = (ph.sb(n, [P, 1]) for n in ("ss", "ln_ms", "rs"))
    (w_loaded, small_loaded, small_turned, small_ready, m_loaded, x_loaded, in_mm, in_out_a, in_out_v, prod_mm, h_ready,
     squared, ln_done, rs_ready, hn_ready, out_mm, hT_ready, h_stored, hi_ready, split_done) = (ph.sem(n) for n in (
         "w_loaded small_loaded small_turned small_ready m_loaded x_loaded in_mm in_out_a in_out_v prod_mm h_ready "
         "squared ln_done rs_ready hn_ready out_mm hT_ready h_stored hi_ready split_done").split())

    def rows(t):
        return bass.ds(t * P, P)

    with nc.Block() as block:

        @block.sync
        def _(sp):
            def load_m(t):
                sp.dma_start(m_tok[:], io["mix_tok"][rows(t), :]).then_inc(m_loaded, 16)

            def load_x(t):
                sp.dma_start(x[:], io["x_s"] if t is None else io["x_p"][rows(t), :]).then_inc(x_loaded, 16)

            load_m(0)
            sp.dma_start(norm_rows[:], io["norm_ffn_w"].rearrange("l (k p) -> (l k) p", p=P)).then_inc(small_loaded, 16)
            sp.dma_start(w[:], io["w_o"][0].rearrange("(k p) n -> p k n", p=P)).then_inc(w_loaded, 16)
            load_x(0)

            def behind(t):
                sp.wait_ge(in_mm, 2 * t)
                load_m(t)
                sp.wait_ge(h_ready, 2 * t + 2)

            with sp.Fori(1, NT - 1) as t:
                behind(t)
                load_x(t)
            behind(NT - 1)
            load_x(None)

        @block.tensor
        def _(pe):
            def turn_in(t):
                pe.wait_ge(m_loaded, 16 * t + 16)
                for n, out in enumerate((in_out_a, in_out_v)):
                    pe.wait_ge(out, t + 1)
                    for k in range(HB):
                        mm = pe.transpose(bank[:, n, k * P:(k + 1) * P], m_tok[:, (n * HB + k) * P:(n * HB + k + 1) * P],
                                          c["ident"][:])
                    mm.then_inc(in_mm, 1)

            def products(t):
                pe.wait_ge(in_out_a, t + 2)
                pe.wait_ge(in_out_v, t + 2)
                pe.wait_ge(h_ready, 2 * t + 2)
                for n in range(ND):
                    for k in range(KM):
                        mm = pe.matmul(bank[:, 2 + n, :], mT[:, k, :], w[:, k, n * BANK:(n + 1) * BANK],
                                       start=(k == 0), stop=(k == KM - 1))
                    mm.then_inc(prod_mm, 1)

            def turn_out(t):
                pe.wait_ge(hn_ready, t + 1)
                for n in range(2):
                    pe.wait_ge(hT_ready, 2 * t + (n + 1))
                    for k in range(HB):
                        mm = pe.transpose(bank[:, 4 + n, k * P:(k + 1) * P],
                                          hn[:, (n * HB + k) * P:(n * HB + k + 1) * P], c["ident"][:])
                    mm.then_inc(out_mm, 1)

            pe.wait_ge(small_loaded, 16)
            pe.transpose(bank[:, 6, 0:KD], norm_rows[:], c["ident"][0:KD, 0:KD]).then_inc(small_turned, 1)
            pe.wait_ge(small_ready, 1)
            turn_in(0)
            pe.wait_ge(w_loaded, 16)
            products(0)
            turn_in(1)
            with pe.Fori(1, NT - 1) as t:
                products(t)
                turn_in(t + 1)
                turn_out(t - 1)
            products(NT - 1)
            turn_out(NT - 2)
            turn_out(NT - 1)

        @block.scalar
        def _(act):
            def norm_factor(t):
                act.wait_ge(h_ready, 2 * t + 4)
                act.dma_start(io["h_tok"][rows(t), :], h[:]).then_inc(h_stored, 16)
                nc.scalar.activation(squares, h[:], ACT.Square, accum_out=ss[:]).then_inc(squared, 1)
                act.wait_ge(squared, t + 1)
                nc.scalar.activation(ln_ms[:], ss[:], ACT.Ln, scale=1.0 / D, bias=c["eps"][:]).then_inc(ln_done, 1)
                act.wait_ge(ln_done, t + 1)
                nc.scalar.activation(rs[:], ln_ms[:], ACT.Exp, scale=-0.5).then_inc(rs_ready, 1)

            def copy_in(t):
                act.wait_ge(in_mm, 2 * t + 1)
                nc.scalar.copy(mT[:, 0:HB, :], bank[:, 0, :].rearrange("p (k t) -> p k t", t=P)).then_inc(in_out_a, 1)

            def split_hi(t):
                act.wait_ge(hT_ready, 2 * t + 4)
                nc.scalar.copy(hn_hi[:, :, rows(t)], hT[:]).then_inc(hi_ready, 1)

            act.sem_inc(in_out_a, 1)
            copy_in(0)
            copy_in(1)
            norm_factor(0)
            with act.Fori(1, NT - 1) as t:
                copy_in(t + 1)
                norm_factor(t)
                split_hi(t - 1)
            norm_factor(NT - 1)
            split_hi(NT - 2)
            split_hi(NT - 1)
            act.wait_ge(h_stored, 16 * (NT + 1))

        @block.vector
        def _(dve):
            def copy_in(t):
                dve.wait_ge(in_mm, 2 * t + 2)
                nc.vector.tensor_copy(mT[:, HB:, :], bank[:, 1, :].rearrange("p (k t) -> p k t", t=P)) \
                    .then_inc(in_out_v, 1)

            def add_x(t):
                dve.wait_ge(x_loaded, 16 * t + 16)
                dve.wait_ge(h_stored, 16 * t + 16)
                dve.wait_ge(hn_ready, t)
                for n in range(ND):
                    dve.wait_ge(prod_mm, 2 * t + (n + 1))
                    nc.vector.tensor_tensor(h[:, n * BANK:(n + 1) * BANK], bank[:, 2 + n, :],
                                            x[:, n * BANK:(n + 1) * BANK], ALU.add).then_inc(h_ready, 1)

            def normalise(t):
                dve.wait_ge(rs_ready, t + 1)
                nc.vector.tensor_scalar(hn[:], h[:], rs[:], None, ALU.mult).then_inc(hn_ready, 1)

            def weigh_out(t):
                for n in range(2):
                    dve.wait_ge(out_mm, 2 * t + (n + 1))
                    if n == 0:
                        dve.wait_ge(split_done, t + 1)
                    nc.vector.tensor_tensor(hT[:, n * HB:(n + 1) * HB, :],
                                            bank[:, 4 + n, :].rearrange("p (k t) -> p k t", t=P),
                                            spread(norm_w[:, n * HB:(n + 1) * HB].unsqueeze(2), [P, HB, P]), ALU.mult) \
                        .then_inc(hT_ready, 1)

            def split_lo(t):
                dve.wait_ge(hi_ready, t + 1)
                nc.vector.tensor_tensor(hn_lo[:, :, rows(t)], hT[:], hn_hi[:, :, rows(t)], ALU.subtract) \
                    .then_inc(split_done, 1)

            dve.sem_inc(in_out_v, 1)
            dve.sem_inc(h_ready, 2)
            dve.sem_inc(hT_ready, 2)
            dve.sem_inc(h_stored, 16)
            dve.sem_inc(split_done, 1)
            dve.wait_ge(small_turned, 1)
            nc.vector.tensor_copy(norm_w[:], bank[:, 6, 0:KD]).then_inc(small_ready, 1)
            dve.wait_ge(small_ready, 1)
            copy_in(0)
            add_x(0)
            copy_in(1)
            normalise(0)
            with dve.Fori(1, NT - 1) as t:
                add_x(t)
                copy_in(t + 1)
                weigh_out(t - 1)
                normalise(t)
                split_lo(t - 1)
            add_x(NT - 1)
            weigh_out(NT - 2)
            normalise(NT - 1)
            split_lo(NT - 2)
            weigh_out(NT - 1)
            split_lo(NT - 1)
    ph.close()


def ffn_up(nc, c, io, bank):
    ph = Phase(nc, "up")
    D, F2, FC, DB, DS, SEQ = (c[k] for k in ("D", "F2", "FC", "DB", "DS", "SEQ"))
    KD, NF2, H2 = D // P, F2 // P, FC - 1
    NF, R = NF2 // 2, DB * H2 + H2
    RS = DB * H2
    chunks = [(n * BANK, BANK, False) for n in range(SEQ // BANK)] + [(SEQ, P, True)]
    NK, UNITS = len(chunks), 2 * len(chunks)
    assert NF % 2 == 0 and SEQ % BANK == 0 and NF2 % 4 == 0

    hn_hi, hn_lo = c["hn_hi"], c["hn_lo"]
    w = ph.sb("w", [P, 2, KD, P])
    w_parts = ph.sb("w_parts", [P, 2, 2, 2, KD, P], F32R)
    raw = ph.sb("raw", [P, 2, 2, H2 + BANK])
    acc = ph.sb("acc", [P, 2, 2, BANK])
    hist = ph.sb("hist", [P, NF2, R])
    vecs = ph.sb("vecs", [P, 4, NF2])
    AW = 4 * BANK
    rows_rest = raw[:].rearrange("p a b n -> p (a b n)")[:, 2 * P:]
    assert F2 <= 2 * AW + 4 * BANK - 2 * P
    places = (acc[:].rearrange("p a b n -> p (a b n)"), w[:].rearrange("p e k n -> p (e k n)"), rows_rest)
    row_parts = [(places[n][0:R, 0:min(F2 - at, AW)], at) for n, at in enumerate((0, AW, 2 * AW)) if at < F2]

    def rows_of(q, n=0, width=BANK):
        at = (4 * q + n) * P
        part, start = row_parts[min(at // AW, 2)]
        return part[:, at - start:at - start + width]

    vec_rows = raw[:].rearrange("p a b n -> p (a b n)")[0:2 * NF2, 0:2 * P].rearrange("r (a p) -> r a p", p=P)

    s = {n: ph.sem(n) for n in (
        "small_loaded rows_loaded setup_turned setup_ready w_loaded w_hi_ready w_split up_mm raw_ready conv_step "
        "conv_done silu_ready g_ready g_stored0 g_stored1 tail_turned tail_read tail_stored").split()}
    BANKS_CREDIT = 8

    wu = io["w_up"][0].rearrange("(k p) (e f n) -> p e f k n", p=P, e=2, n=P)

    def chan(e, f):
        return e * NF + f

    def each_f(eng, body):
        with eng.Fori(0, NF // 2 - 1) as i:
            for a in range(2):
                body(i, a, False)
        body(NF // 2 - 1, 0, False)
        body(NF // 2 - 1, 1, True)

    def each_chunk(i, a):
        for n, ch in enumerate(chunks):
            K = a * NK + n
            yield n, ch, 2 * UNITS * i + (UNITS * a + 2 * n), K % 2, NK * i + K // 2

    def pair(n):
        return 4 if chunks[n][2] else 2 * (n % 2)

    with nc.Block() as block:

        @block.sync
        def _(sp):
            sp.dma_start(vec_rows[:, 0, :], io["ffn_conv_w"][:, 0:2].rearrange("l i (k p) -> (l i k) p", p=P)) \
                .then_inc(s["small_loaded"], 16)
            sp.dma_start(vec_rows[0:NF2, 1, :], io["ffn_conv_w"][:, 2:3].rearrange("l i (k p) -> (l i k) p", p=P)) \
                .then_inc(s["small_loaded"], 16)
            sp.dma_start(vec_rows[NF2:, 1, :], io["ffn_conv_b"].rearrange("l (k p) -> (l k) p", p=P)) \
                .then_inc(s["small_loaded"], 16)
            for part, at in row_parts:
                sp.dma_start(part[0:RS, :], io["ffn_state"][:, at:at + part.shape[1]]).then_inc(s["rows_loaded"], 16)

            def load(f):
                sp.wait_ge(s["w_split"], f)
                for e in range(2):
                    sp.dma_start(w[:, e], wu[:, e, bass.ds(f, 1)].rearrange("p o k n -> p (o k) n")) \
                        .then_inc(s["w_loaded"], 16)

            sp.wait_ge(s["setup_turned"], 1)
            load(0)

            def body(i, a, last):
                f = 2 * i + a
                if not last:
                    load(f + 1)
                for n, (col, width, _), _, slot, _ in each_chunk(i, a):
                    sp.wait_ge(s["g_ready"], NK * f + (n + 1))
                    sp.dma_start(io["g"][bass.ds(f * P, P), col:col + width], acc[:, slot, 0, 0:width]) \
                        .then_inc(s[f"g_stored{slot}"], 16)

            each_f(sp, body)
            for a in range(2):
                sp.wait_ge(s[f"g_stored{a}"], 16 * (NF * NK // 2) + 16)

        @block.tensor
        def _(pe):
            pe.sem_inc(s["up_mm"], UNITS)
            pe.wait_ge(s["small_loaded"], 48)
            pe.wait_ge(s["rows_loaded"], 16 * len(row_parts))
            for n in range(2):
                pe.transpose(bank[:, 0, n * 2 * NF2:(n + 1) * 2 * NF2], vec_rows[:, n, :],
                             c["ident"][0:2 * NF2, 0:2 * NF2])
            for n in range(NF2):
                mm = pe.transpose(bank[:, 1 + n * RS // BANK, n * RS % BANK:n * RS % BANK + RS],
                                  rows_of(n // 4, n % 4, P)[0:RS, :], c["ident"][0:RS, 0:RS])
            mm.then_inc(s["setup_turned"], 1)
            pe.wait_ge(s["setup_ready"], 2 + (NF2 * RS + BANK - 1) // BANK)

            def body(i, a, last):
                pe.wait_ge(s["w_split"], 2 * i + (a + 1))
                for n, (col, width, _), unit, _, _ in each_chunk(i, a):
                    cols = slice(col, col + width)
                    for e in range(2):
                        pe.wait_ge(s["raw_ready"], 2 * unit + (2 * e + 2))
                        for k in range(KD):
                            for m, (part, x) in enumerate(((0, hn_hi), (0, hn_lo), (1, hn_hi))):
                                mm = pe.matmul(bank[:, pair(n) + e, 0:width], w_parts[:, a, part, e, k, :],
                                               x[:, k, cols], start=(k == 0 and m == 0), stop=(k == KD - 1 and m == 2))
                        mm.then_inc(s["up_mm"], 1)

            each_f(pe, body)
            for q in range(NF2 // 4):
                if q >= 2:
                    pe.wait_ge(s["tail_read"], q - 1)
                else:
                    pe.wait_ge(s["g_ready"], NF * NK)
                for n in range(4):
                    mm = pe.transpose(bank[0:R, 6 + q % 2, n * P:(n + 1) * P], hist[:, 4 * q + n, :], c["ident"][:])
                mm.then_inc(s["tail_turned"], 1)

        @block.scalar
        def _(act):
            act.sem_inc(s["raw_ready"], BANKS_CREDIT)
            for a in range(2):
                act.sem_inc(s[f"g_stored{a}"], 16)
            act.wait_ge(s["setup_ready"], 2 + (NF2 * RS + BANK - 1) // BANK)

            def split_hi(i, a):
                f = 2 * i + a
                act.wait_ge(s["w_loaded"], 32 * f + 32)
                act.wait_ge(s["up_mm"], UNITS * f)
                nc.scalar.copy(w_parts[:, a, 0], w[:]).then_inc(s["w_hi_ready"], 1)

            def body(i, a, last):
                for n, (col, width, streams), unit, slot, stores in each_chunk(i, a):
                    if n == 2 and not last:
                        split_hi(*((i, 1) if a == 0 else (i + 1, 0)))
                    act.wait_ge(s[f"g_stored{slot}"], 16 * stores + 16)
                    for e in range(2):
                        act.wait_ge(s["up_mm"], unit + (e + 1 + UNITS))
                        act.wait_ge(s["conv_done"], unit + (e + 1))
                        src = bank[:, pair(n) + e, 0:width]
                        if streams:
                            nc.scalar.copy(
                                raw[:, slot, e, 0:DB * (H2 + DS)].rearrange("p (b r) -> p b r", b=DB)[:, :, H2:],
                                src.rearrange("p (b r) -> p b r", b=DB)).then_inc(s["raw_ready"], 1)
                        else:
                            nc.scalar.copy(raw[:, slot, e, H2:], src).then_inc(s["raw_ready"], 1)
                        at = bass.ds(chan(e, 2 * i + a), 1)
                        nc.scalar.activation(acc[:, slot, e, 0:width], src, ACT.Identity,
                                             scale=vecs[:, 2, at], bias=vecs[:, 3, at]).then_inc(s["raw_ready"], 1)
                    act.wait_ge(s["conv_done"], unit + 5)
                    nc.scalar.activation(acc[:, slot, 0, 0:width], acc[:, slot, 0, 0:width], ACT.Silu) \
                        .then_inc(s["silu_ready"], 1)

            split_hi(0, 0)
            each_f(act, body)
            act.wait_ge(s["tail_read"], NF2 // 4)
            for part, at in row_parts:
                cols = slice(at, at + part.shape[1])
                act.dma_start(io["ffn_s"][:, cols], part[0:RS, :]).then_inc(s["tail_stored"], 16)
                act.dma_start(io["ffn_p"][:, cols], part[RS:R, :]).then_inc(s["tail_stored"], 16)
            act.wait_ge(s["tail_stored"], 32 * len(row_parts))

        @block.vector
        def _(dve):
            cp, stt = nc.vector.tensor_copy, nc.vector.scalar_tensor_tensor

            def move(dst, src):
                return nc.vector.tensor_scalar(dst, src, 1.0, None, ALU.mult)

            def split_lo(i, a):
                dve.wait_ge(s["w_hi_ready"], 2 * i + (a + 1))
                nc.vector.tensor_tensor(w_parts[:, a, 1], w[:], w_parts[:, a, 0], ALU.subtract) \
                    .then_inc(s["w_split"], 1)

            dve.sem_inc(s["conv_done"], 4)
            nc.vector.memset(hist[:, :, RS:R], 0.0).then_inc(s["setup_ready"], 1)
            dve.wait_ge(s["setup_turned"], 1)
            cp(vecs[:].rearrange("p a n -> p (a n)"), bank[:, 0, 0:4 * NF2]).then_inc(s["setup_ready"], 1)
            per = BANK // RS
            for n in range((NF2 + per - 1) // per):
                tiles = min(per, NF2 - n * per)
                cp(hist[:, n * per:n * per + tiles, 0:RS],
                   bank[:, 1 + n, 0:tiles * RS].rearrange("p (f r) -> p f r", r=RS)).then_inc(s["setup_ready"], 1)
            dve.wait_ge(s["setup_ready"], 2 + (NF2 * RS + BANK - 1) // BANK)

            def body(i, a, last):
                f = 2 * i + a
                for n, (col, width, streams), unit, slot, _ in each_chunk(i, a):
                    if n == 2 and not last:
                        split_lo(*((i, 1) if a == 0 else (i + 1, 0)))
                    for e in range(2):
                        at, st = bass.ds(chan(e, f), 1), 3 * unit + 3 * e
                        if streams:
                            r = raw[:, slot, e, 0:DB * (H2 + DS)].rearrange("p (b r) -> p b r", b=DB)
                            u = acc[:, slot, e, 0:width].rearrange("p (b r) -> p b r", b=DB)
                            past = hist[:, at, 0:RS].rearrange("p o (b r) -> p (o b) r", b=DB)
                            old, new = r[:, :, 0:H2], r[:, :, DS:]
                            taps = [r[:, :, k:k + DS] for k in range(H2)]
                        else:
                            r, u = raw[:, slot, e], acc[:, slot, e]
                            past = hist[:, at, RS:R].rearrange("p o r -> p (o r)")
                            old, new = r[:, 0:H2], r[:, BANK:]
                            taps = [r[:, k:k + BANK] for k in range(H2)]
                        dve.wait_ge(s["conv_done"], unit + (e + 1))
                        move(old, past).then_inc(s["conv_step"], 1)
                        dve.wait_ge(s["conv_step"], st + 1)
                        dve.wait_ge(s["raw_ready"], 2 * unit + (2 * e + BANKS_CREDIT + 2))
                        move(past, new).then_inc(s["conv_step"], 1)
                        stt(u, taps[1], vecs[:, 1, at], u, ALU.mult, ALU.add).then_inc(s["conv_step"], 1)
                        dve.wait_ge(s["conv_step"], st + 3)
                        stt(u, taps[0], vecs[:, 0, at], u, ALU.mult, ALU.add).then_inc(s["conv_done"], 1)
                    dve.wait_ge(s["silu_ready"], NK * f + (n + 1))
                    dve.wait_ge(s["conv_done"], unit + 6)
                    nc.vector.tensor_tensor(acc[:, slot, 0, 0:width], acc[:, slot, 0, 0:width],
                                            acc[:, slot, 1, 0:width], ALU.mult).then_inc(s["g_ready"], 1)

            split_lo(0, 0)
            each_f(dve, body)
            for a in range(2):
                dve.wait_ge(s[f"g_stored{a}"], 16 * (NF * NK // 2) + 16)
            for q in range(NF2 // 4):
                dve.wait_ge(s["tail_turned"], q + 1)
                cp(rows_of(q), bank[0:R, 6 + q % 2, :]).then_inc(s["tail_read"], 1)
    ph.close()


def mix_and_up(nc, c, io, bank):
    with ExitStack() as stack:
        for n in ("hn_hi", "hn_lo"):
            c[n] = stack.enter_context(nc.sbuf_tensor(n, [P, c["D"] // P, c["SEQ"] + P], F32R))
        mix(nc, c, io, bank)
        ffn_up(nc, c, io, bank)


def ffn_down(nc, c, io, bank):
    ph = Phase(nc, "down")
    D, F2, SEQ = c["D"], c["F2"], c["SEQ"]
    NF, TB = F2 // 2 // P, BANK // P
    NB, ND, UT = SEQ // BANK, D // BANK, TB // 2
    assert NF % 2 == 0 and SEQ % BANK == 0 and ND == 2 and 2 * TB == 8

    w_hi, w_lo = (ph.sb(n, [P, NF, D], F32R) for n in ("w_hi", "w_lo"))
    g_raw = ph.sb("g_raw", [P, 2, BANK])
    g_hi, g_lo = (ph.sb(n, [P, 2, UT * P], F32R) for n in ("g_hi", "g_lo"))
    y = ph.sb("y", [P, TB, D])
    norm_w = ph.sb("norm_w", [P, D])
    ss, ln_ms, rs = (ph.sb(n, [P, TB]) for n in ("ss", "ln_ms", "rs"))

    s = {n: ph.sem(n) for n in (
        "norm_loaded w0_loaded w1_loaded w_hi_ready w_split g0_loaded g1_loaded g_hi_ready g_split g_used down_mm "
        "r_ready squared ln_done rs_ready weighed yn_ready").split()}
    h_loaded, y_stored = ([ph.sem(f"{n}{j}") for j in range(TB)] for n in ("h_loaded", "y_stored"))
    SPLIT_CREDIT = 4

    class Place:

        def __init__(self, b, streams):
            self.b, self.streams = b, streams
            self.tiles = 1 if streams else TB
            self.units = 1 if streams else 2
            self.cols = slice(SEQ, SEQ + P) if streams else bass.ds(b * BANK, BANK)
            self.width = self.tiles * P
            self.tile0 = b * TB

        def unit(self, f, q):
            return self.b * (2 * NF) + (f if self.streams else 2 * f + q)

        def slot(self, a, q):
            return a if self.streams else q

        def width_of_unit(self):
            return P if self.streams else UT * P

        def tiles_of_unit(self, q):
            return range(1) if self.streams else range(UT * q, UT * (q + 1))

    def blocks(eng, body):
        body(Place(0, False), Place(1, False), True)
        with eng.Fori(1, NB - 1) as b:
            body(Place(b, False), Place(b + 1, False), False)
        body(Place(NB - 1, False), Place(NB, True), False)
        body(Place(NB, True), None, False)

    with nc.Block() as block:

        @block.sync
        def _(sp):
            def load_w(f, a):
                if not isinstance(f, int) or f >= 2:
                    sp.wait_ge(s["w_split"], f - 1)
                sp.dma_start(y[:, a], io["w_down"][0][bass.ds(f * P, P), :]).then_inc(s[f"w{a}_loaded"], 16)

            def load_g(at, f, a):
                sp.wait_ge(s["g_split"], at.unit(f, 0) + (SPLIT_CREDIT - at.units))
                sp.dma_start(g_raw[:, a, 0:at.width], io["g"][bass.ds(f * P, P), at.cols]) \
                    .then_inc(s[f"g{a}_loaded"], 16)

            def body(at, following, first):
                def step(f, a):
                    if first:
                        load_w(f, a)
                    load_g(at, f, a)

                if first:
                    step(0, 0)
                    step(1, 1)
                with sp.Fori(1 if first else 0, NF // 2) as i:
                    for a in range(2):
                        step(2 * i + a, a)

            sp.dma_start(norm_w[:], io["norm_final_w"].partition_broadcast(P)).then_inc(s["norm_loaded"], 16)
            blocks(sp, body)

        @block.tensor
        def _(pe):
            def body(at, following, first):
                def step(f, a, start, stop):
                    if first:
                        pe.wait_ge(s["w_split"], f + 1)
                    for q in range(at.units):
                        pe.wait_ge(s["g_split"], at.unit(f, q) + (SPLIT_CREDIT + 1))
                        slot = at.slot(a, q)
                        for m, j in enumerate(at.tiles_of_unit(q)):
                            if start:
                                pe.wait_ge(s["squared"], at.tile0 + (j + 1))
                            for g, w, only in ((g_hi, w_hi, 0), (g_hi, w_lo, 1), (g_lo, w_hi, 2)):
                                for n in range(ND):
                                    mm = pe.matmul(bank[:, ND * j + n, :], g[:, slot, m * P:(m + 1) * P],
                                                   w[:, bass.ds(f, 1), n * BANK:(n + 1) * BANK]
                                                   .rearrange("p o n -> p (o n)"),
                                                   start=(start and only == 0), stop=(stop and only == 2))
                                    if m == 0 and only == 0 and n == 0:
                                        mm.then_inc(s["g_used"], 1)
                                    if stop and only == 2:
                                        mm.then_inc(s["down_mm"], 1)

                step(0, 0, True, False)
                step(1, 1, False, False)
                with pe.Fori(1, NF // 2 - 1) as i:
                    for a in range(2):
                        step(2 * i + a, a, False, False)
                step(NF - 2, 0, False, False)
                step(NF - 1, 1, False, True)

            blocks(pe, body)

        def each_step(eng, at, split):
            split(at, 1, 1)
            with eng.Fori(1, NF // 2) as i:
                for a in range(2):
                    split(at, 2 * i + a, a)

        def split_steps(eng, split_unit, split_w, drain):
            def body(at, following, first):
                def split(at, f, a):
                    if first:
                        split_w(f, a)
                    for q in range(at.units):
                        split_unit(at, f, a, q)

                if first:
                    split(at, 0, 0)
                each_step(eng, at, split)
                for q in range(at.units):
                    if following is not None and q < following.units:
                        split_unit(following, 0, 0, q)
                    for j in at.tiles_of_unit(q):
                        drain(at, j)

            return body

        @block.scalar
        def _(act):
            def split_w(f, a):
                act.wait_ge(s[f"w{a}_loaded"], 8 * (f - a) + 16)
                nc.scalar.copy(w_hi[:, bass.ds(f, 1), :], y[:, a:a + 1]) \
                    .then_inc(s["w_hi_ready"], 1)

            def split_unit(at, f, a, q):
                if q == 0:
                    act.wait_ge(s[f"g{a}_loaded"], at.b * (8 * NF) + (8 * (f - a) + 16))
                act.wait_ge(s["g_used"], at.unit(f, q))
                n = at.width_of_unit()
                nc.scalar.copy(g_hi[:, at.slot(a, q), 0:n], g_raw[:, a, q * n:(q + 1) * n]) \
                    .then_inc(s["g_hi_ready"], 1)

            def square(at, j):
                act.wait_ge(s["r_ready"], 2 * at.tile0 + (2 * j + 2))
                nc.scalar.activation(bank[:, 2 * j:2 * j + 2, :].rearrange("p a n -> p (a n)"), y[:, j], ACT.Square,
                                     accum_out=ss[:, j:j + 1]).then_inc(s["squared"], 1)

            steps = split_steps(act, split_unit, split_w, square)

            def body(at, following, first):
                steps(at, following, first)
                n = at.tiles
                act.wait_ge(s["squared"], at.tile0 + (TB + n))
                nc.scalar.activation(ln_ms[:, 0:n], ss[:, 0:n], ACT.Ln, scale=1.0 / D, bias=c["eps"][:]) \
                    .then_inc(s["ln_done"], 1)
                act.wait_ge(s["ln_done"], at.b + 1)
                act.wait_ge(s["yn_ready"], at.tile0)
                nc.scalar.activation(rs[:, 0:n], ln_ms[:, 0:n], ACT.Exp, scale=-0.5).then_inc(s["rs_ready"], 1)

            act.sem_inc(s["squared"], TB)
            blocks(act, body)

        @block.vector
        def _(dve):
            def split_w(f, a):
                dve.wait_ge(s["w_hi_ready"], f + 1)
                nc.vector.tensor_tensor(w_lo[:, bass.ds(f, 1), :], y[:, a:a + 1],
                                        w_hi[:, bass.ds(f, 1), :], ALU.subtract).then_inc(s["w_split"], 1)

            def split_unit(at, f, a, q):
                dve.wait_ge(s["g_hi_ready"], at.unit(f, q) + 1)
                n, slot = at.width_of_unit(), at.slot(a, q)
                nc.vector.tensor_tensor(g_lo[:, slot, 0:n], g_raw[:, a, q * n:(q + 1) * n], g_hi[:, slot, 0:n],
                                        ALU.subtract).then_inc(s["g_split"], 1)

            def drain(at, j):
                dve.wait_ge(h_loaded[j], 16 * at.b + 16)
                for n in range(ND):
                    dve.wait_ge(s["down_mm"], 2 * at.tile0 + (2 * j + n + 1))
                    cols = slice(n * BANK, (n + 1) * BANK)
                    nc.vector.tensor_tensor(y[:, j, cols], bank[:, ND * j + n, :], y[:, j, cols], ALU.add) \
                        .then_inc(s["r_ready"], 1)

            dve.sem_inc(s["g_split"], SPLIT_CREDIT)
            blocks(dve, split_steps(dve, split_unit, split_w, drain))

        @block.gpsimd
        def _(pool):
            def load_h(at, j):
                src = io["h_tok"][SEQ:SEQ + P, :] if at.streams else io["h_tok"][bass.ds(at.b * BANK + j * P, P), :]
                pool.dma_start(y[:, j], src).then_inc(h_loaded[j], 16)

            def body(at, following, first):
                for j in range(at.tiles):
                    if j == 0:
                        pool.wait_ge(s["rs_ready"], at.b + 1)
                    nc.gpsimd.tensor_tensor(y[:, j], y[:, j], norm_w[:], ALU.mult).then_inc(s["weighed"], 1)
                    pool.wait_ge(s["weighed"], at.tile0 + (j + 1))
                    nc.gpsimd.tensor_tensor(y[:, j], y[:, j], spread(rs[:, j:j + 1], [P, D]), ALU.mult) \
                        .then_inc(s["yn_ready"], 1)
                    pool.wait_ge(s["yn_ready"], at.tile0 + (j + 1))
                    dst = io["y_s"] if at.streams else io["y_p"][bass.ds(at.b * BANK + j * P, P), :]
                    pool.dma_start(dst, y[:, j]).then_inc(y_stored[j], 16)
                if following is not None:
                    for j in range(following.tiles):
                        pool.wait_ge(y_stored[j], 16 * at.b + 16)
                        load_h(following, j)

            pool.wait_ge(s["norm_loaded"], 16)
            for j in (2, 3, 0, 1):
                if j < 2:
                    pool.wait_ge(s["w_split"], NF - 1 + j)
                load_h(Place(0, False), j)
            blocks(pool, body)
            for j in range(TB):
                pool.wait_ge(y_stored[j], 16 * (NB + (j == 0)))
    ph.close()


def build(nc, arg, out):
    _, SEQ, D = arg["x_prompt"].shape
    DB, DS, _ = arg["x_sample"].shape
    _, _, PAST, FH, FD = arg["cache_fox_k"].shape
    _, _, GH, DK, DV = arg["state_gdn"].shape
    CW, GC = arg["gdn_conv_w"].shape[1:]
    FC, F2 = arg["ffn_conv_w"].shape[1:]
    c = dict(SEQ=SEQ, D=D, DB=DB, DS=DS, PAST=PAST, FH=FH, FD=FD, FW=FH * FD, GH=GH, DK=DK, DV=DV, GW=GH * DV,
             CW=CW, GC=GC, FC=FC, F2=F2, NT=SEQ // P + 1)
    assert arg["x_prompt"].shape[0] == 1 and DB * DS == P and FH * DS == P and DK == P and DV == P

    TOK = SEQ + P
    scratch = {n: nc.dram_tensor(f"scratch_{n}", s, F32, kind="Internal").ap() for n, s in (
        ("q_tok", (TOK, FH * FD)), ("z_tok", (TOK, GH * DV)), ("gb_tok", (TOK, 2 * GH)), ("gch", (GC, TOK)),
        ("mix_tok", (TOK, FH * FD + GH * DV)), ("h_tok", (TOK, D)), ("g", (F2 // 2, TOK)))}
    io = dict(arg, **scratch)
    io["x_p"] = arg["x_prompt"].rearrange("a t d -> (a t) d")
    io["x_s"] = arg["x_sample"].rearrange("a t d -> (a t) d")
    io["conv_state"] = arg["state_gdn_conv"].rearrange("l b r n -> (l b r) n")
    io["ffn_state"] = arg["state_ffn_conv"].rearrange("l b r n -> (l b r) n")
    io["y_p"] = out[0].rearrange("a t d -> (a t) d")
    io["y_s"] = out[1].rearrange("a t d -> (a t) d")
    for n, i in (("k_p", 2), ("v_p", 3), ("k_s", 8), ("v_s", 9)):
        io[n] = out[i].rearrange("l a t h d -> (l a t) (h d)")
    for n, i in (("logf_p", 4), ("logf_s", 10), ("conv_p", 6), ("ffn_p", 7), ("conv_s", 12), ("ffn_s", 13)):
        io[n] = out[i].rearrange("l a t h -> (l a t) h")
    io["S_p"], io["S_s"] = out[5][0, 0], out[11][0]

    with ExitStack() as whole:
        bank = whole.enter_context(nc.psum_tensor("bank", [P, 8, BANK], F32))
        c["eps"] = whole.enter_context(nc.sbuf_tensor("eps", [P, 1], F32))
        with ExitStack() as constants:
            def sb(name, shape):
                return constants.enter_context(nc.sbuf_tensor(name, shape, F32))

            for n in ("ones", "ident", "tri", "tri_s", "same_stream", "causal", "after", "decay_mask", "decay_mask_s",
                      "level0_t"):
                c[n] = sb(n, [P, P])
            c["level"] = [sb(f"level{n}", [P, P]) for n in range(7)]
            c["stream_rows"] = sb("stream_rows", [P, DB])
            c["before_q"] = sb("before_q", [P, DB, DS])
            c["later_in_stream"], c["causal_s"] = sb("later_in_stream", [P, DS]), sb("causal_s", [P, DS])
            for phase in PHASES:
                phase(nc, c, io, bank)
        ffn_down(nc, c, io, bank)


PHASES = [project, delta, fox_prompt, fox_sample, mix_and_up]

_INS = ['x_prompt', 'x_sample', 'cache_fox_k', 'cache_fox_v', 'cache_fox_logf', 'state_gdn', 'state_gdn_conv',
        'state_ffn_conv', 'w_in', 'b_fox_f', 'gdn_conv_w', 'gdn_a_log', 'gdn_dt_bias', 'gdn_norm_w', 'w_o',
        'norm_mix_w', 'norm_ffn_w', 'w_up', 'ffn_conv_w', 'ffn_conv_b', 'w_down', 'norm_final_w']


def kernel(**inputs):
    import numpy as _np
    import concourse.bacc as _bacc
    from concourse.bass_utils import run_bass_kernel_spmd as _run

    nc = _bacc.Bacc("TRN2", target_bir_lowering=False, num_devices=1)
    arrays, arg = {}, {}
    for name in _INS:
        a = _np.ascontiguousarray(inputs[name])
        arrays[f"in_{name}_dram"] = a
        arg[name] = nc.dram_tensor(f"in_{name}_dram", a.shape, mybir.dt.from_np(a.dtype), kind="ExternalInput").ap()
    s = {n: a.shape for n, a in arg.items()}
    fox_p = (1,) + s["x_prompt"][:2] + s["cache_fox_k"][3:]
    fox_s = (1,) + s["x_sample"][:2] + s["cache_fox_k"][3:]
    outs = [s["x_prompt"], s["x_sample"],
            fox_p, fox_p, fox_p[:4], (1, 1) + s["state_gdn"][2:], (1, 1) + s["state_gdn_conv"][2:],
            (1, 1) + s["state_ffn_conv"][2:],
            fox_s, fox_s, fox_s[:4], s["state_gdn"], s["state_gdn_conv"], s["state_ffn_conv"]]
    out = [nc.dram_tensor(f"out_{i}_dram", shape, F32, kind="ExternalOutput").ap() for i, shape in enumerate(outs)]
    build(nc, arg, out)
    r = _run(nc, [arrays], core_ids=[0])
    return tuple(r.results[0][f"out_{i}_dram"] for i in range(len(outs)))
```
